# Optimizing a Trainium2 kernel written in Bass

```python
import math
import jax
import jax.numpy as jnp
from jax import lax
import numpy as np

D_MODEL = 1024
BATCH = 1
SEQ = 256
DEPTH = 2

D_MIX = D_MODEL
ML_HEADS = 4
ML_DH = 64
ML_W = ML_HEADS * ML_DH
ML_CHUNK = 64
SSM_HEADS = 4
SSM_P = 64
SSM_W = SSM_HEADS * SSM_P
SSM_GROUPS = 2
SSM_N = 64
SSM_CONV = 4
SSM_CONV_DIM = SSM_W + 2 * SSM_GROUPS * SSM_N
SSM_CHUNK = 64
AT_HEADS = 4
AT_DH = 64
AT_W = AT_HEADS * AT_DH
DILATED = ((128, 1), (512, 4), (2048, 16))
ROPE_THETA = 10000.0
GLA_HEADS = 4
GLA_DK = 32
GLA_DV = 64
GLA_W = GLA_HEADS * GLA_DV
GLA_GATE_RANK = 16
GLA_TAU = 16.0
GLA_CHUNK = 64
N_EXPERTS = 64
TOP_K = 8
N_GROUPS = 8
TOPK_GROUPS = 4
D_EXPERT = 256
D_SHARED = 256
ROUTED_SCALE = 2.5
MOE_BLOCK = 128
ALPHA = (2 * DEPTH) ** 0.25
BETA = (8 * DEPTH) ** -0.25
LN_EPS = 1e-5

IN_SIZES = (ML_W, ML_W, ML_W, ML_W, ML_HEADS, ML_HEADS,
            SSM_W, SSM_CONV_DIM, SSM_HEADS,
            AT_W, AT_W, AT_W,
            GLA_HEADS * GLA_DK, GLA_HEADS * GLA_DK, GLA_W, GLA_W, GLA_GATE_RANK)
D_IN = sum(IN_SIZES)

kernel_name = 'hybrid_mlstm_ssd_dilated_gla_moe'

def layer_norm(x, g, b):
    xf = x.astype(jnp.float32)
    mu = xf.mean(-1, keepdims=True)
    var = jnp.mean(jnp.square(xf - mu), -1, keepdims=True)
    y = (xf - mu) * lax.rsqrt(var + LN_EPS) * g.astype(jnp.float32) + b.astype(jnp.float32)
    return y.astype(x.dtype)

def head_norm(x, w, center):
    if center:
        x = x - x.mean(-1, keepdims=True)
    x = x * lax.rsqrt(jnp.mean(x * x, -1, keepdims=True) + LN_EPS)
    return x.reshape(*x.shape[:-2], -1) * w

def to_chunks(t, L):
    B, H, S = t.shape[:3]
    return jnp.moveaxis(t.reshape(B, H, S // L, L, *t.shape[3:]), 2, 0)

def from_chunks(t):
    nc, B, H, L = t.shape[:4]
    return jnp.moveaxis(t, 0, 2).reshape(B, H, nc * L, *t.shape[4:])

def mlstm_chunked(q, k, v, li, lf):
    B, H, S, dh = q.shape
    L = ML_CHUNK
    k = k * dh ** -0.5
    causal = jnp.tril(jnp.ones((L, L), bool))

    def step(carry, inp):
        C, n, m = carry
        qc, kc, vc, lic, lfc = inp
        b = jnp.cumsum(lfc, -1)
        log_d = jnp.where(causal, b[..., :, None] - b[..., None, :] + lic[..., None, :], -jnp.inf)
        log_inter = b + m[..., None]
        m_t = jnp.maximum(log_inter, log_d.max(-1))
        w_inter = jnp.exp(log_inter - m_t)
        s = jnp.einsum('bhtd,bhsd->bhts', qc, kc) * jnp.exp(log_d - m_t[..., None])
        num = jnp.einsum('bhts,bhsv->bhtv', s, vc) + w_inter[..., None] * jnp.einsum('bhtd,bhdv->bhtv', qc, C)
        den = s.sum(-1) + w_inter * jnp.einsum('bhtd,bhd->bht', qc, n)
        h = num / jnp.maximum(jnp.abs(den), jnp.exp(-m_t))[..., None]
        b_last = b[..., -1]
        log_s = b_last[..., None] - b + lic
        m_new = jnp.maximum(b_last + m, log_s.max(-1))
        w_s = jnp.exp(log_s - m_new[..., None])
        w_c = jnp.exp(b_last + m - m_new)
        kw = kc * w_s[..., None]
        C = w_c[..., None, None] * C + jnp.einsum('bhsd,bhsv->bhdv', kw, vc)
        n = w_c[..., None] * n + kw.sum(2)
        return (C, n, m_new), h

    init = (jnp.zeros((B, H, dh, dh), q.dtype), jnp.zeros((B, H, dh), q.dtype),
            jnp.full((B, H), -jnp.inf, q.dtype))
    _, h = lax.scan(step, init, tuple(to_chunks(t, L) for t in (q, k, v, li, lf)))
    return from_chunks(h)

def causal_conv(x, w, b):
    K, C = w.shape
    xp = jnp.pad(x, ((0, 0), (K - 1, 0), (0, 0)))
    y = lax.conv_general_dilated(xp, w[:, None, :], (1,), 'VALID',
                                 dimension_numbers=('NWC', 'WIO', 'NWC'), feature_group_count=C)
    return y + b

def ssd(x, dt, A, Bm, Cm, Dskip):
    Bsz, S, H, P = x.shape
    G, N = Bm.shape[2], Bm.shape[3]
    R = H // G
    L = SSM_CHUNK
    nc = S // L
    a = (dt * A).reshape(Bsz, nc, L, G, R)
    xc = (x * dt[..., None]).reshape(Bsz, nc, L, G, R, P)
    Bc = Bm.reshape(Bsz, nc, L, G, N)
    Cc = Cm.reshape(Bsz, nc, L, G, N)
    acs = jnp.cumsum(a, axis=2)
    causal = jnp.tril(jnp.ones((L, L), bool))
    seg = jnp.where(causal[:, :, None, None], acs[:, :, :, None] - acs[:, :, None, :], -jnp.inf)
    cb = jnp.einsum('bclgn,bcsgn->bclsg', Cc, Bc)
    y_diag = jnp.einsum('bclsgr,bcsgrp->bclgrp', cb[..., None] * jnp.exp(seg), xc)
    decay_states = jnp.exp(acs[:, :, -1:] - acs)
    states = jnp.einsum('bclgn,bclgrp->bcgrpn', Bc, decay_states[..., None] * xc)
    chunk_decay = jnp.exp(acs[:, :, -1])

    def step(s, inp):
        st, dec = inp
        return dec[..., None, None] * s + st, s

    s0 = jnp.zeros((Bsz, G, R, P, N), x.dtype)
    _, prev = lax.scan(step, s0, (jnp.moveaxis(states, 1, 0), jnp.moveaxis(chunk_decay, 1, 0)))
    prev = jnp.moveaxis(prev, 0, 1)
    y_off = jnp.einsum('bclgn,bcgrpn->bclgrp', Cc, prev) * jnp.exp(acs)[..., None]
    return (y_diag + y_off).reshape(Bsz, S, H, P) + x * Dskip[:, None]

def rope(x, pos):
    half = x.shape[-1] // 2
    inv = ROPE_THETA ** (-jnp.arange(half, dtype=jnp.float32) / half)
    ang = pos.astype(jnp.float32)[:, None] * inv
    cos = jnp.cos(ang)[None, :, None, :]
    sin = jnp.sin(ang)[None, :, None, :]
    x1, x2 = x[..., :half], x[..., half:]
    return jnp.concatenate([x1 * cos - x2 * sin, x2 * cos + x1 * sin], -1)

def dilated_branch(q, k, v, window, dilation):
    B, S, H, E = q.shape
    span = window // dilation
    nb = -(-S // window)
    pad = nb * window - S

    def blocks(t):
        t = jnp.pad(t, ((0, 0), (0, pad), (0, 0), (0, 0)))
        return t.reshape(B, nb, span, dilation, H, E)

    def with_prev(t):
        prev = jnp.pad(t, ((0, 0), (1, 0), (0, 0), (0, 0), (0, 0), (0, 0)))[:, :-1]
        return jnp.concatenate([prev, t], axis=2)

    qb = blocks(q)
    kk = with_prev(blocks(k))
    vv = with_prev(blocks(v))
    s = jnp.einsum('bnidhe,bnjdhe->bndhij', qb, kk) * E ** -0.5
    i = jnp.arange(span)[:, None]
    j = jnp.arange(2 * span)[None, :]
    rel = span + i - j
    valid = ((rel >= 0) & (rel <= span))[None] & ((jnp.arange(nb)[:, None, None] * span + j - span) >= 0)
    s = jnp.where(valid[None, :, None, None], s, -jnp.inf)
    m = s.max(-1, keepdims=True)
    p = jnp.exp(s - m)
    den = p.sum(-1)
    den_t = jnp.transpose(den, (0, 1, 4, 2, 3))
    o = jnp.einsum('bndhij,bnjdhe->bnidhe', p, vv) / den_t[..., None]
    lse = jnp.transpose(m[..., 0], (0, 1, 4, 2, 3)) + jnp.log(den_t)
    o = o.reshape(B, nb * window, H, E)[:, :S]
    lse = lse.reshape(B, nb * window, H)[:, :S]
    return o, lse

def gla_chunked(q, k, v, lg):
    B, H, S, dk = q.shape
    dv = v.shape[-1]
    L = GLA_CHUNK
    q = q * dk ** -0.5
    causal = jnp.tril(jnp.ones((L, L), bool))

    def step(state, inp):
        qc, kc, vc, gc = inp
        b = jnp.cumsum(gc, axis=2)
        diff = jnp.where(causal[:, :, None], b[:, :, :, None, :] - b[:, :, None, :, :], -jnp.inf)
        att = jnp.einsum('bhtsd,bhsd->bhts', qc[:, :, :, None, :] * jnp.exp(diff), kc)
        o = jnp.einsum('bhts,bhsv->bhtv', att, vc) + jnp.einsum('bhtd,bhdv->bhtv', qc * jnp.exp(b), state)
        b_last = b[:, :, -1:]
        state = jnp.exp(b_last[:, :, 0])[..., None] * state + jnp.einsum('bhsd,bhsv->bhdv', kc * jnp.exp(b_last - b), vc)
        return state, o

    s0 = jnp.zeros((B, H, dk, dv), q.dtype)
    _, o = lax.scan(step, s0, tuple(to_chunks(t, L) for t in (q, k, v, lg)))
    return from_chunks(o)

def token_mixer(x, w_in, ml_i_bias, ml_f_bias, ml_norm_w, ssm_conv_w, ssm_conv_b, ssm_dt_bias,
                ssm_a_log, ssm_d, ssm_norm_w, gla_gate_w2, gla_gate_b, gla_norm_w, w_out):
    B, S, _ = x.shape
    f32 = jnp.float32
    h = jnp.einsum('bsd,de->bse', x, w_in)
    parts = jnp.split(h, np.cumsum(IN_SIZES)[:-1].tolist(), axis=-1)
    (mq, mk, mv, mo, mi, mf, sz, sxbc, sdt, aq, ak, av, gq, gk, gv, gr, ga) = [p.astype(f32) for p in parts]

    def heads_first(t, n):
        return t.reshape(B, S, n, -1).transpose(0, 2, 1, 3)

    li = (mi + ml_i_bias.astype(f32)).transpose(0, 2, 1)
    lf = jax.nn.log_sigmoid(mf + ml_f_bias.astype(f32)).transpose(0, 2, 1)
    h_ml = mlstm_chunked(heads_first(mq, ML_HEADS), heads_first(mk, ML_HEADS), heads_first(mv, ML_HEADS), li, lf)
    y_ml = jax.nn.sigmoid(mo) * head_norm(h_ml.transpose(0, 2, 1, 3), ml_norm_w.astype(f32), True)

    xbc = jax.nn.silu(causal_conv(sxbc, ssm_conv_w.astype(f32), ssm_conv_b.astype(f32)))
    sx, sB, sC = jnp.split(xbc, [SSM_W, SSM_W + SSM_GROUPS * SSM_N], axis=-1)
    dt = jax.nn.softplus(sdt + ssm_dt_bias.astype(f32))
    A = -jnp.exp(ssm_a_log.astype(f32))
    y = ssd(sx.reshape(B, S, SSM_HEADS, SSM_P), dt, A, sB.reshape(B, S, SSM_GROUPS, SSM_N),
            sC.reshape(B, S, SSM_GROUPS, SSM_N), ssm_d.astype(f32))
    y = y.reshape(B, S, SSM_W) * jax.nn.silu(sz)
    y_ssm = y * lax.rsqrt(jnp.mean(y * y, -1, keepdims=True) + LN_EPS) * ssm_norm_w.astype(f32)

    pos = jnp.arange(S)
    q = rope(aq.reshape(B, S, AT_HEADS, AT_DH), pos)
    k = rope(ak.reshape(B, S, AT_HEADS, AT_DH), pos)
    v = av.reshape(B, S, AT_HEADS, AT_DH)
    outs, lses = zip(*[dilated_branch(q, k, v, w, d) for (w, d) in DILATED])
    wts = jax.nn.softmax(jnp.stack(lses), axis=0)
    y_at = jnp.einsum('gbsh,gbshe->bshe', wts, jnp.stack(outs)).reshape(B, S, AT_W)

    lg = jax.nn.log_sigmoid(ga @ gla_gate_w2.astype(f32) + gla_gate_b.astype(f32)) / GLA_TAU
    o = gla_chunked(heads_first(gq, GLA_HEADS), heads_first(gk, GLA_HEADS), heads_first(gv, GLA_HEADS),
                    heads_first(lg, GLA_HEADS))
    y_gla = head_norm(o.transpose(0, 2, 1, 3), gla_norm_w.astype(f32), False) * jax.nn.silu(gr)

    y = jnp.concatenate([y_ml, y_ssm, y_at, y_gla], axis=-1).astype(x.dtype)
    return jnp.einsum('bse,ed->bsd', y, w_out)

def moe(x, router_w, router_bias, w_gate, w_up, w_down, sh_gate, sh_up, sh_down):
    B, S, D = x.shape
    xf = x.reshape(-1, D)
    T = xf.shape[0]
    E = N_EXPERTS
    scores = jax.nn.sigmoid((xf @ router_w).astype(jnp.float32))
    sel = scores + router_bias.astype(jnp.float32)
    grp_score = lax.top_k(sel.reshape(T, N_GROUPS, E // N_GROUPS), 2)[0].sum(-1)
    _, top_g = lax.top_k(grp_score, TOPK_GROUPS)
    gmask = (top_g[..., None] == jnp.arange(N_GROUPS)).any(1)
    sel = jnp.where(jnp.repeat(gmask, E // N_GROUPS, axis=1), sel, -jnp.inf)
    _, top_e = lax.top_k(sel, TOP_K)
    g = jnp.take_along_axis(scores, top_e, axis=1)
    g = g / g.sum(-1, keepdims=True) * ROUTED_SCALE
    M = T * TOP_K
    e_flat = top_e.reshape(-1)
    tok_flat = jnp.repeat(jnp.arange(T, dtype=jnp.int32), TOP_K)
    order = jnp.argsort(e_flat)
    e_sorted = e_flat[order]
    tok_sorted = tok_flat[order]
    g_sorted = g.reshape(-1)[order]
    counts = jnp.zeros((E,), jnp.int32).at[e_flat].add(1)
    start = jnp.cumsum(counts) - counts
    padded = (counts + MOE_BLOCK - 1) // MOE_BLOCK * MOE_BLOCK
    pend = jnp.cumsum(padded)
    pstart = pend - padded
    dest = pstart[e_sorted] + jnp.arange(M, dtype=jnp.int32) - start[e_sorted]
    P = M + E * MOE_BLOCK
    nblk = P // MOE_BLOCK
    row_tok = jnp.full((P,), T, jnp.int32).at[dest].set(tok_sorted)
    row_gate = jnp.zeros((P,), g.dtype).at[dest].set(g_sorted)
    blk_exp = jnp.minimum(jnp.searchsorted(pend, jnp.arange(nblk, dtype=jnp.int32) * MOE_BLOCK, side='right'), E - 1)
    x_pad = jnp.concatenate([xf, jnp.zeros((1, D), xf.dtype)], axis=0)

    def body(acc, inp):
        tok, gate, e = inp
        xb = x_pad[tok]
        hb = jax.nn.silu(xb @ w_gate[e]) * (xb @ w_up[e])
        yb = (hb @ w_down[e]) * gate[:, None].astype(xb.dtype)
        return acc.at[tok].add(yb), None

    acc, _ = lax.scan(body, jnp.zeros((T + 1, D), x.dtype),
                      (row_tok.reshape(nblk, MOE_BLOCK), row_gate.reshape(nblk, MOE_BLOCK), blk_exp))
    shared = (jax.nn.silu(xf @ sh_gate) * (xf @ sh_up)) @ sh_down
    return (acc[:T] + shared).reshape(B, S, D)

def setup_inputs(seed: int = 0) -> dict:
    key = jax.random.key(seed)
    ks = iter(jax.random.split(key, 32))
    f32 = jnp.float32
    L = DEPTH
    D = D_MODEL

    def nrm(shape, scale):
        return jax.random.normal(next(ks), shape, f32) * scale

    x = nrm((BATCH, SEQ, D), 1.0)
    w_in = nrm((L, D, D_IN), D ** -0.5)
    ml_i_bias = nrm((L, ML_HEADS), 0.1)
    ml_f_bias = jnp.linspace(3.0, 6.0, ML_HEADS, dtype=f32)[None] + nrm((L, ML_HEADS), 0.1)
    ml_norm_w = 1.0 + nrm((L, ML_W), 0.02)
    ssm_conv_w = nrm((L, SSM_CONV, SSM_CONV_DIM), SSM_CONV ** -0.5)
    ssm_conv_b = nrm((L, SSM_CONV_DIM), 0.02)
    dt0 = jnp.exp(jax.random.uniform(next(ks), (L, SSM_HEADS), f32, math.log(1e-3), math.log(1e-1)))
    ssm_dt_bias = dt0 + jnp.log(-jnp.expm1(-dt0))
    ssm_a_log = jnp.log(jax.random.uniform(next(ks), (L, SSM_HEADS), f32, 1.0, 16.0))
    ssm_d = 1.0 + nrm((L, SSM_HEADS), 0.1)
    ssm_norm_w = 1.0 + nrm((L, SSM_W), 0.02)
    gla_gate_w2 = nrm((L, GLA_GATE_RANK, GLA_HEADS * GLA_DK), GLA_GATE_RANK ** -0.5)
    gla_gate_b = nrm((L, GLA_HEADS * GLA_DK), 0.1)
    gla_norm_w = 1.0 + nrm((L, GLA_W), 0.02)
    w_out = nrm((L, D_MIX, D), D_MIX ** -0.5 * BETA)
    ln1_g = 1.0 + nrm((L, D), 0.02)
    ln1_b = nrm((L, D), 0.02)
    router_w = nrm((L, D, N_EXPERTS), D ** -0.5)
    router_bias = nrm((L, N_EXPERTS), 0.01)
    exp_w_gate = nrm((L, N_EXPERTS, D, D_EXPERT), D ** -0.5)
    exp_w_up = nrm((L, N_EXPERTS, D, D_EXPERT), D ** -0.5)
    exp_w_down = nrm((L, N_EXPERTS, D_EXPERT, D), D_EXPERT ** -0.5 * BETA)
    sh_w_gate = nrm((L, D, D_SHARED), D ** -0.5)
    sh_w_up = nrm((L, D, D_SHARED), D ** -0.5)
    sh_w_down = nrm((L, D_SHARED, D), D_SHARED ** -0.5 * BETA)
    ln2_g = 1.0 + nrm((L, D), 0.02)
    ln2_b = nrm((L, D), 0.02)
    return {'x': x, 'w_in': w_in, 'ml_i_bias': ml_i_bias, 'ml_f_bias': ml_f_bias, 'ml_norm_w': ml_norm_w,
            'ssm_conv_w': ssm_conv_w, 'ssm_conv_b': ssm_conv_b, 'ssm_dt_bias': ssm_dt_bias,
            'ssm_a_log': ssm_a_log, 'ssm_d': ssm_d, 'ssm_norm_w': ssm_norm_w,
            'gla_gate_w2': gla_gate_w2, 'gla_gate_b': gla_gate_b, 'gla_norm_w': gla_norm_w,
            'w_out': w_out, 'ln1_g': ln1_g, 'ln1_b': ln1_b, 'router_w': router_w, 'router_bias': router_bias,
            'exp_w_gate': exp_w_gate, 'exp_w_up': exp_w_up, 'exp_w_down': exp_w_down,
            'sh_w_gate': sh_w_gate, 'sh_w_up': sh_w_up, 'sh_w_down': sh_w_down,
            'ln2_g': ln2_g, 'ln2_b': ln2_b}

def reference(x, w_in, ml_i_bias, ml_f_bias, ml_norm_w, ssm_conv_w, ssm_conv_b, ssm_dt_bias, ssm_a_log,
              ssm_d, ssm_norm_w, gla_gate_w2, gla_gate_b, gla_norm_w, w_out, ln1_g, ln1_b, router_w,
              router_bias, exp_w_gate, exp_w_up, exp_w_down, sh_w_gate, sh_w_up, sh_w_down, ln2_g, ln2_b):
    for l in range(DEPTH):
        y = token_mixer(x, w_in[l], ml_i_bias[l], ml_f_bias[l], ml_norm_w[l], ssm_conv_w[l], ssm_conv_b[l],
                        ssm_dt_bias[l], ssm_a_log[l], ssm_d[l], ssm_norm_w[l], gla_gate_w2[l], gla_gate_b[l],
                        gla_norm_w[l], w_out[l])
        x = layer_norm(ALPHA * x + y, ln1_g[l], ln1_b[l])
        y = moe(x, router_w[l], router_bias[l], exp_w_gate[l], exp_w_up[l], exp_w_down[l],
                sh_w_gate[l], sh_w_up[l], sh_w_down[l])
        x = layer_norm(ALPHA * x + y, ln2_g[l], ln2_b[l])
    return x


_drawn_inputs = setup_inputs


def setup_inputs(seed=0):
    import zlib

    import numpy as np

    out = dict(_drawn_inputs(seed))
    spreads = {}
    factors = {'ml_i_bias': 180.14, 'ml_norm_w': 4.495, 'ssm_norm_w': 2.984, 'gla_norm_w': 6.394}
    for name, (base, spread) in spreads.items():
        noise = np.random.default_rng([zlib.crc32(name.encode()), seed]).standard_normal(out[name].shape)
        drawn = base * np.exp(spread * noise) if base else spread * noise
        out[name] = jnp.asarray(drawn.astype(out[name].dtype))
    for name, factor in factors.items():
        out[name] = (out[name] * factor).astype(out[name].dtype)
    return out
```

```python
from contextlib import ExitStack

import concourse.bass as bass
from concourse import mybir

F32 = mybir.dt.float32
I32 = mybir.dt.int32
ALU = mybir.AluOpType
ACT = mybir.ActivationFunctionType
AX = mybir.AxisListType.X

P = 128
T = 256
NT = T // P
D = 1024
KD = D // P
DEPTH = 2
H = 4
DH = 64
DK = 32
EXPERTS = 64
PAIRS = EXPERTS // 2
TOP_K = 8
GROUPS = 8
F = 256
CAP = 64
ROUNDS = T // CAP
ALPHA = (2 * DEPTH) ** 0.25
EPS = 1e-5
TAU = 16.0
BLK = 32
NB = T // BLK
SCORE = 3 * P
CLAMP = 80.0

GROUPS_IN = [
    ("small", P, True), ("mlstm_qk", 512, True), ("conv", 512, True), ("gla_qk", 256, True),
    ("mlstm_vo", 512, False), ("gla_vr", 512, False), ("att_qk", 512, False), ("att_v_ssm_z", 512, False),
]
WIN_COLS = sum(g[1] for g in GROUPS_IN)

ROW = {}
_at = 0
for _name, _n in (("ln1_g", D), ("ln1_b", D), ("ln2_g", D), ("ln2_b", D), ("ml_norm", 256), ("ssm_norm", 256),
                  ("gla_norm", 256), ("ssm_d", H), ("router_bias", EXPERTS)):
    ROW[_name] = slice(_at, _at + _n)
    _at += _n
ROWS = _at
COL = {"bias": slice(0, 1), "a_log": slice(1, 2), "gla_b": slice(2, 3), "taps": slice(3, 19),
       "conv_b": slice(19, 23), "gate_w2": slice(23, 151)}
COLS = 151
CST = {}
_at = 0
for _name, _n in (("ident", P), ("before", P), ("ones", T), ("causal", SCORE), ("att_add", SCORE),
                  ("att_mul", SCORE), ("cos", NT * 32), ("sin", NT * 32), ("slot", CAP), ("head", H * P),
                  ("tri", BLK), ("earlier", GROUPS * GROUPS)):
    CST[_name] = slice(_at, _at + _n)
    _at += _n
CSTS = _at


def hybrid_kernel(nc, x_in, w_in, cols_in, rows_in, cst_in, w_out, router_w, e_gate, e_up, e_down,
                  sh_gate, sh_up, sh_down, out, debug=None, layers=DEPTH):
    with ExitStack() as ctx:
        def sb(name, n, dt=F32):
            return ctx.enter_context(nc.sbuf_tensor(name, [P, n], dt))

        def sem(name):
            return ctx.enter_context(nc.semaphore(name))

        wbuf = sb("wbuf", 24576)
        stage = sb("stage", 8192)
        X = sb("X", NT * D)
        XT = sb("XT", KD * T)
        ACC = sb("ACC", NT * D)
        rowp = sb("rowp", ROWS)
        colp = sb("colp", COLS)
        cst = sb("cst", CSTS)
        misc = sb("misc", 5632)
        last_pair2 = sb("last_pair2", 1, I32)

        def view(t, at, *dims):
            n = 1
            for d in dims:
                n *= d
            ap = t[:, at:at + n]
            if len(dims) == 1:
                return ap
            names = "abcd"[:len(dims)]
            return ap.rearrange("p (" + " ".join(names) + ") -> p " + " ".join(names),
                                **{c: d for c, d in zip(names, dims)})

        Xv = view(X, 0, NT, D)
        XT3 = view(XT, 0, KD, T)
        ACCv = view(ACC, 0, NT, D)
        wgu = [view(wbuf, 8192 * b, 2, 2, KD, F) for b in range(2)]
        wdn = [view(wbuf, 16384 + 4096 * b, 2, 2, D) for b in range(2)]

        pos = [8192]

        def scr(*dims):
            n = 1
            for d in dims:
                n *= d
            at = pos[0]
            pos[0] += n
            assert pos[0] <= 24576
            return view(wbuf, at, *dims)

        mqkT = scr(4, T)
        mvx = scr(NT, H, DH + 1)
        mo = scr(NT, 256)
        convin = scr(4, T + 3)
        convout = scr(4, T)
        gqkT = scr(2, T)
        gv = scr(NT, 256)
        gr = scr(NT, 256)
        aqk = scr(NT, 8, 2, 32)
        rot = scr(NT, 8, 2, 32)
        rtmp = scr(NT, 8, 32)
        aqkT = scr(4, T)
        av = scr(NT, 256)
        sz = scr(NT, 256)
        sx = scr(NT, 256)
        xdt = scr(NT, 256)
        gdec = scr(T)
        gb = scr(T)
        gd1 = scr(T)
        gd2 = scr(T)
        gl = scr(T)
        ge = scr(3, T)
        mpos = [0]

        def mscr(*dims):
            n = 1
            for d in dims:
                n *= d
            at = mpos[0]
            mpos[0] += n
            assert mpos[0] <= 5632, mpos
            return view(misc, at, *dims)

        z = mscr(T)
        lt = mscr(T)
        lsg = mscr(T)
        lsp = mscr(T)
        R = mscr(T)
        C0 = mscr(T)
        MR = mscr(T)
        RC = mscr(NT, P)
        nac = mscr(NT, H)
        enm = mscr(NT, H)
        acol = mscr(1)
        rm = mscr(2, 2)
        rden = mscr(NT, H)
        st1 = mscr(NT, H)
        st2 = mscr(NT, H)
        st3 = mscr(NT, H)
        E = [mscr(SCORE) for _ in range(2)]
        Pm = [mscr(SCORE) for _ in range(2)]
        kx = view(stage, 0, 28 * BLK)
        PT = view(stage, 1024, H, SCORE)
        PTa = [view(stage, 2560 + SCORE * i, SCORE) for i in range(2)]
        tmp = view(stage, 4096, NT, D)
        wsm = view(stage, 0, KD, P)
        mpos[0] = 0
        Sel = [mscr(NT, 2, CAP) for _ in range(2)]
        SelG = [mscr(NT, 2, CAP) for _ in range(2)]
        SelT = mscr(T)
        XG = mscr(KD, 2 * CAP)
        HS = mscr(F)
        Hh = mscr(F)
        HT = mscr(2, 2 * CAP)
        YS = mscr(D)
        G = mscr(NT, EXPERTS)
        rank = mscr(NT, EXPERTS)
        SC = mscr(NT, EXPERTS)
        r0 = 1280
        selm = view(misc, r0, NT, EXPERTS)
        selr = view(misc, r0 + 128, NT, EXPERTS)
        m8 = view(misc, r0 + 256, NT, GROUPS, 8)
        grp = view(misc, r0 + 384, NT, GROUPS)
        cmp1 = view(misc, r0 + 400, NT, GROUPS, GROUPS)
        cmp2 = view(misc, r0 + 528, NT, GROUPS, GROUPS)
        gmask = view(misc, r0 + 656, NT, GROUPS)
        t8 = view(misc, r0 + 672, NT, 8)
        Mk = view(misc, r0 + 688, NT, EXPERTS)
        gs = view(misc, r0 + 816, NT)
        cnt = view(misc, r0 + 818, 2)
        shh = view(misc, r0 + 832, NT, F)
        lnb = sb("lnb", 64)
        bst = view(lnb, 0, NT, 2, 6)
        bag = view(lnb, 24, NT, 2)
        rstd = view(lnb, 28, NT)

        def C(name):
            return cst[:, CST[name]]

        ident = C("ident")
        before = C("before")
        ones = C("ones")
        sh_w = view(stage, 0, 2, KD, F)
        sh_d = view(stage, 4096, 2, D)
        rw = view(stage, 6144, KD, EXPERTS)
        wo = view(stage, 0, KD, D)
        shT = view(stage, 6656, 2, T)

        ps = [ctx.enter_context(nc.psum_tensor(f"ps{i}", [P, 512], F32)) for i in range(4)]
        psA = ctx.enter_context(nc.psum_tensor("psA", [P, 4, 512], F32))
        ps = [t[:, :] for t in ps] + [psA[:, i, :] for i in range(4)]

        cst_loaded = sem("cst_loaded")
        gu_loaded = [sem(f"gu_loaded{b}") for b in range(2)]
        dn_loaded = [sem(f"dn_loaded{b}") for b in range(2)]
        gu_used = [sem(f"gu_used{b}") for b in range(2)]
        dn_used = [sem(f"dn_used{b}") for b in range(2)]
        layer_done = sem("layer_done")
        layer_open = sem("layer_open")
        out_stored = sem("out_stored")
        sp_held = sem("sp_held")
        pool_held = sem("pool_held")
        cleared = []

        def lsem(name):
            s = sem(name)
            cleared.append(s)
            return s

        small_loaded = lsem("small_loaded")
        in_loaded = [lsem(f"in_loaded{b}") for b in range(2)]
        stage_used = lsem("stage_used")
        wo_loaded = lsem("wo_loaded")
        shared_loaded = lsem("shared_loaded")
        stage_free = lsem("stage_free")
        mixers_done = lsem("mixers_done")
        proj_done = lsem("proj_done")
        proj_read = lsem("proj_read")
        xt_done = lsem("xt_done")
        xt_read = lsem("xt_read")
        gate_rows = lsem("gate_rows")
        gla_gate = lsem("gla_gate")
        logs_ready = lsem("logs_ready")
        gla_logs = lsem("gla_logs")
        rows_ready = lsem("rows_ready")
        cols_done = lsem("cols_done")
        cols_ready = lsem("cols_ready")
        conv_raw = lsem("conv_raw")
        conv_ready = lsem("conv_ready")
        sxt_done = lsem("sxt_done")
        sx_ready = lsem("sx_ready")
        rope_ready = lsem("rope_ready")
        qkt_done = lsem("qkt_done")
        qkt_read = lsem("qkt_read")
        score_done = lsem("score_done")
        score_read = lsem("score_read")
        bc_done = lsem("bc_done")
        bc_read = lsem("bc_read")
        arg_ready = lsem("arg_ready")
        exp_ready = lsem("exp_ready")
        prob_ready = lsem("prob_ready")
        prob_used = lsem("prob_used")
        at_arg = lsem("at_arg")
        at_exp = lsem("at_exp")
        at_prob = lsem("at_prob")
        at_tr = lsem("at_tr")
        at_trc = lsem("at_trc")
        at_used = lsem("at_used")
        o_done = lsem("o_done")
        o_read = lsem("o_read")
        gla_arg = lsem("gla_arg")
        gla_exp = lsem("gla_exp")
        gla_qk = lsem("gla_qk")
        gla_sc = lsem("gla_sc")
        gla_pt = lsem("gla_pt")
        rms_in = lsem("rms_in")
        rms_out = lsem("rms_out")
        y_ready = lsem("y_ready")
        yt_done = lsem("yt_done")
        yt_read = lsem("yt_read")
        op_done = lsem("op_done")
        op_read = lsem("op_read")
        x1_ready = lsem("x1_ready")
        rt_done = lsem("rt_done")
        score_sig = lsem("score_sig")
        mask_ready = lsem("mask_ready")
        rank_done = lsem("rank_done")
        rounds_ready = lsem("rounds_ready")
        sh_done = lsem("sh_done")
        sh_silu = lsem("sh_silu")
        sh_hid = lsem("sh_hid")
        sht_done = lsem("sht_done")
        sht_read = lsem("sht_read")
        sho_done = lsem("sho_done")
        dve_own = lsem("dve_own")
        act_own = lsem("act_own")
        sel_ready = lsem("sel_ready")
        selg_ready = lsem("selg_ready")
        rank_next = lsem("rank_next")
        gathered = lsem("gathered")
        xg_act = lsem("xg_act")
        xg_dve = lsem("xg_dve")
        gu_done = lsem("gu_done")
        silu_done = lsem("silu_done")
        h_done = lsem("h_done")
        ht_tr = lsem("ht_tr")
        ht_done = lsem("ht_done")
        st_tr = lsem("st_tr")
        st_done = lsem("st_done")
        dn_done = lsem("dn_done")
        ys_act = lsem("ys_act")
        ys_dve = lsem("ys_dve")
        sc_done = lsem("sc_done")
        acc_done = lsem("acc_done")

        ACC0 = 4
        block = ctx.enter_context(nc.Block())

        def head_rows(h):
            return slice(DH * (h % 2), DH * (h % 2) + DH)

        @block.sync
        def _(sp):
            sp.dma_start(cst[:, :], cst_in).then_inc(cst_loaded, 16)
            sp.dma_start(Xv, x_in.rearrange("(t p) d -> p t d", p=P)).then_inc(cst_loaded, 16)
            before_dp = sp.alloc_register("sp_before")
            sp.reg_mov(before_dp, 0)
            with sp.Fori(0, layers) as l:
                base = sp.snap(before_dp)
                sp.dma_start(rowp[:, :], rows_in[l].partition_broadcast(P)).then_inc(small_loaded, 16)
                sp.dma_start(colp[:, :], cols_in[l]).then_inc(small_loaded, 16)
                at = 0
                for gi, (name, n, _) in enumerate(GROUPS_IN):
                    if gi >= 2:
                        sp.wait_ge(stage_used, gi - 1)
                    b = gi % 2
                    sp.dma_start(stage[:, 4096 * b:4096 * b + KD * n],
                                 w_in[l][:, at:at + KD * n]).then_inc(in_loaded[b], 16)
                    at += KD * n
                    if gi == 1:
                        sp.wait_ge(gu_used[0], base + 1)
                        sp.sem_inc(sp_held, 1)
                        sp.dma_start(wgu[0][:, :, 0, :, :], e_gate[l][0]).then_inc(gu_loaded[0], 16)
                        sp.dma_start(wgu[0][:, :, 1, :, :], e_up[l][0]).then_inc(gu_loaded[0], 16)
                sp.wait_ge(stage_free, 1)
                sp.dma_start(wo, w_out[l].rearrange("(k p) d -> p k d", p=P)).then_inc(wo_loaded, 16)
                sp.wait_ge(mixers_done, 1)
                sp.wait_ge(gu_used[1], base + 1)
                sp.sem_inc(sp_held, 1)
                sp.dma_start(wgu[1][:, :, 0, :, :], e_gate[l][1]).then_inc(gu_loaded[1], 16)
                sp.dma_start(wgu[1][:, :, 1, :, :], e_up[l][1]).then_inc(gu_loaded[1], 16)
                sp.wait_ge(stage_free, 2)
                sp.dma_start(rw, router_w[l].rearrange("(p k) e -> p k e", k=KD)).then_inc(shared_loaded, 16)
                sp.dma_start(sh_w[:, 0], sh_gate[l].rearrange("(p k) f -> p k f", k=KD)).then_inc(shared_loaded, 16)
                sp.dma_start(sh_w[:, 1], sh_up[l].rearrange("(p k) f -> p k f", k=KD)).then_inc(shared_loaded, 16)
                sp.dma_start(sh_d, sh_down[l].rearrange("(p k) d -> p k d", k=2)).then_inc(shared_loaded, 16)
                sp.wait_ge(rounds_ready, 1)
                last = sp.value_load(last_pair2[0:1, 0:1], min_val=PAIRS // 2 - 1, max_val=ROUNDS * PAIRS // 2 - 1)
                pairs2 = last + 1

                def load_down(j, b):
                    sp.wait_ge(dn_used[b], base + j + 1)
                    sp.sem_inc(sp_held, 1)
                    sp.dma_start(wdn[b], e_down[l][(j * 2 + b) % PAIRS]).then_inc(dn_loaded[b], 16)

                with sp.Fori(0, last) as j:
                    for b in range(2):
                        load_down(j, b)
                        sp.wait_ge(gu_used[b], base + j + 2)
                        sp.sem_inc(sp_held, 1)
                        sp.dma_start(wgu[b][:, :, 0, :, :], e_gate[l][(j * 2 + 2 + b) % PAIRS]).then_inc(gu_loaded[b], 16)
                        sp.dma_start(wgu[b][:, :, 1, :, :], e_up[l][(j * 2 + 2 + b) % PAIRS]).then_inc(gu_loaded[b], 16)
                for b in range(2):
                    load_down(last, b)
                sp.reg_add(before_dp, before_dp, pairs2)
                sp.sem_inc(layer_done, 1)
                sp.wait_ge(layer_open, l + 1)
                sp.sem_inc(sp_held, 1)
            sp.dma_start(out.rearrange("(t p) d -> p t d", p=P), Xv).then_inc(out_stored, 16)
            sp.wait_ge(out_stored, 16)

        @block.gpsimd
        def _(pool):
            with pool.Fori(0, layers) as l:
                pool.wait_ge(layer_done, 4 * (l + 1))
                pool.sem_inc(pool_held, 1)
                for s in cleared:
                    pool.sem_clear(s)
                pool.sem_inc(layer_open, 1)

        @block.tensor
        def _(pe):
            before_dp = pe.alloc_register("pe_before")
            pe.reg_mov(before_dp, 0)
            for b in range(2):
                pe.sem_inc(gu_used[b], 1)
                pe.sem_inc(dn_used[b], 1)
            pe.wait_ge(cst_loaded, 32)

            def transpose_x(n0):
                xs = Xv.rearrange("p t (q k) -> p t k q", k=KD)
                for u in range(4):
                    if u >= 2:
                        pe.wait_ge(xt_read, n0 + u - 1)
                    for kk in range(2):
                        for t in range(NT):
                            at = kk * T + t * P
                            mm = pe.transpose(ps[u % 2][:, at:at + P], xs[:, t, 2 * u + kk, :], ident)
                    mm.then_inc(xt_done, 1)

            with pe.Fori(0, layers) as l:
                base = pe.snap(before_dp)
                transpose_x(0)
                pe.wait_ge(xt_read, 4)
                u = 0
                count = [0, 0]
                for gi, (name, n, chan) in enumerate(GROUPS_IN):
                    b = gi % 2
                    count[b] += 16
                    pe.wait_ge(in_loaded[b], count[b])
                    w = view(stage, 4096 * b, KD, n)
                    for h in range(max(n // 256, 1)):
                        if u >= 2:
                            pe.wait_ge(proj_read, u - 1)
                        bank = ps[u % 2]
                        if chan:
                            for m in range(min(2, n // P)):
                                for k in range(KD):
                                    c = (2 * h + m) * P
                                    mm = pe.matmul(bank[:, m * T:(m + 1) * T], w[:, k, c:c + P], XT3[:, k, :],
                                                   start=(k == 0), stop=(k == KD - 1))
                        else:
                            for k in range(KD):
                                mm = pe.matmul(bank, XT3[:, k, h * P:(h + 1) * P], w[:, k, :],
                                               start=(k == 0), stop=(k == KD - 1))
                        mm.then_inc(proj_done, 1)
                        u += 1
                    pe.wait_ge(proj_done, u)
                    pe.sem_inc(stage_used, 1)
                    if gi == 1:
                        pe.wait_ge(gate_rows, 1)
                        pe.matmul(ps[2][:, 0:T], colp[96:112, COL["gate_w2"]], z[96:112, :],
                                  start=True, stop=True).then_inc(gla_gate, 1)
                    if gi == 3:
                        pe.wait_ge(rows_ready, 1)
                        for t in range(NT):
                            mm = pe.transpose(ps[3][:, t * P:(t + 1) * P], R[:, t * P:(t + 1) * P], ident)
                        mm.then_inc(cols_done, 1)
                pe.wait_ge(conv_ready, 1)
                pe.wait_ge(cols_ready, 2)
                for t in range(NT):
                    for c in range(2):
                        mm = pe.transpose(ps[3][:, t * 256 + c * P:t * 256 + (c + 1) * P],
                                          convout[:, c, t * P:(t + 1) * P], ident)
                mm.then_inc(sxt_done, 1)
                pe.wait_ge(rope_ready, 1)
                rf = rot.rearrange("p t h s e -> p t (h s e)")
                for c in range(4):
                    for t in range(NT):
                        mm = pe.transpose(ps[4 + c // 2][:, (c % 2) * T + t * P:(c % 2) * T + (t + 1) * P],
                                          rf[:, t, c * P:(c + 1) * P], ident)
                mm.then_inc(qkt_done, 1)

                def transposed_scores(bank, keys, queries):
                    pe.matmul(bank[:, 0:T], keys[:, 0:P], queries[:, 0:T], start=True, stop=True)
                    return pe.matmul(bank[:, T:T + P], keys[:, P:T], queries[:, P:T], start=True, stop=True)

                def apply(out0, out1, p, values):
                    pe.matmul(out0, p[:, 0:P], values(0), start=True, stop=True)
                    pe.matmul(out1, p[:, P:2 * P], values(0), start=True, stop=False)
                    return pe.matmul(out1, p[:, 2 * P:3 * P], values(1), start=False, stop=True)

                def ml_scores(h):
                    if h == 0:
                        pe.wait_ge(proj_read, 14)
                        pe.wait_ge(sx_ready, 1)
                    if h >= 2:
                        pe.wait_ge(score_read, h - 1)
                        pe.wait_ge(bc_read, h - 1)
                    r = head_rows(h)
                    transposed_scores(ps[h % 2], mqkT[r, 2 + h // 2, :], mqkT[r, h // 2, :]).then_inc(score_done, 1)
                    pe.matmul(ps[2 + h % 2][:, 0:T], cst[0:H, CST["head"]][:, h * P:(h + 1) * P], MR[0:H, :],
                              start=True, stop=True).then_inc(bc_done, 1)

                def ml_apply(h):
                    if h == 0:
                        pe.wait_ge(qkt_read, 1)
                    pe.wait_ge(prob_ready, h + 1)
                    c = h * (DH + 1)
                    apply(ps[4][:, c:c + DH + 1], ps[5][:, c:c + DH + 1], Pm[h % 2],
                          lambda t: mvx[:, t, h, :]).then_inc(prob_used, 1)

                for h in range(H + 1):
                    if h < H:
                        ml_scores(h)
                    if h >= 1:
                        ml_apply(h - 1)
                for g in range(2):
                    r = slice(64 * g, 64 * g + 64)
                    mm = transposed_scores(ps[6 + g], convout[r, 2, :], convout[r, 3, :])
                mm.then_inc(score_done, 1)

                def ssm_decay(h):
                    pe.wait_ge(bc_read, H + h - 1)
                    pe.matmul(ps[2 + h % 2][:, 0:T], cst[64:64 + H, CST["head"]][:, h * P:(h + 1) * P],
                              R[64:64 + H, :], start=True, stop=True).then_inc(bc_done, 1)

                def ssm_apply(h):
                    if h == 0:
                        pe.wait_ge(o_read, 1)
                    pe.wait_ge(prob_ready, H + h + 1)
                    apply(ps[5][:, h * DH:(h + 1) * DH], ps[5][:, 256 + h * DH:256 + (h + 1) * DH], Pm[h % 2],
                          lambda t: xdt[:, t, h * DH:(h + 1) * DH]).then_inc(prob_used, 1)

                for h in range(H + 1):
                    if h < H:
                        ssm_decay(h)
                    if h >= 1:
                        ssm_apply(h - 1)

                def at_scores(h):
                    if h == 0:
                        pe.wait_ge(score_read, H)
                    if h >= 2:
                        pe.wait_ge(score_read, H + h - 1)
                    r = head_rows(h)
                    q, k = aqkT[r, h // 2, :], aqkT[r, 2 + h // 2, :]
                    pe.matmul(ps[h % 2][:, 0:P], q[:, 0:P], k[:, 0:P], start=True, stop=True)
                    pe.matmul(ps[h % 2][:, P:SCORE], q[:, P:T], k, start=True, stop=True).then_inc(score_done, 1)

                def at_transposes(h):
                    pe.wait_ge(at_prob, h + 1)
                    if h == 0:
                        pe.wait_ge(bc_read, 2 * H)
                    if h >= 2:
                        pe.wait_ge(at_trc, h - 1)
                    for i in range(3):
                        mm = pe.transpose(ps[2 + h % 2][:, i * P:(i + 1) * P], Pm[h % 2][:, i * P:(i + 1) * P], ident)
                    mm.then_inc(at_tr, 1)

                def at_apply(h):
                    pe.wait_ge(at_trc, h + 1)
                    apply(ps[4][:, h * DH:(h + 1) * DH], ps[4][:, 256 + h * DH:256 + (h + 1) * DH], PTa[h % 2],
                          lambda t: av[:, t, h * DH:(h + 1) * DH]).then_inc(at_used, 1)

                for h in range(H + 2):
                    if h < H:
                        at_scores(h)
                    if 1 <= h <= H:
                        at_transposes(h - 1)
                    if h >= 2:
                        at_apply(h - 2)

                pe.wait_ge(o_read, 3)
                pe.wait_ge(gla_qk, 1)
                for j in range(NB):
                    js = slice(BLK * j, BLK * (j + 1))
                    jj, t = j % 4, j // 4
                    col = BLK * j if t == 0 else 2 * P + BLK * jj
                    for h in range(H):
                        r = slice(DK * h, DK * (h + 1))
                        mm = pe.matmul(psA[BLK * jj:BLK * (jj + 1), h, col:col + BLK], ge[r, 1, js], ge[r, 0, js],
                                       start=True, stop=True)
                        k0 = BLK * (j * (j - 1) // 2)
                        if t == 0 and j > 0:
                            mm = pe.matmul(psA[0:BLK * j, h, col:col + BLK], kx[r, k0:k0 + BLK * j], ge[r, 2, js],
                                           start=True, stop=True)
                        if t == 1:
                            mm = pe.matmul(psA[:, h, BLK * j:BLK * j + BLK], kx[r, k0:k0 + P], ge[r, 2, js],
                                           start=True, stop=True)
                            if jj > 0:
                                mm = pe.matmul(psA[0:BLK * jj, h, col:col + BLK],
                                               kx[r, k0 + P:k0 + P + BLK * jj], ge[r, 2, js], start=True, stop=True)
                mm.then_inc(gla_sc, 1)
                pe.wait_ge(gla_pt, 1)
                for h in range(H):
                    mm = apply(ps[0][:, h * DH:(h + 1) * DH], ps[0][:, 256 + h * DH:256 + (h + 1) * DH], PT[:, h, :],
                               lambda t: gv[:, t, h * DH:(h + 1) * DH])
                mm.then_inc(o_done, 1)

                pe.wait_ge(y_ready, 1)
                for u in range(4):
                    if u >= 2:
                        pe.wait_ge(yt_read, u - 1)
                    for kk in range(2):
                        k = 2 * u + kk
                        for t in range(NT):
                            mm = pe.transpose(ps[2 + u % 2][:, kk * T + t * P:kk * T + (t + 1) * P],
                                              ACCv[:, t, k * P:(k + 1) * P], ident)
                    mm.then_inc(yt_done, 1)
                pe.wait_ge(yt_read, 4)
                pe.wait_ge(wo_loaded, 16)
                for t in range(NT):
                    for n in range(2):
                        bank = ps[4 + 2 * t + n]
                        for k in range(KD):
                            mm = pe.matmul(bank, XT3[:, k, t * P:(t + 1) * P], wo[:, k, n * 512:(n + 1) * 512],
                                           start=(k == 0), stop=(k == KD - 1))
                        mm.then_inc(op_done, 1)
                pe.wait_ge(op_done, 4)
                pe.sem_inc(stage_free, 1)

                pe.wait_ge(x1_ready, 1)
                transpose_x(4)
                pe.wait_ge(xt_read, 8)
                pe.wait_ge(shared_loaded, 64)
                for t in range(NT):
                    for k in range(KD):
                        mm = pe.matmul(ps[2][:, t * EXPERTS:(t + 1) * EXPERTS], XT3[:, k, t * P:(t + 1) * P],
                                       rw[:, k, :], start=(k == 0), stop=(k == KD - 1))
                mm.then_inc(rt_done, 1)
                for t in range(NT):
                    for k in range(KD):
                        mm = pe.matmul(ps[4 + t], XT3[:, k, t * P:(t + 1) * P], sh_w[:, :, k, :],
                                       start=(k == 0), stop=(k == KD - 1))
                    mm.then_inc(sh_done, 1)
                pe.wait_ge(mask_ready, 1)
                pe.matmul(ps[3][:, 0:EXPERTS], before, Mk[:, 0, :], start=True, stop=True)
                pe.matmul(ps[3][:, EXPERTS:2 * EXPERTS], ones[:, 0:P], Mk[:, 0, :], start=True, stop=False)
                pe.matmul(ps[3][:, EXPERTS:2 * EXPERTS], before, Mk[:, 1, :], start=False, stop=True)
                pe.matmul(ps[3][:, 2 * EXPERTS:3 * EXPERTS], ones[:, 0:P], Mk[:, 0, :], start=True, stop=False)
                pe.matmul(ps[3][:, 2 * EXPERTS:3 * EXPERTS], ones[:, 0:P], Mk[:, 1, :],
                          start=False, stop=True).then_inc(rank_done, 1)
                pe.wait_ge(sh_hid, 2)
                for t in range(NT):
                    for k in range(2):
                        mm = pe.transpose(ps[7][:, k * T + t * P:k * T + (t + 1) * P],
                                          shh[:, t, :].rearrange("p (f k) -> p k f", k=2)[:, k, :], ident)
                mm.then_inc(sht_done, 1)
                pe.wait_ge(sht_read, 1)
                for t in range(NT):
                    for n in range(2):
                        for k in range(2):
                            mm = pe.matmul(ps[4 + 2 * t + n], shT[:, k, t * P:(t + 1) * P],
                                           sh_d[:, k, n * 512:(n + 1) * 512], start=(k == 0), stop=(k == 1))
                        mm.then_inc(sho_done, 1)

                xs = Xv.rearrange("p t (q k) -> p t k q", k=KD)

                def gather(g, b):
                    pe.wait_ge(sel_ready, g + 1)
                    for q in range(2):
                        for k in range(4 * q, 4 * q + 4):
                            for t in range(NT):
                                mm = pe.matmul(ps[1 + q][:, (k % 4) * P:(k % 4 + 1) * P], xs[:, t, k, :],
                                               Sel[b][:, t, :, :], start=(t == 0), stop=(t == NT - 1))
                        mm.then_inc(gathered, 1)

                def scatter(g):
                    pe.wait_ge(st_done, g + 1)
                    pe.wait_ge(ys_act, g + 1)
                    pe.wait_ge(ys_dve, g + 1)
                    for t in range(NT):
                        for n in range(2):
                            q = 2 * t + n
                            pe.wait_ge(acc_done, 4 * g + q - 1 + ACC0)
                            pe.matmul(ps[5 + q % 2], SelT[:, t * P:(t + 1) * P], YS[:, n * 512:(n + 1) * 512],
                                      start=True, stop=True).then_inc(sc_done, 1)

                pe.wait_ge(rounds_ready, 1)
                last = pe.value_load(last_pair2[0:1, 0:1], min_val=PAIRS // 2 - 1, max_val=ROUNDS * PAIRS // 2 - 1)
                pairs2 = last + 1
                pe.sem_inc(ht_tr, 1)
                pe.sem_inc(dn_done, 2)
                pe.wait_ge(acc_done, ACC0)
                gather(0, 0)
                with pe.Fori(0, pairs2) as j:
                    for b in range(2):
                        g = 2 * j + b
                        pe.wait_ge(gu_loaded[b], (base + j + 1) * 32)
                        pe.wait_ge(xg_act, g + 1)
                        pe.wait_ge(xg_dve, g + 1)
                        pe.wait_ge(h_done, g + 1)
                        for k in range(KD):
                            for e in range(2):
                                mm = pe.matmul(ps[0][64 * e:64 * e + CAP, :],
                                               XG[:, k, CAP * e:CAP * (e + 1)], wgu[b][:, e, :, k, :],
                                               start=(k == 0), stop=(k == KD - 1))
                        mm.then_inc(gu_done, 1)
                        gather(g + 1, 1 - b)
                        pe.wait_ge(h_done, g + 2)
                        pe.wait_ge(ht_done, g + 1)
                        pe.wait_ge(st_done, g + 1)
                        for k in range(2):
                            mm = pe.transpose(ps[7][:, k * P:(k + 1) * P],
                                              Hh.rearrange("p (f k) -> p k f", k=2)[:, k, :], ident)
                        mm.then_inc(ht_tr, 1)
                        pe.wait_ge(gu_done, g + 1)
                        pe.sem_inc(gu_used[b], 1)
                        scatter(g)
                        pe.wait_ge(selg_ready, g + 1)
                        pe.wait_ge(ht_done, g + 2)
                        for t in range(NT):
                            mm = pe.transpose(ps[7][:, T + t * P:T + (t + 1) * P], SelG[b][:, t, :, :], ident)
                        mm.then_inc(st_tr, 1)
                        pe.wait_ge(dn_loaded[b], (base + j + 1) * 16)
                        for n in range(2):
                            for k in range(2):
                                for e in range(2):
                                    mm = pe.matmul(ps[3 + n][64 * e:64 * e + CAP, :], HT[:, k, CAP * e:CAP * (e + 1)],
                                                   wdn[b][:, e, k, n * 512:(n + 1) * 512],
                                                   start=(k == 0), stop=(k == 1))
                            mm.then_inc(dn_done, 1)
                        pe.wait_ge(dn_done, 2 * g + 4)
                        pe.sem_inc(dn_used[b], 1)
                scatter(2 * pairs2)
                pe.reg_add(before_dp, before_dp, pairs2)
                pe.sem_inc(layer_done, 1)
                pe.wait_ge(layer_open, l + 1)

        @block.scalar
        def _(act):
            own = [0]

            def link(ins):
                own[0] += 1
                ins.then_inc(act_own, 1)
                act.wait_ge(act_own, own[0])

            def copy(o, i):
                return act.activation(o, i, ACT.Copy)

            act.wait_ge(cst_loaded, 32)
            with act.Fori(0, layers) as l:
                own[0] = 0
                for u in range(0, 4, 2):
                    act.wait_ge(xt_done, u + 1)
                    if u:
                        act.wait_ge(xt_read, u)
                    copy(XT3[:, 2 * u:2 * u + 2, :], ps[0].rearrange("p (k t) -> p k t", k=2)).then_inc(xt_read, 1)
                act.wait_ge(small_loaded, 32)
                act.wait_ge(proj_done, 1)
                link(act.activation(z, ps[0][:, 0:T], ACT.Identity, bias=colp[:, COL["bias"]]))
                act.sem_inc(proj_read, 1)
                act.sem_inc(gate_rows, 1)

                def log1p_exp(o, i):
                    link(act.activation(o, i, ACT.Abs))
                    link(act.activation(o, o, ACT.Exp, scale=-1.0))
                    link(act.activation(o, o, ACT.Ln, bias=1.0))

                log1p_exp(lt, z)
                link(act.activation(acol[64:64 + H, :], colp[64:64 + H, COL["a_log"]], ACT.Exp))
                act.sem_inc(logs_ready, 1)

                def unit(u, *moves):
                    act.wait_ge(proj_done, u + 1)
                    for ins in moves:
                        last = ins()
                    last.then_inc(proj_read, 1)

                for i, u in enumerate((1, 2)):
                    unit(u, lambda: copy(mqkT[:, 2 * i:2 * i + 2, :], ps[u % 2].rearrange("p (m t) -> p m t", m=2)))
                act.wait_ge(gla_gate, 1)
                link(act.activation(gdec, ps[2][:, 0:T], ACT.Identity, bias=colp[:, COL["gla_b"]]))
                log1p_exp(gl, gdec)
                act.sem_inc(gla_logs, 1)
                for i, u in enumerate((3, 4)):
                    unit(u, lambda: copy(convin[:, 2 * i:2 * i + 2, 3:T + 3],
                                         ps[u % 2].rearrange("p (m t) -> p m t", m=2)))
                unit(5, lambda: copy(gqkT, ps[1].rearrange("p (m t) -> p m t", m=2)))
                act.wait_ge(cols_done, 1)
                link(act.activation(enm, ps[3].rearrange("p (t c) -> p t c", c=P)[:, 0:NT, 32:32 + H], ACT.Exp, scale=-1.0))
                act.sem_inc(cols_ready, 1)
                act.wait_ge(dve_own, 1)
                for t in range(NT):
                    b = ps[t]
                    unit(6 + t, lambda: copy(mvx[:, t, :, 0:DH], b[:, 0:256].rearrange("p (h d) -> p h d", h=H)),
                         lambda: act.activation(mo[:, t, :], b[:, 256:512], ACT.Sigmoid))
                for t in range(NT):
                    b = ps[t]
                    unit(8 + t, lambda: copy(gv[:, t, :], b[:, 0:256]),
                         lambda: act.activation(gr[:, t, :], b[:, 256:512], ACT.Silu))
                act.wait_ge(conv_raw, 1)
                for c in range(4):
                    ins = act.activation(convout[:, c, :], convout[:, c, :], ACT.Silu, bias=colp[:, 19 + c:20 + c])
                ins.then_inc(conv_ready, 1)
                for t in range(NT):
                    unit(10 + t, lambda: copy(aqk[:, t].rearrange("p h s e -> p (h s e)"), ps[t]))
                for t in range(NT):
                    b = ps[t]
                    unit(12 + t, lambda: copy(av[:, t, :], b[:, 0:256]),
                         lambda: act.activation(sz[:, t, :], b[:, 256:512], ACT.Silu))
                act.wait_ge(qkt_done, 1)
                for c in range(2):
                    ins = copy(aqkT[:, 2 * c:2 * c + 2, :], ps[4 + c].rearrange("p (m t) -> p m t", m=2))
                ins.then_inc(qkt_read, 1)
                act.wait_ge(cols_ready, 2)

                def decay(n, c0, bias):
                    act.wait_ge(arg_ready, n + 1)
                    e = E[n % 2]
                    act.activation(e[:, 0:T], e[:, 0:T], ACT.Exp, bias=bias(0))
                    act.activation(e[:, T:SCORE], e[:, T:SCORE], ACT.Exp, bias=bias(1)).then_inc(exp_ready, 1)

                for h in range(H):
                    decay(h, 0, lambda t: RC[:, t, h:h + 1])
                for h in range(H):
                    decay(H + h, 0, lambda t: nac[:, t, h:h + 1])
                for h in range(H):
                    act.wait_ge(at_arg, h + 1)
                    e = E[h % 2]
                    act.activation(e[:, 0:P], e[:, 0:P], ACT.Exp, scale=-1.0, bias=rm[:, h % 2, 0:1])
                    act.activation(e[:, P:SCORE], e[:, P:SCORE], ACT.Exp, scale=-1.0,
                                   bias=rm[:, h % 2, 1:2]).then_inc(at_exp, 1)
                    act.wait_ge(at_tr, h + 1)
                    if h >= 2:
                        act.wait_ge(at_used, h - 1)
                    copy(PTa[h % 2], ps[2 + h % 2][:, 0:SCORE]).then_inc(at_trc, 1)
                act.wait_ge(gla_arg, 1)
                act.activation(ge[:, 0, :], gd1, ACT.Exp)
                act.activation(ge[:, 1, :], gd1, ACT.Exp, scale=-1.0)
                act.activation(ge[:, 2, :], gd2, ACT.Exp)
                for j in range(1, NB):
                    k0 = BLK * (j * (j - 1) // 2)
                    ins = act.activation(kx[:, k0:k0 + BLK * j], gb[:, 0:BLK * j], ACT.Exp, scale=-1.0,
                                         bias=gb[:, BLK * j - 1:BLK * j])
                ins.then_inc(gla_exp, 1)
                act.wait_ge(rms_in, 1)
                for r in (st1, st2, st3):
                    ins = act.activation(r, r, ACT.Sqrt)
                ins.then_inc(rms_out, 1)
                for u in range(0, 4, 2):
                    act.wait_ge(yt_done, u + 1)
                    if u:
                        act.wait_ge(yt_read, u)
                    copy(XT3[:, 2 * u:2 * u + 2, :], ps[2].rearrange("p (k t) -> p k t", k=2)).then_inc(yt_read, 1)
                act.wait_ge(rms_in, 2)
                act.activation(rstd, rstd, ACT.Sqrt).then_inc(rms_out, 1)
                for u in range(0, 4, 2):
                    act.wait_ge(xt_done, 4 + u + 1)
                    act.wait_ge(xt_read, 4 + u)
                    copy(XT3[:, 2 * u:2 * u + 2, :], ps[0].rearrange("p (k t) -> p k t", k=2)).then_inc(xt_read, 1)
                act.wait_ge(rt_done, 1)
                act.activation(SC, ps[2][:, 0:NT * EXPERTS].rearrange("p (t e) -> p t e", t=NT),
                               ACT.Sigmoid).then_inc(score_sig, 1)
                for t in range(NT):
                    act.wait_ge(sh_done, t + 1)
                    act.activation(shh[:, t, :], ps[4 + t][:, 0:F], ACT.Silu).then_inc(sh_silu, 1)
                act.wait_ge(sht_done, 1)
                copy(shT, ps[7].rearrange("p (k t) -> p k t", k=2)).then_inc(sht_read, 1)
                act.wait_ge(rounds_ready, 1)
                last = act.value_load(last_pair2[0:1, 0:1], min_val=PAIRS // 2 - 1, max_val=ROUNDS * PAIRS // 2 - 1)
                pairs2 = last + 1

                def gathered_half(g):
                    act.wait_ge(gathered, 2 * g + 1)
                    copy(XG[:, 0:4, :], ps[1].rearrange("p (k s) -> p k s", k=4)).then_inc(xg_act, 1)

                act.sem_inc(ht_done, 1)
                gathered_half(0)
                with act.Fori(0, pairs2) as j:
                    for b in range(2):
                        g = 2 * j + b
                        act.wait_ge(gu_done, g + 1)
                        act.wait_ge(h_done, g + 1)
                        act.activation(HS, ps[0][:, 0:F], ACT.Silu).then_inc(silu_done, 1)
                        gathered_half(g + 1)
                        act.wait_ge(ht_tr, g + 2)
                        act.wait_ge(dn_done, 2 * g + 2)
                        copy(HT, ps[7][:, 0:T].rearrange("p (k s) -> p k s", k=2)).then_inc(ht_done, 1)
                        act.wait_ge(dn_done, 2 * g + 3)
                        act.wait_ge(sc_done, 4 * g + 4)
                        copy(YS[:, 0:512], ps[3]).then_inc(ys_act, 1)
                act.wait_ge(rms_in, 3)
                act.activation(rstd, rstd, ACT.Sqrt).then_inc(rms_out, 1)
                act.sem_inc(layer_done, 1)
                act.wait_ge(layer_open, l + 1)

        @block.vector
        def _(dve):
            own = [0]

            def link(ins):
                own[0] += 1
                ins.then_inc(dve_own, 1)
                dve.wait_ge(dve_own, own[0])

            def tt(o, a, b, op):
                return dve.tensor_tensor(o, a, b, op)

            def mul(o, a, b):
                return tt(o, a, b, ALU.mult)

            def add(o, a, b):
                return tt(o, a, b, ALU.add)

            def heads(ap):
                return ap.rearrange("p t (h d) -> p t h d", h=H)

            def over(ap, n):
                return ap.unsqueeze(3).broadcast_to([P, ap.shape[1], ap.shape[2], n])

            def layer_norm(src, g, b, n_rms, done):
                for t in range(NT):
                    for n in range(2):
                        link(dve.bn_stats(bst[:, t, n, :], src[:, t, n * 512:(n + 1) * 512]))
                    link(dve.bn_aggr(bag[:, t, :], bst[:, t, :, :].rearrange("p n s -> p (n s)")))
                link(dve.tensor_scalar(rstd.unsqueeze(2), bag[:, :, 1:2], EPS, None, ALU.add))
                dve.sem_inc(rms_in, 1)
                dve.wait_ge(rms_out, n_rms)
                link(dve.reciprocal(rstd, rstd))
                for t in range(NT):
                    link(dve.tensor_scalar(src[:, t, :], src[:, t, :], bag[:, t, 0:1], rstd[:, t:t + 1],
                                           ALU.subtract, ALU.mult))
                    link(mul(src[:, t, :], src[:, t, :], rowp[:, ROW[g]]))
                    link(add(Xv[:, t, :], src[:, t, :], rowp[:, ROW[b]]))

            dve.wait_ge(cst_loaded, 32)
            with dve.Fori(0, layers) as l:
                own[0] = 0
                link(dve.memset(mvx[:, :, :, DH:DH + 1], 1.0))
                link(dve.memset(convin[:, :, 0:3], 0.0))
                link(dve.memset(R, 0.0))
                for u in range(1, 4, 2):
                    dve.wait_ge(xt_done, u + 1)
                    dve.wait_ge(xt_read, u)
                    dve.tensor_copy(XT3[:, 2 * u:2 * u + 2, :],
                                    ps[1].rearrange("p (k t) -> p k t", k=2)).then_inc(xt_read, 1)
                dve.wait_ge(small_loaded, 32)
                dve.wait_ge(logs_ready, 1)
                fr, dr = slice(32, 32 + H), slice(64, 64 + H)
                link(dve.scalar_tensor_tensor(lsg[fr], z[fr], 0.0, lt[fr], ALU.min, ALU.subtract))
                link(dve.scalar_tensor_tensor(lsp[dr], z[dr], 0.0, lt[dr], ALU.max, ALU.add))
                link(dve.tensor_copy(R[96:96 + H], lsp[dr]))
                link(dve.tensor_scalar(lsp[dr], lsp[dr], acol[dr], -1.0, ALU.mult, ALU.mult))
                link(dve.tensor_tensor_scan(R[dr], ones[dr], lsp[dr], 0.0, ALU.mult, ALU.add))
                link(dve.tensor_tensor_scan(lsg[fr], ones[fr], lsg[fr], 0.0, ALU.mult, ALU.add))
                link(dve.tensor_copy(C0[0:H], lsg[fr]))
                link(tt(R[0:H], z[0:H], C0[0:H], ALU.subtract))
                link(dve.tensor_tensor_scan(MR[0:H], R[0:H], R[0:H], -3.0e38, ALU.max, ALU.max))
                link(add(C0[0:H], C0[0:H], MR[0:H]))
                link(dve.tensor_copy(R[fr], C0[0:H]))
                dve.sem_inc(rows_ready, 1)
                dve.wait_ge(gla_logs, 1)
                link(dve.scalar_tensor_tensor(gl, gdec, 0.0, gl, ALU.min, ALU.subtract))
                link(dve.tensor_scalar(gl, gl, 1.0 / TAU, None, ALU.mult))
                link(dve.tensor_tensor_scan(gb, ones, gl, 0.0, ALU.mult, ALU.add))
                b3 = gb.rearrange("p (j i) -> p j i", i=BLK)
                link(tt(gd1.rearrange("p (j i) -> p j i", i=BLK), b3,
                        b3[:, :, BLK // 2 - 1:BLK // 2].broadcast_to([P, NB, BLK]), ALU.subtract))
                link(dve.tensor_scalar(gd1, gd1, CLAMP, -CLAMP, ALU.min, ALU.max))
                link(dve.tensor_copy(gd2[:, 0:BLK], gb[:, 0:BLK]))
                link(tt(gd2[:, BLK:T].rearrange("p (j i) -> p j i", i=BLK), b3[:, 1:NB, :],
                        b3[:, 0:NB - 1, BLK - 1:BLK].broadcast_to([P, NB - 1, BLK]), ALU.subtract))
                dve.wait_ge(cols_done, 1)
                dve.wait_ge(cols_ready, 1)
                link(dve.tensor_copy(RC, ps[3][:, 0:T].rearrange("p (t c) -> p t c", c=P)))
                link(dve.tensor_scalar(nac, RC[:, :, 64:64 + H], -1.0, None, ALU.mult))
                dve.sem_inc(cols_ready, 1)
                dve.wait_ge(proj_read, 5)
                for c in range(4):
                    for i in range(4):
                        w = colp[:, 3 + 4 * c + i:4 + 4 * c + i]
                        if i == 0:
                            link(dve.tensor_scalar(convout[:, c, :], convin[:, c, 0:T], w, None, ALU.mult))
                        else:
                            link(dve.scalar_tensor_tensor(convout[:, c, :], convin[:, c, i:i + T], w,
                                                          convout[:, c, :], ALU.mult, ALU.add))
                dve.sem_inc(conv_raw, 1)
                dve.wait_ge(proj_read, 12)
                for t in range(NT):
                    cos = cst[:, CST["cos"]][:, 32 * t:32 * t + 32].unsqueeze(1).broadcast_to([P, 8, 32])
                    sin = cst[:, CST["sin"]][:, 32 * t:32 * t + 32].unsqueeze(1).broadcast_to([P, 8, 32])
                    x1, x2 = aqk[:, t, :, 0, :], aqk[:, t, :, 1, :]
                    link(mul(rot[:, t, :, 0, :], x1, cos))
                    link(mul(rtmp[:, t], x2, sin))
                    link(tt(rot[:, t, :, 0, :], rot[:, t, :, 0, :], rtmp[:, t], ALU.subtract))
                    link(mul(rot[:, t, :, 1, :], x2, cos))
                    link(mul(rtmp[:, t], x1, sin))
                    link(add(rot[:, t, :, 1, :], rot[:, t, :, 1, :], rtmp[:, t]))
                dve.sem_inc(rope_ready, 1)
                dve.wait_ge(sxt_done, 1)
                link(dve.tensor_copy(sx, ps[3].rearrange("p (t c) -> p t c", t=NT)))
                link(mul(heads(xdt), heads(sx), over(RC[:, :, 96:96 + H], DH)))
                dve.sem_inc(sx_ready, 1)

                def decay_arg(n, sign):
                    dve.wait_ge(bc_done, n + 1)
                    bc = ps[2 + n % 2]
                    e = E[n % 2]
                    cm = C("causal")
                    link(tt(e[:, 0:T], cm[:, 0:T], bc[:, 0:T], sign))
                    link(tt(e[:, T:SCORE], cm[:, T:SCORE], bc[:, P:T], sign))
                    dve.sem_inc(bc_read, 1)
                    dve.sem_inc(arg_ready, 1)

                def ml_prob(h):
                    dve.wait_ge(exp_ready, h + 1)
                    dve.wait_ge(score_done, h + 1)
                    if h >= 2:
                        dve.wait_ge(prob_used, h - 1)
                    link(dve.scalar_tensor_tensor(Pm[h % 2], ps[h % 2][:, 0:SCORE], DH ** -0.5, E[h % 2],
                                                  ALU.mult, ALU.mult))
                    dve.sem_inc(score_read, 1)
                    dve.sem_inc(prob_ready, 1)

                def ssm_prob(h):
                    dve.wait_ge(exp_ready, H + h + 1)
                    dve.wait_ge(score_done, H + 1)
                    dve.wait_ge(prob_used, H + h - 1)
                    link(mul(Pm[h % 2], ps[6 + h // 2][:, 0:SCORE], E[h % 2]))
                    dve.sem_inc(prob_ready, 1)

                for h in range(H):
                    decay_arg(h, ALU.subtract)
                    if h >= 1:
                        ml_prob(h - 1)
                ml_prob(H - 1)
                decay_arg(H, ALU.add)
                decay_arg(H + 1, ALU.add)
                dve.wait_ge(prob_used, H)
                for t in range(NT):
                    o = ps[4 + t][:, 0:H * (DH + 1)].rearrange("p (h d) -> p h d", h=H)
                    den = rden[:, t, :].unsqueeze(2)
                    link(dve.tensor_scalar(den, o[:, :, DH:DH + 1], -1.0, None, ALU.mult))
                    link(tt(den, den, o[:, :, DH:DH + 1], ALU.max))
                    link(tt(rden[:, t, :], rden[:, t, :], enm[:, t, :], ALU.max))
                    link(dve.reciprocal(rden[:, t, :], rden[:, t, :]))
                    link(mul(ACCv[:, t, 0:256].rearrange("p (h d) -> p h d", h=H), o[:, :, 0:DH],
                             den.broadcast_to([P, H, DH])))
                dve.sem_inc(o_read, 1)
                for h in range(H):
                    ssm_prob(h)
                    if h + 2 < H:
                        decay_arg(H + h + 2, ALU.add)

                def mean_square(o, src, sq, scale):
                    link(mul(sq, src, src))
                    link(dve.tensor_reduce(o.unsqueeze(3), heads(sq), AX, ALU.add))
                    link(dve.tensor_scalar(o, o, scale, EPS, ALU.mult, ALU.add))

                yml, ysm, yat, ygl = (ACCv[:, :, 256 * i:256 * (i + 1)] for i in range(4))
                link(dve.tensor_reduce(st2.unsqueeze(3), heads(yml), AX, ALU.add))
                link(dve.tensor_scalar(st2, st2, 1.0 / DH, None, ALU.mult))
                link(tt(heads(yml), heads(yml), over(st2, DH), ALU.subtract))
                mean_square(st1, yml, tmp[:, :, 0:256], 1.0 / DH)
                dve.wait_ge(prob_used, 2 * H)
                link(mul(heads(sx), heads(sx), rowp[:, ROW["ssm_d"]].unsqueeze(1).unsqueeze(3)
                         .broadcast_to([P, NT, H, DH])))
                link(add(ysm, sx, ps[5].rearrange("p (t c) -> p t c", t=NT)))
                link(mul(ysm, ysm, sz))
                dve.sem_inc(o_read, 1)
                link(mul(tmp[:, :, 0:256], ysm, ysm))
                link(dve.memset(st3, 1.0))
                link(dve.tensor_reduce(st3[:, :, 0:1], tmp[:, :, 0:256], AX, ALU.add))
                link(dve.tensor_scalar(st3, st3, 1.0 / 256, EPS, ALU.mult, ALU.add))

                def at_prob_of(h):
                    am = C("att_add")
                    dve.wait_ge(score_done, H + 1 + h + 1)
                    e, r = E[h % 2], rm[:, h % 2, :]
                    link(dve.tensor_tensor_reduce(e[:, 0:P], ps[h % 2][:, 0:P], am[:, 0:P], -(DH ** -0.5), 3.0e38,
                                                  ALU.add, ALU.min, r[:, 0:1]))
                    link(dve.tensor_tensor_reduce(e[:, P:SCORE], ps[h % 2][:, P:SCORE], am[:, P:SCORE],
                                                  -(DH ** -0.5), 3.0e38, ALU.add, ALU.min, r[:, 1:2]))
                    dve.sem_inc(score_read, 1)
                    dve.sem_inc(at_arg, 1)

                def at_weights(h):
                    dve.wait_ge(at_exp, h + 1)
                    if h >= 2:
                        dve.wait_ge(at_tr, h - 1)
                    p, e, mm = Pm[h % 2], E[h % 2], C("att_mul")
                    for t, s in ((0, slice(0, P)), (1, slice(P, SCORE))):
                        link(dve.tensor_tensor_reduce(p[:, s], e[:, s], mm[:, s], 1.0, 0.0, ALU.mult, ALU.add,
                                                      rden[:, t, h:h + 1]))
                    dve.sem_inc(at_prob, 1)

                for h in range(H):
                    at_prob_of(h)
                    if h >= 1:
                        at_weights(h - 1)
                at_weights(H - 1)
                dve.wait_ge(at_used, H)
                link(dve.reciprocal(rden, rden))
                link(mul(heads(yat), ps[4].rearrange("p (t h d) -> p t h d", t=NT, h=H), over(rden, DH)))
                dve.sem_inc(o_read, 1)
                dve.sem_inc(gla_arg, 1)
                dve.wait_ge(gla_exp, 1)
                q, k = gqkT[:, 0, :], gqkT[:, 1, :]
                link(dve.memset(PT, 0.0))
                link(dve.scalar_tensor_tensor(ge[:, 0, :], q, DK ** -0.5, ge[:, 0, :], ALU.mult, ALU.mult))
                link(mul(ge[:, 1, :], k, ge[:, 1, :]))
                link(dve.scalar_tensor_tensor(ge[:, 2, :], q, DK ** -0.5, ge[:, 2, :], ALU.mult, ALU.mult))
                for j in range(1, NB):
                    k0 = BLK * (j * (j - 1) // 2)
                    link(mul(kx[:, k0:k0 + BLK * j], k[:, 0:BLK * j], kx[:, k0:k0 + BLK * j]))
                dve.sem_inc(gla_qk, 1)
                dve.wait_ge(gla_sc, 1)
                for j in range(NB):
                    jj, t = j % 4, j // 4
                    col = BLK * j if t == 0 else 2 * P + BLK * jj
                    r = slice(BLK * jj, BLK * (jj + 1))
                    link(mul(PT[r, :, col:col + BLK], psA[r, :, col:col + BLK],
                             cst[r, CST["tri"]].unsqueeze(1).broadcast_to([BLK, H, BLK])))
                    if jj > 0:
                        link(dve.tensor_copy(PT[0:BLK * jj, :, col:col + BLK], psA[0:BLK * jj, :, col:col + BLK]))
                link(dve.tensor_copy(PT[:, :, P:2 * P], psA[:, :, P:2 * P]))
                dve.sem_inc(gla_pt, 1)
                dve.wait_ge(o_done, 1)
                link(dve.tensor_copy(ygl, ps[0].rearrange("p (t c) -> p t c", t=NT)))
                mean_square(st2, ygl, tmp[:, :, 0:256], 1.0 / DH)
                dve.sem_inc(rms_in, 1)
                dve.wait_ge(rms_out, 1)
                for s in (st1, st2, st3):
                    link(dve.reciprocal(s, s))
                link(mul(heads(yml), heads(yml), over(st1, DH)))
                link(mul(heads(ygl), heads(ygl), over(st2, DH)))

                def row(name):
                    return rowp[:, ROW[name]].unsqueeze(1).broadcast_to([P, NT, 256])

                link(mul(yml, yml, row("ml_norm")))
                link(mul(yml, yml, mo))
                link(mul(ygl, ygl, row("gla_norm")))
                link(mul(ygl, ygl, gr))
                link(mul(ysm, ysm, st3[:, :, 0:1].broadcast_to([P, NT, 256])))
                link(mul(ysm, ysm, row("ssm_norm")))
                dve.sem_inc(stage_free, 1)
                dve.sem_inc(mixers_done, 1)
                dve.sem_inc(y_ready, 1)
                for u in range(1, 4, 2):
                    dve.wait_ge(yt_done, u + 1)
                    dve.wait_ge(yt_read, u)
                    dve.tensor_copy(XT3[:, 2 * u:2 * u + 2, :],
                                    ps[3].rearrange("p (k t) -> p k t", k=2)).then_inc(yt_read, 1)
                for t in range(NT):
                    for n in range(2):
                        dve.wait_ge(op_done, 2 * t + n + 1)
                        xs = Xv[:, t, n * 512:(n + 1) * 512]
                        link(dve.scalar_tensor_tensor(xs, xs, ALPHA, ps[4 + 2 * t + n], ALU.mult, ALU.add))
                layer_norm(Xv, "ln1_g", "ln1_b", 2, None)
                dve.sem_inc(x1_ready, 1)
                for u in range(1, 4, 2):
                    dve.wait_ge(xt_done, 4 + u + 1)
                    dve.wait_ge(xt_read, 4 + u)
                    dve.tensor_copy(XT3[:, 2 * u:2 * u + 2, :],
                                    ps[1].rearrange("p (k t) -> p k t", k=2)).then_inc(xt_read, 1)
                dve.wait_ge(score_sig, 1)
                rb = rowp[:, ROW["router_bias"]].unsqueeze(1).broadcast_to([P, NT, EXPERTS])
                link(add(selm, SC, rb))
                for t in range(NT):
                    for g in range(GROUPS):
                        ins = dve.max(m8[:, t, g, :], selm[:, t, 8 * g:8 * g + 8])
                link(ins)
                link(add(grp.unsqueeze(3), m8[:, :, :, 0:1], m8[:, :, :, 1:2]))
                theirs = grp.unsqueeze(2).broadcast_to([P, NT, GROUPS, GROUPS])
                mine = grp.unsqueeze(3).broadcast_to([P, NT, GROUPS, GROUPS])
                link(tt(cmp1, theirs, mine, ALU.is_gt))
                link(tt(cmp2, theirs, mine, ALU.is_equal))
                earlier = C("earlier").rearrange("p (a b) -> p a b", a=GROUPS).unsqueeze(1)\
                    .broadcast_to([P, NT, GROUPS, GROUPS])
                link(mul(cmp2, cmp2, earlier))
                link(add(cmp1, cmp1, cmp2))
                link(dve.tensor_reduce(gmask.unsqueeze(3), cmp1, AX, ALU.add))
                link(dve.tensor_scalar(gmask, gmask, float(GROUPS // 2), None, ALU.is_lt))
                gm = over(gmask, 8)
                s4 = selm.rearrange("p t (g e) -> p t g e", g=GROUPS)
                link(mul(s4, s4, gm))
                link(dve.tensor_scalar(gmask, gmask, -1.0, 1.0e30, ALU.add, ALU.mult))
                link(add(s4, s4, gm))
                for t in range(NT):
                    link(dve.max(t8[:, t, :], selm[:, t, :]))
                    link(dve.match_replace(selr[:, t, :], t8[:, t, :], selm[:, t, :], -3.0e38))
                link(dve.tensor_scalar(Mk, selr, -2.0e38, None, ALU.is_lt))
                dve.sem_inc(mask_ready, 1)
                link(mul(G, SC, Mk))
                link(dve.tensor_reduce(gs.unsqueeze(2), G, AX, ALU.add))
                link(dve.reciprocal(gs, gs))
                link(dve.tensor_scalar(gs, gs, 2.5, None, ALU.mult))
                link(mul(G, G, gs.unsqueeze(2).broadcast_to([P, NT, EXPERTS])))
                dve.wait_ge(rank_done, 1)
                rk = ps[3][:, 0:NT * EXPERTS].rearrange("p (t e) -> p t e", t=NT)
                link(dve.scalar_tensor_tensor(rank, rk, 1.0, Mk, ALU.add, ALU.mult))
                link(dve.tensor_scalar(rank, rank, -1.0, None, ALU.add))
                link(dve.tensor_reduce(cnt[:, 0:1], ps[3][:, 2 * EXPERTS:3 * EXPERTS], AX, ALU.max))
                link(dve.memset(cnt[:, 1:2], 1.0))
                for r in range(1, ROUNDS):
                    link(dve.scalar_tensor_tensor(cnt[:, 1:2], cnt[:, 0:1], float(CAP * r), cnt[:, 1:2],
                                                  ALU.is_gt, ALU.add))
                link(dve.tensor_scalar(last_pair2[:, :], cnt[:, 1:2], float(PAIRS // 2), -1.0, ALU.mult, ALU.add))
                dve.sem_inc(rounds_ready, 1)
                for t in range(NT):
                    dve.wait_ge(sh_silu, t + 1)
                    mul(shh[:, t, :], shh[:, t, :], ps[4 + t][:, F:2 * F]).then_inc(sh_hid, 1)
                for t in range(NT):
                    for n in range(2):
                        dve.wait_ge(sho_done, 2 * t + n + 1)
                        s = slice(n * 512, (n + 1) * 512)
                        dve.scalar_tensor_tensor(ACCv[:, t, s], Xv[:, t, s], ALPHA, ps[4 + 2 * t + n],
                                                 ALU.mult, ALU.add).then_inc(acc_done, 1)

                slot = C("slot").unsqueeze(1).unsqueeze(1).broadcast_to([P, NT, 2, CAP])

                def selection(g, b):
                    e0 = (g % PAIRS) * 2
                    mine = rank[:, :, bass.ds(e0, 2)]
                    tt(Sel[b], slot, over(mine, CAP), ALU.is_equal).then_inc(sel_ready, 1)
                    dve.wait_ge(sel_ready, g + 1)
                    mul(SelG[b], Sel[b], over(G[:, :, bass.ds(e0, 2)], CAP)).then_inc(selg_ready, 1)
                    dve.tensor_scalar(mine, mine, -float(CAP), None, ALU.add).then_inc(rank_next, 1)
                    dve.wait_ge(rank_next, g + 1)

                def gathered_half(g):
                    dve.wait_ge(gathered, 2 * g + 2)
                    dve.tensor_copy(XG[:, 4:8, :], ps[2].rearrange("p (k s) -> p k s", k=4)).then_inc(xg_dve, 1)

                def add_rows(g):
                    for t in range(NT):
                        for n in range(2):
                            q = 2 * t + n
                            dve.wait_ge(sc_done, 4 * g + q + 1)
                            dve.wait_ge(acc_done, 4 * g + q + ACC0 - 3)
                            a = ACCv[:, t, n * 512:(n + 1) * 512]
                            add(a, a, ps[5 + q % 2]).then_inc(acc_done, 1)

                last = dve.value_load(last_pair2[0:1, 0:1], min_val=PAIRS // 2 - 1, max_val=ROUNDS * PAIRS // 2 - 1)
                pairs2 = last + 1
                dve.sem_inc(h_done, 1)
                dve.wait_ge(sh_hid, 2)
                dve.wait_ge(sht_done, 1)
                dve.memset(SelT, 0.0).then_inc(st_done, 1)
                dve.memset(YS[:, 0:512], 0.0).then_inc(ys_act, 1)
                dve.memset(YS[:, 512:D], 0.0).then_inc(ys_dve, 1)
                selection(0, 0)
                selection(1, 1)
                gathered_half(0)
                with dve.Fori(0, pairs2) as j:
                    for b in range(2):
                        g = 2 * j + b
                        dve.wait_ge(silu_done, g + 1)
                        dve.wait_ge(ht_tr, g + 1)
                        mul(Hh, HS, ps[0][:, F:2 * F]).then_inc(h_done, 1)
                        gathered_half(g + 1)
                        add_rows(g)
                        dve.wait_ge(st_tr, g + 1)
                        dve.tensor_copy(SelT, ps[7][:, T:2 * T]).then_inc(st_done, 1)
                        selection(g + 2, b)
                        dve.wait_ge(dn_done, 2 * g + 4)
                        dve.tensor_copy(YS[:, 512:D], ps[4]).then_inc(ys_dve, 1)
                add_rows(2 * pairs2)
                dve.wait_ge(acc_done, 8 * pairs2 + 4 + ACC0)
                layer_norm(ACCv, "ln2_g", "ln2_b", 3, None)
                dve.sem_inc(layer_done, 1)
                dve.wait_ge(layer_open, l + 1)


IN_AT = {"mlstm_qk": (0,), "conv": (1288,), "gla_qk": (2572,), "mlstm_vo": (512,), "gla_vr": (2828,),
         "att_qk": (1804,)}


def constants():
    import numpy as np
    c = np.zeros((P, CSTS), np.float32)
    i = np.arange(P)
    c[:, CST["ident"]] = np.eye(P)
    c[:, CST["before"]] = i[:, None] < i[None, :]
    c[:, CST["ones"]] = 1.0
    causal = np.where(i[:, None] <= i[None, :], 0.0, -1.0e30)
    c[:, CST["causal"]] = np.concatenate([causal, np.zeros((P, P)), causal], 1)
    t, s = np.arange(T)[:, None], np.arange(T)[None, :]
    n = ((t >= s) & (t - s <= 128)).astype(np.float32)
    for window, dilation in ((512, 4), (2048, 16)):
        n += (t >= s) & ((t - s) % dilation == 0) & ((t - s) // dilation <= window // dilation)
    n = np.concatenate([n[:P, :P], n[P:, :]], 1)
    c[:, CST["att_mul"]] = n
    c[:, CST["att_add"]] = np.where(n > 0, 0.0, -1.0e30)
    inv = np.float32(10000.0) ** (-np.arange(32, dtype=np.float32) / np.float32(32))
    ang = np.arange(T, dtype=np.float32)[:, None] * inv.astype(np.float32)
    for name, f in (("cos", np.cos), ("sin", np.sin)):
        c[:, CST[name]] = f(ang).astype(np.float32).reshape(NT, P, 32).transpose(1, 0, 2).reshape(P, -1)
    c[:, CST["slot"]] = np.arange(CAP)
    for r in (0, 64):
        for h in range(H):
            c[r + h, CST["head"].start + h * P:CST["head"].start + (h + 1) * P] = 1.0
    c[:, CST["tri"]] = (i % BLK)[:, None] <= np.arange(BLK)[None, :]
    g = np.arange(GROUPS)
    c[:, CST["earlier"]] = (g[None, :] < g[:, None]).reshape(1, -1)
    return c


def layout(w):
    import numpy as np
    w = {k: np.asarray(v) for k, v in w.items()}
    win = w["w_in"].reshape(DEPTH, P, KD, -1)
    small = np.zeros((DEPTH, P, KD, P), np.float32)
    small[..., 0:H] = win[..., 1024:1028]
    small[..., 32:32 + H] = win[..., 1028:1032]
    small[..., 64:64 + H] = win[..., 1800:1804]
    small[..., 96:112] = win[..., 3340:3356]
    parts = [small]
    for name, n, _ in GROUPS_IN[1:]:
        if name == "att_v_ssm_z":
            parts.append(np.concatenate([win[..., 2316:2572], win[..., 1032:1288]], -1))
        else:
            parts.append(win[..., IN_AT[name][0]:IN_AT[name][0] + n])
    w_in = np.concatenate([p.reshape(DEPTH, P, -1) for p in parts], -1)
    rows = np.concatenate([w["ln1_g"], w["ln1_b"], w["ln2_g"], w["ln2_b"], w["ml_norm_w"], w["ssm_norm_w"],
                           w["gla_norm_w"], w["ssm_d"], w["router_bias"]], -1)
    cols = np.zeros((DEPTH, P, COLS), np.float32)
    cols[:, 0:H, 0] = w["ml_i_bias"]
    cols[:, 32:32 + H, 0] = w["ml_f_bias"]
    cols[:, 64:64 + H, 0] = w["ssm_dt_bias"]
    cols[:, 64:64 + H, 1] = w["ssm_a_log"]
    cols[:, :, 2] = w["gla_gate_b"]
    cols[:, :, COL["taps"]] = w["ssm_conv_w"].reshape(DEPTH, 4, 4, P).transpose(0, 3, 2, 1).reshape(DEPTH, P, 16)
    cols[:, :, COL["conv_b"]] = w["ssm_conv_b"].reshape(DEPTH, 4, P).transpose(0, 2, 1)
    cols[:, 96:112, COL["gate_w2"]] = w["gla_gate_w2"]
    return {"x": w["x"][0], "w_in": w_in, "cols": cols, "rows": rows, "cst": constants(), "w_out": w["w_out"],
            "router_w": w["router_w"], "exp_w_gate": w["exp_w_gate"], "exp_w_up": w["exp_w_up"],
            "exp_w_down": w["exp_w_down"], "sh_w_gate": w["sh_w_gate"], "sh_w_up": w["sh_w_up"],
            "sh_w_down": w["sh_w_down"]}


def build(nc, arrays, **more):
    import numpy as np
    a = {}
    for name, v in arrays.items():
        a[name] = nc.dram_tensor(f"in_{name}", v.shape, mybir.dt.from_np(v.dtype), kind="ExternalInput").ap()
    out = nc.dram_tensor("out_0", (T, D), F32, kind="ExternalOutput").ap()
    hybrid_kernel(nc, a["x"], a["w_in"], a["cols"], a["rows"], a["cst"], a["w_out"], a["router_w"],
                  a["exp_w_gate"].rearrange("l (g e) (p k) f -> l g p e k f", e=2, k=KD),
                  a["exp_w_up"].rearrange("l (g e) (p k) f -> l g p e k f", e=2, k=KD),
                  a["exp_w_down"].rearrange("l (g e) (p k) d -> l g p e k d", e=2, k=2),
                  a["sh_w_gate"], a["sh_w_up"], a["sh_w_down"], out, **more)


def kernel(**inputs):
    import numpy as np
    from concourse import bacc
    from concourse.bass_utils import run_bass_kernel_spmd

    arrays = {k: np.ascontiguousarray(v) for k, v in layout(inputs).items()}
    nc = bacc.Bacc("TRN2", target_bir_lowering=False, num_devices=1)
    build(nc, arrays)
    r = run_bass_kernel_spmd(nc, [{f"in_{k}": v for k, v in arrays.items()}], core_ids=[0])
    return r.results[0]["out_0"].reshape(1, T, D)
```

```python
from contextlib import ExitStack

import concourse.bass as bass
from concourse import mybir

F32 = mybir.dt.float32
I32 = mybir.dt.int32
BF16 = mybir.dt.bfloat16
ALU = mybir.AluOpType
ACT = mybir.ActivationFunctionType
AX = mybir.AxisListType.X

P = 128
T = 256
NT = T // P
D = 1024
KD = D // P
DEPTH = 2
H = 4
DH = 64
DK = 32
EXPERTS = 64
PAIRS = EXPERTS // 2
TOP_K = 8
GROUPS = 8
F = 256
CAP = 64
ROUNDS = T // CAP
ALPHA = (2 * DEPTH) ** 0.25
EPS = 1e-5
TAU = 16.0
BLK = 32
NB = T // BLK
SCORE = 3 * P
CLAMP = 80.0

GROUPS_IN = [
    ("small", P, True), ("mlstm_qk", 512, True), ("gla_qk", 256, True), ("att_qk", 512, False),
    ("conv", 512, True), ("gla_vr", 512, False), ("mlstm_vo", 512, False), ("att_v_ssm_z", 512, False),
]
UNITS = [max(g[1] // 256, 1) for g in GROUPS_IN]
FIRST = {g[0]: sum(UNITS[:i]) for i, g in enumerate(GROUPS_IN)}
YORDER = (0, 3, 2, 1)

ROW = {}
_at = 0
for _name, _n in (("ln1_g", D), ("ln1_b", D), ("ln2_g", D), ("ln2_b", D), ("ml_norm", 256), ("ssm_norm", 256),
                  ("gla_norm", 256), ("ssm_d", H), ("router_bias", EXPERTS)):
    ROW[_name] = slice(_at, _at + _n)
    _at += _n
ROWS = _at
COL = {"bias": slice(0, 1), "a_log": slice(1, 2), "gla_b": slice(2, 3), "taps": slice(3, 19),
       "conv_b": slice(19, 23), "gate_w2": slice(23, 151)}
COLS = 151
CST = {}
_at = 0
for _name, _n in (("ident", P), ("before", P), ("ones", T), ("causal", SCORE), ("att_add", SCORE),
                  ("att_mul", SCORE), ("cos", NT * 32), ("sin", NT * 32), ("slot", CAP), ("head", H * P),
                  ("tri", BLK), ("earlier", GROUPS * GROUPS)):
    CST[_name] = slice(_at, _at + _n)
    _at += _n
CSTS = _at


def hybrid_kernel(nc, x_in, w_in, cols_in, rows_in, cst_in, w_out, router_w, e_gate, e_up, e_down,
                  sh_gate, sh_up, sh_down, out, debug=None, layers=DEPTH):
    with ExitStack() as ctx:
        def sb(name, n, dt=F32):
            return ctx.enter_context(nc.sbuf_tensor(name, [P, n], dt))

        def sem(name):
            return ctx.enter_context(nc.semaphore(name))

        wbuf = sb("wbuf", 24576)
        stage = sb("stage", 8192)
        X = sb("X", NT * D)
        XT = sb("XT", KD * T)
        ACC = sb("ACC", NT * D)
        rowp = sb("rowp", ROWS)
        colp = sb("colp", COLS)
        cst = sb("cst", CSTS)
        misc = sb("misc", 5632)
        last_pair2 = sb("last_pair2", 1, I32)

        def view(t, at, *dims):
            n = 1
            for d in dims:
                n *= d
            ap = t[:, at:at + n]
            if len(dims) == 1:
                return ap
            names = "abcd"[:len(dims)]
            return ap.rearrange("p (" + " ".join(names) + ") -> p " + " ".join(names),
                                **{c: d for c, d in zip(names, dims)})

        Xv = view(X, 0, NT, D)
        XT3 = view(XT, 0, KD, T)
        ACCv = view(ACC, 0, NT, D)
        wgu = [view(wbuf, 8192 * b, 2, 2, KD, F) for b in range(2)]
        wdn = [view(wbuf, 16384 + 4096 * b, 2, 2, D) for b in range(2)]

        pos = [8192]

        def scr(*dims):
            n = 1
            for d in dims:
                n *= d
            at = pos[0]
            pos[0] += n
            assert pos[0] <= 24576
            return view(wbuf, at, *dims)

        mqkT = scr(4, T)
        mvx = scr(NT, H, DH + 1)
        mo = scr(NT, 256)
        convin = scr(4, T + 3)
        convout = scr(4, T)
        gqkT = scr(2, T)
        gv = scr(NT, 256)
        gr = scr(NT, 256)
        aqk = scr(NT, 8, 2, 32)
        rtmp = scr(NT, 8, 32)
        pss = view(wbuf, pos[0] - 1536, H, SCORE)
        rot = view(ACC, 0, NT, 8, 2, 32)
        kx = view(ACC, 1024, 28 * BLK)
        aqkT = scr(4, T)
        av = scr(NT, 256)
        sz = scr(NT, 256)
        sx = scr(NT, 256)
        xdt = scr(NT, 256)
        gdec = scr(T)
        gb = scr(T)
        gd1 = scr(T)
        gd2 = scr(T)
        gl = scr(T)
        ge = scr(3, T)
        PT = scr(H, SCORE)
        PTa = scr(H, SCORE)
        mpos = [0]

        def mscr(*dims):
            n = 1
            for d in dims:
                n *= d
            at = mpos[0]
            mpos[0] += n
            assert mpos[0] <= 5632, mpos
            return view(misc, at, *dims)

        z = mscr(T)
        lt = mscr(T)
        lsg = mscr(T)
        lsp = mscr(T)
        R = mscr(T)
        C0 = mscr(T)
        MR = mscr(T)
        RC = mscr(NT, P)
        nac = mscr(NT, H)
        enm = mscr(NT, H)
        acol = mscr(1)
        rm = mscr(2, 2)
        rden = mscr(NT, H)
        aden = mscr(NT, H)
        st1 = mscr(NT, H)
        st2 = mscr(NT, H)
        st3 = mscr(NT, H)
        E = [mscr(SCORE) for _ in range(2)]
        Pm = [mscr(SCORE) for _ in range(2)]
        pml = mscr(H, SCORE)
        tmp = view(misc, 0, NT, 256)
        mpos[0] = 0
        def mscr16(*dims):
            n = 1
            for d in dims:
                n *= d
            ap = mscr(n // 2).bitcast(BF16)
            names = "abcd"[:len(dims)]
            return ap if len(dims) == 1 else ap.rearrange(
                "p (" + " ".join(names) + ") -> p " + " ".join(names), **{c: d for c, d in zip(names, dims)})

        Sel = [mscr16(NT, 2, CAP) for _ in range(2)]
        SelT = [mscr16(T) for _ in range(2)]
        Gp = [mscr16(NT, 2, 4) for _ in range(2)]
        gslot = mscr(4)[:, 0:1]
        XG = mscr(KD, 2 * CAP)
        HS = mscr(F)
        Hh = mscr(F)
        HT = mscr(2, 2 * CAP)
        Y3 = mscr16(3, D)
        YR = mscr(D)
        G = mscr(NT, EXPERTS)
        rank = mscr(NT, EXPERTS)
        SC = mscr(NT, EXPERTS)
        Gs = mscr16(NT, EXPERTS, 4)
        ident16 = mscr16(P)
        X3 = [sb("X_first", D)[:, :].bitcast(BF16), XT[:, 0:D].bitcast(BF16), XT[:, D:2 * D].bitcast(BF16)]
        X3 = [x.rearrange("p (t d) -> p t d", t=NT) for x in X3]
        r0 = 512
        selm = view(misc, r0, NT, EXPERTS)
        selr = view(misc, r0 + 128, NT, EXPERTS)
        m8 = view(misc, r0 + 256, NT, GROUPS, 8)
        grp = view(misc, r0 + 384, NT, GROUPS)
        cmp1 = view(misc, r0 + 400, NT, GROUPS, GROUPS)
        cmp2 = view(misc, r0 + 528, NT, GROUPS, GROUPS)
        gmask = view(misc, r0 + 656, NT, GROUPS)
        t8 = view(misc, r0 + 672, NT, 8)
        Mk = view(misc, r0 + 688, NT, EXPERTS)
        gs = view(misc, r0 + 816, NT)
        cnt = view(misc, r0 + 818, 2)
        shh = view(misc, 2304, NT, F)
        lnb = sb("lnb", 64)
        bst = view(lnb, 0, NT, 2, 6)
        bag = view(lnb, 24, NT, 2)
        rstd = view(lnb, 28, NT)

        def C(name):
            return cst[:, CST[name]]

        ident = C("ident")
        before = C("before")
        ones = C("ones")
        sh_w = view(stage, 0, 2, KD, F)
        sh_d = view(stage, 4096, 2, D)
        rw = view(stage, 6144, KD, EXPERTS)
        wo = view(stage, 0, KD, D)
        shT = view(stage, 6656, 2, T)

        ps = [ctx.enter_context(nc.psum_tensor(f"ps{i}", [P, 512], F32)) for i in range(4)]
        psA = ctx.enter_context(nc.psum_tensor("psA", [P, 4, 512], F32))
        ps = [t[:, :] for t in ps] + [psA[:, i, :] for i in range(4)]

        cst_loaded = sem("cst_loaded")
        in_loaded = [sem(f"in_loaded{b}") for b in range(2)]
        gu_loaded = [sem(f"gu_loaded{b}") for b in range(2)]
        dn_loaded = [sem(f"dn_loaded{b}") for b in range(2)]
        gu_used = [sem(f"gu_used{b}") for b in range(2)]
        dn_used = [sem(f"dn_used{b}") for b in range(2)]
        layer_done = sem("layer_done")
        layer_open = sem("layer_open")
        out_stored = sem("out_stored")
        sp_held = sem("sp_held")
        pool_held = sem("pool_held")
        cleared = []

        def lsem(name):
            s = sem(name)
            cleared.append(s)
            return s

        cols_loaded = lsem("cols_loaded")
        rows_loaded = lsem("rows_loaded")
        wo_loaded = [lsem(f"wo_loaded{b}") for b in range(2)]
        router_loaded = lsem("router_loaded")
        shared_loaded = lsem("shared_loaded")
        mixers_done = lsem("mixers_done")
        proj_done = lsem("proj_done")
        proj_read = lsem("proj_read")
        xt_done = lsem("xt_done")
        xt_read = lsem("xt_read")
        gate_rows = lsem("gate_rows")
        gla_gate = lsem("gla_gate")
        logs_ready = lsem("logs_ready")
        gla_logs = lsem("gla_logs")
        rows_ready = lsem("rows_ready")
        cols_done = lsem("cols_done")
        cols_ready = lsem("cols_ready")
        conv_raw = lsem("conv_raw")
        conv_ready = lsem("conv_ready")
        sxt_done = lsem("sxt_done")
        sx_ready = lsem("sx_ready")
        rope_ready = lsem("rope_ready")
        qkt_done = lsem("qkt_done")
        qkt_read = lsem("qkt_read")
        score_done = lsem("score_done")
        score_read = lsem("score_read")
        bc_done = lsem("bc_done")
        bc_read = lsem("bc_read")
        arg_ready = lsem("arg_ready")
        exp_ready = lsem("exp_ready")
        prob_ready = lsem("prob_ready")
        prob_used = lsem("prob_used")
        at_arg = lsem("at_arg")
        at_exp = lsem("at_exp")
        at_prob = lsem("at_prob")
        at_tr = lsem("at_tr")
        at_trc = lsem("at_trc")
        at_used = lsem("at_used")
        o_done = lsem("o_done")
        o_read = lsem("o_read")
        gla_arg = lsem("gla_arg")
        gla_exp = lsem("gla_exp")
        gla_qk = lsem("gla_qk")
        gla_sc = lsem("gla_sc")
        gla_pt = lsem("gla_pt")
        rms_in = lsem("rms_in")
        rms_out = lsem("rms_out")
        gates_ready = lsem("gates_ready")
        y_ready = lsem("y_ready")
        yt_done = lsem("yt_done")
        yt_read = lsem("yt_read")
        op_done = lsem("op_done")
        op_read = lsem("op_read")
        x1_ready = lsem("x1_ready")
        rt_done = lsem("rt_done")
        score_sig = lsem("score_sig")
        mask_ready = lsem("mask_ready")
        rank_done = lsem("rank_done")
        rounds_ready = lsem("rounds_ready")
        sh_done = lsem("sh_done")
        sh_silu = lsem("sh_silu")
        sh_hid = lsem("sh_hid")
        sht_done = lsem("sht_done")
        sht_read = lsem("sht_read")
        sho_done = lsem("sho_done")
        dve_own = lsem("dve_own")
        act_own = lsem("act_own")
        sel_ready = lsem("sel_ready")
        selg_ready = lsem("selg_ready")
        rank_next = lsem("rank_next")
        gathered = lsem("gathered")
        xg_act = lsem("xg_act")
        xg_dve = lsem("xg_dve")
        silu_done = lsem("silu_done")
        h_done = lsem("h_done")
        ht_tr = lsem("ht_tr")
        ht_done = lsem("ht_done")
        st_tr = lsem("st_tr")
        st_done = lsem("st_done")
        dn_half = lsem("dn_half")
        ys_hi = lsem("ys_hi")
        ys_rest = lsem("ys_rest")
        ys_mid = lsem("ys_mid")
        ys_lo = lsem("ys_lo")
        x_hi = lsem("x_hi")
        x_rest = lsem("x_rest")
        x_mid = lsem("x_mid")
        x_split = lsem("x_split")
        sc_done = lsem("sc_done")
        acc_done = lsem("acc_done")

        selT_ps = ps[7][:, T:T + P].bitcast(BF16)
        gate_ps = ps[7][:, 3 * P:3 * P + 8]
        ACC0 = 4
        block = ctx.enter_context(nc.Block())

        def head_rows(h):
            return slice(DH * (h % 2), DH * (h % 2) + DH)

        @block.sync
        def _(sp):
            sp.dma_start(Xv, x_in.rearrange("(t p) d -> p t d", p=P)).then_inc(cst_loaded, 16)
            sp.dma_start(cst[:, :], cst_in).then_inc(cst_loaded, 16)
            before_dp = sp.alloc_register("sp_before")
            sp.reg_mov(before_dp, 0)


            def load_in(l, gi):
                at = KD * sum(g[1] for g in GROUPS_IN[:gi])
                n = KD * GROUPS_IN[gi][1]
                b = gi % 2
                sp.dma_start(stage[:, 4096 * b:4096 * b + n], w_in[l][:, at:at + n]).then_inc(in_loaded[b], 16)

            load_in(0, 0)
            load_in(0, 1)
            with sp.Fori(0, layers) as l:
                base = sp.snap(before_dp)
                sp.dma_start(colp[:, :], cols_in[l]).then_inc(cols_loaded, 16)
                for gi in range(1, len(GROUPS_IN)):
                    if gi >= 2:
                        sp.wait_ge(proj_done, sum(UNITS[:gi - 1]))
                        load_in(l, gi)
                    if gi == 2:
                        sp.dma_start(rowp[:, :], rows_in[l].partition_broadcast(P)).then_inc(rows_loaded, 16)
                    if gi == 3:
                        sp.wait_ge(gu_used[0], base + 1)
                        sp.sem_inc(sp_held, 1)
                        sp.dma_start(wgu[0][:, :, 0, :, :], e_gate[l][0]).then_inc(gu_loaded[0], 16)
                        sp.dma_start(wgu[0][:, :, 1, :, :], e_up[l][0]).then_inc(gu_loaded[0], 16)
                for b in range(2):
                    sp.wait_ge(proj_done, sum(UNITS[:len(UNITS) - 1 + b]))
                    sp.dma_start(wo[:, 4 * b:4 * b + 4, :], w_out[l][512 * b:512 * b + 512]
                                 .rearrange("(k p) d -> p k d", p=P)).then_inc(wo_loaded[b], 16)
                sp.wait_ge(mixers_done, 1)
                sp.wait_ge(gu_used[1], base + 1)
                sp.sem_inc(sp_held, 1)
                sp.dma_start(wgu[1][:, :, 0, :, :], e_gate[l][1]).then_inc(gu_loaded[1], 16)
                sp.dma_start(wgu[1][:, :, 1, :, :], e_up[l][1]).then_inc(gu_loaded[1], 16)
                sp.wait_ge(op_done, 4)
                sp.dma_start(rw, router_w[l].rearrange("(p k) e -> p k e", k=KD)).then_inc(router_loaded, 16)
                sp.dma_start(sh_w[:, 0], sh_gate[l].rearrange("(p k) f -> p k f", k=KD)).then_inc(shared_loaded, 16)
                sp.dma_start(sh_w[:, 1], sh_up[l].rearrange("(p k) f -> p k f", k=KD)).then_inc(shared_loaded, 16)
                sp.dma_start(sh_d, sh_down[l].rearrange("(p k) d -> p k d", k=2)).then_inc(shared_loaded, 16)
                def load_down(j, b):
                    sp.wait_ge(dn_used[b], base + j + 1)
                    sp.sem_inc(sp_held, 1)
                    sp.dma_start(wdn[b], e_down[l][(j * 2 + b) % PAIRS]).then_inc(dn_loaded[b], 16)

                load_down(0, 0)
                sp.wait_ge(rounds_ready, 1)
                last = sp.value_load(last_pair2[0:1, 0:1], min_val=PAIRS // 2 - 1, max_val=ROUNDS * PAIRS // 2 - 1)
                pairs2 = last + 1
                with sp.Fori(0, last) as j:
                    for b in range(2):
                        load_down(j + b, 1 - b)
                        sp.wait_ge(gu_used[b], base + j + 2)
                        sp.sem_inc(sp_held, 1)
                        sp.dma_start(wgu[b][:, :, 0, :, :], e_gate[l][(j * 2 + 2 + b) % PAIRS]).then_inc(gu_loaded[b], 16)
                        sp.dma_start(wgu[b][:, :, 1, :, :], e_up[l][(j * 2 + 2 + b) % PAIRS]).then_inc(gu_loaded[b], 16)
                load_down(last, 1)
                for gi in range(2):
                    load_in((l + 1) % DEPTH, gi)
                sp.reg_add(before_dp, before_dp, pairs2)
                sp.sem_inc(layer_done, 1)
                sp.wait_ge(layer_open, l + 1)
                sp.sem_inc(sp_held, 1)
            for b in range(2):
                sp.wait_ge(in_loaded[b], 16 * (layers * len(GROUPS_IN) // 2 + 1))
            sp.dma_start(out.rearrange("(t p) d -> p t d", p=P), Xv).then_inc(out_stored, 16)
            sp.wait_ge(out_stored, 16)

        @block.gpsimd
        def _(pool):
            with pool.Fori(0, layers) as l:
                pool.wait_ge(layer_done, 4 * (l + 1))
                pool.sem_inc(pool_held, 1)
                for s in cleared:
                    pool.sem_clear(s)
                pool.sem_inc(layer_open, 1)

        @block.tensor
        def _(pe):
            before_dp = pe.alloc_register("pe_before")
            pe.reg_mov(before_dp, 0)
            for b in range(2):
                pe.sem_inc(gu_used[b], 1)
                pe.sem_inc(dn_used[b], 1)
            pe.wait_ge(cst_loaded, 32)

            def transpose_x(n0, ready=None):
                xs = Xv.rearrange("p t (q k) -> p t k q", k=KD)
                for u in range(4):
                    t = u // 2
                    if ready and u % 2 == 0:
                        pe.wait_ge(ready, t + 1)
                    if u >= 2:
                        pe.wait_ge(xt_read, n0 + u - 1)
                    for kk in range(4):
                        mm = pe.transpose(ps[u % 2][:, kk * P:(kk + 1) * P], xs[:, t, 4 * (u % 2) + kk, :], ident)
                    mm.then_inc(xt_done, 1)

            def transposed_scores(bank, keys, queries):
                pe.matmul(bank[:, 0:T], keys[:, 0:P], queries[:, 0:T], start=True, stop=True)
                return pe.matmul(bank[:, T:T + P], keys[:, P:T], queries[:, P:T], start=True, stop=True)

            def apply(out0, out1, p, values):
                pe.matmul(out0, p[:, 0:P], values(0), start=True, stop=True)
                pe.matmul(out1, p[:, P:2 * P], values(0), start=True, stop=False)
                return pe.matmul(out1, p[:, 2 * P:3 * P], values(1), start=False, stop=True)

            def head_row(bank, rows, h):
                r = slice(rows.start, rows.start + H)
                src = MR if rows.start == 0 else R
                pe.matmul(bank[:, 0:T], cst[r, CST["head"]][:, h * P:(h + 1) * P], src[r, :],
                          start=True, stop=True).then_inc(bc_done, 1)

            def gla_gate_rows():
                pe.wait_ge(gate_rows, 1)
                pe.matmul(ps[2][:, 0:T], colp[96:112, COL["gate_w2"]], z[96:112, :],
                          start=True, stop=True).then_inc(gla_gate, 1)

            def gate_columns():
                pe.wait_ge(rows_ready, 1)
                for t in range(NT):
                    mm = pe.transpose(ps[3][:, t * P:(t + 1) * P], R[:, t * P:(t + 1) * P], ident)
                mm.then_inc(cols_done, 1)

            def ml_scores(h):
                if h == 0:
                    pe.wait_ge(proj_read, FIRST["mlstm_qk"] + 2)
                    pe.wait_ge(cols_ready, 2)
                else:
                    pe.wait_ge(score_read, max(h - 1, 0))
                    pe.wait_ge(bc_read, max(h - 1, 0))
                r = head_rows(h)
                transposed_scores(ps[4 + h % 2], mqkT[r, 2 + h // 2, :], mqkT[r, h // 2, :]).then_inc(score_done, 1)
                head_row(ps[2 + h % 2], slice(0, H), h)

            def rotated_columns():
                pe.wait_ge(rope_ready, 1)
                rf = rot.rearrange("p t h s e -> p t (h s e)")
                for c in range(4):
                    for t in range(NT):
                        mm = pe.transpose(ps[6 + c // 2][:, (c % 2) * T + t * P:(c % 2) * T + (t + 1) * P],
                                          rf[:, t, c * P:(c + 1) * P], ident)
                mm.then_inc(qkt_done, 1)

            def at_scores(h):
                pe.wait_ge(score_read, H + h - 1)
                if h == 0:
                    pe.wait_ge(qkt_read, 1)
                r = head_rows(h)
                q, k = aqkT[r, h // 2, :], aqkT[r, 2 + h // 2, :]
                bank = ps[4 + h % 2]
                pe.matmul(bank[:, 0:P], q[:, 0:P], k[:, 0:P], start=True, stop=True)
                pe.matmul(bank[:, P:SCORE], q[:, P:T], k, start=True, stop=True).then_inc(score_done, 1)

            def at_transposes(h):
                pe.wait_ge(at_prob, h + 1)
                if h >= 2:
                    pe.wait_ge(at_trc, h - 1)
                for i in range(3):
                    mm = pe.transpose(ps[6 + h % 2][:, i * P:(i + 1) * P], Pm[h % 2][:, i * P:(i + 1) * P], ident)
                mm.then_inc(at_tr, 1)

            def ssm_columns():
                pe.wait_ge(conv_ready, 1)
                pe.wait_ge(bc_read, H)
                for t in range(NT):
                    for c in range(2):
                        mm = pe.transpose(ps[2][:, t * 256 + c * P:t * 256 + (c + 1) * P],
                                          convout[:, c, t * P:(t + 1) * P], ident)
                mm.then_inc(sxt_done, 1)

            def gla_scores():
                pe.wait_ge(score_read, 2 * H)
                pe.wait_ge(at_trc, H)
                pe.wait_ge(gla_qk, 1)
                for j in range(NB):
                    js = slice(BLK * j, BLK * (j + 1))
                    jj, t = j % 4, j // 4
                    col = BLK * j if t == 0 else 2 * P + BLK * jj
                    k0 = BLK * (j * (j - 1) // 2)
                    for h in range(H):
                        r = slice(DK * h, DK * (h + 1))
                        mm = pe.matmul(psA[BLK * jj:BLK * (jj + 1), h, col:col + BLK], ge[r, 1, js], ge[r, 0, js],
                                       start=True, stop=True)
                        if t == 0 and j > 0:
                            mm = pe.matmul(psA[0:BLK * j, h, col:col + BLK], kx[r, k0:k0 + BLK * j], ge[r, 2, js],
                                           start=True, stop=True)
                        if t == 1:
                            mm = pe.matmul(psA[:, h, BLK * j:BLK * j + BLK], kx[r, k0:k0 + P], ge[r, 2, js],
                                           start=True, stop=True)
                            if jj > 0:
                                mm = pe.matmul(psA[0:BLK * jj, h, col:col + BLK],
                                               kx[r, k0 + P:k0 + P + BLK * jj], ge[r, 2, js], start=True, stop=True)
                mm.then_inc(gla_sc, 1)

            def ssm_maps():
                pe.wait_ge(gla_pt, 1)
                for g in range(2):
                    r = slice(64 * g, 64 * g + 64)
                    mm = transposed_scores(ps[6 + g], convout[r, 2, :], convout[r, 3, :])
                mm.then_inc(score_done, 1)

            def ssm_decay(h):
                if h >= 2:
                    pe.wait_ge(bc_read, H + h - 1)
                head_row(ps[4 + h % 2], slice(64, 64 + H), h)

            def ml_apply():
                pe.wait_ge(proj_read, FIRST["mlstm_vo"] + 2)
                pe.wait_ge(sx_ready, 1)
                pe.wait_ge(prob_ready, H)
                for h in range(H):
                    c = h * (DH + 1)
                    mm = apply(ps[2][:, c:c + DH + 1], ps[3][:, c:c + DH + 1], pml[:, h, :], lambda t: mvx[:, t, h, :])
                mm.then_inc(o_done, 1)

            def rows_of(bank, maps, values):
                for h in range(H):
                    mm = apply(bank[:, h * DH:(h + 1) * DH], bank[:, 256 + h * DH:256 + (h + 1) * DH], maps[:, h, :],
                               lambda t: values[:, t, h * DH:(h + 1) * DH])
                mm.then_inc(o_done, 1)

            BETWEEN = {
                2: [gla_gate_rows],
                3: [gate_columns],
                5: [lambda: ml_scores(0), lambda: ml_scores(1)],
                6: [lambda: ml_scores(2), lambda: ml_scores(3)],
                7: [rotated_columns],
                8: [lambda: at_scores(0), lambda: at_scores(1)],
                9: [lambda: at_transposes(0), lambda: at_transposes(1), lambda: at_scores(2), lambda: at_scores(3)],
                10: [lambda: at_transposes(2), lambda: at_transposes(3), ssm_columns],
                11: [gla_scores],
                12: [ssm_maps, lambda: ssm_decay(0), lambda: ssm_decay(1), ml_apply],
                13: [lambda: ssm_decay(2), lambda: ssm_decay(3)],
            }

            with pe.Fori(0, layers) as l:
                base = pe.snap(before_dp)
                transpose_x(0)
                pe.wait_ge(xt_read, 4)
                u = 0
                count = [0, 0]
                for gi, (name, n, chan) in enumerate(GROUPS_IN):
                    b = gi % 2
                    count[b] += 16
                    pe.wait_ge(in_loaded[b], l * (8 * len(GROUPS_IN)) + count[b])
                    w = view(stage, 4096 * b, KD, n)
                    for h in range(UNITS[gi]):
                        if u >= 2:
                            pe.wait_ge(proj_read, u - 1)
                        bank = ps[u % 2]
                        if chan:
                            for m in range(min(2, n // P)):
                                for k in range(KD):
                                    c = (2 * h + m) * P
                                    mm = pe.matmul(bank[:, m * T:(m + 1) * T], w[:, k, c:c + P], XT3[:, k, :],
                                                   start=(k == 0), stop=(k == KD - 1))
                        else:
                            for k in range(KD):
                                mm = pe.matmul(bank, XT3[:, k, h * P:(h + 1) * P], w[:, k, :],
                                               start=(k == 0), stop=(k == KD - 1))
                        mm.then_inc(proj_done, 1)
                        for step in BETWEEN.get(u, []):
                            step()
                        u += 1
                pe.wait_ge(proj_read, 14)
                rows_of(ps[0], PT, gv)
                pe.wait_ge(at_trc, H)
                rows_of(ps[1], PTa, av)
                pe.wait_ge(prob_ready, 2 * H)
                pe.wait_ge(o_read, 1)
                rows_of(ps[2], pss, xdt)
                for i, m in enumerate(YORDER):
                    pe.wait_ge(y_ready, i + 1)
                    bank = ps[(3, 0, 1, 2)[i]]
                    for kk in range(2):
                        k = 2 * m + kk
                        for t in range(NT):
                            mm = pe.transpose(bank[:, kk * T + t * P:kk * T + (t + 1) * P],
                                              ACCv[:, t, k * P:(k + 1) * P], ident)
                    mm.then_inc(yt_done, 1)
                    pe.wait_ge(yt_read, i + 1)
                    pe.wait_ge(wo_loaded[m // 2], 16)
                    for t in range(NT):
                        for n in range(2):
                            for k in range(2 * m, 2 * m + 2):
                                mm = pe.matmul(ps[4 + 2 * t + n], XT3[:, k, t * P:(t + 1) * P],
                                               wo[:, k, n * 512:(n + 1) * 512], start=(i == 0 and k == 2 * m),
                                               stop=(i == 3 and k == 2 * m + 1))
                            if i == 3:
                                mm.then_inc(op_done, 1)

                transpose_x(4, x1_ready)
                pe.wait_ge(xt_read, 8)
                pe.wait_ge(router_loaded, 16)
                for t in range(NT):
                    for k in range(KD):
                        mm = pe.matmul(ps[2][:, t * EXPERTS:(t + 1) * EXPERTS], XT3[:, k, t * P:(t + 1) * P],
                                       rw[:, k, :], start=(k == 0), stop=(k == KD - 1))
                mm.then_inc(rt_done, 1)
                pe.wait_ge(shared_loaded, 48)
                for t in range(NT):
                    for k in range(KD):
                        mm = pe.matmul(ps[4 + t], XT3[:, k, t * P:(t + 1) * P], sh_w[:, :, k, :],
                                       start=(k == 0), stop=(k == KD - 1))
                    mm.then_inc(sh_done, 1)
                pe.wait_ge(mask_ready, 1)
                pe.matmul(ps[3][:, 0:EXPERTS], before, Mk[:, 0, :], start=True, stop=True)
                pe.matmul(ps[3][:, EXPERTS:2 * EXPERTS], ones[:, 0:P], Mk[:, 0, :], start=True, stop=False)
                pe.matmul(ps[3][:, EXPERTS:2 * EXPERTS], before, Mk[:, 1, :], start=False, stop=True)
                pe.matmul(ps[3][:, 2 * EXPERTS:3 * EXPERTS], ones[:, 0:P], Mk[:, 0, :], start=True, stop=False)
                pe.matmul(ps[3][:, 2 * EXPERTS:3 * EXPERTS], ones[:, 0:P], Mk[:, 1, :],
                          start=False, stop=True).then_inc(rank_done, 1)
                pe.wait_ge(sh_hid, 2)
                for t in range(NT):
                    for k in range(2):
                        mm = pe.transpose(ps[7][:, k * T + t * P:k * T + (t + 1) * P],
                                          shh[:, t, :].rearrange("p (f k) -> p k f", k=2)[:, k, :], ident)
                mm.then_inc(sht_done, 1)
                pe.wait_ge(sht_read, 1)
                for t in range(NT):
                    for n in range(2):
                        for k in range(2):
                            mm = pe.matmul(ps[4 + 2 * t + n], shT[:, k, t * P:(t + 1) * P],
                                           sh_d[:, k, n * 512:(n + 1) * 512], start=(k == 0), stop=(k == 1))
                        mm.then_inc(sho_done, 1)

                xs = [x.rearrange("p t (q k) -> p t k q", k=KD) for x in X3]

                def gather(g, b):
                    pe.wait_ge(sel_ready, g + 1)
                    for q in range(2):
                        for k in range(4 * q, 4 * q + 4):
                            for i in range(3 * NT):
                                mm = pe.matmul(ps[1 + q][:, (k % 4) * P:(k % 4 + 1) * P], xs[i // NT][:, i % NT, k, :],
                                               Sel[b][:, i % NT, :, :], start=(i == 0), stop=(i == 3 * NT - 1))
                        mm.then_inc(gathered, 1)

                def scatter(g, b):
                    pe.wait_ge(ys_lo, 2 * g + 2)
                    for t in range(NT):
                        for n in range(2):
                            q = 2 * t + n
                            pe.wait_ge(acc_done, 4 * g + q - 1 + ACC0)
                            for i in range(3):
                                mm = pe.matmul(ps[5 + q % 2], SelT[1 - b][:, t * P:(t + 1) * P],
                                               Y3[:, i, n * 512:(n + 1) * 512], start=(i == 0), stop=(i == 2))
                            mm.then_inc(sc_done, 1)

                def transposed_map(g, b):
                    pe.wait_ge(selg_ready, g + 1)
                    for t in range(NT):
                        pe.transpose(selT_ps[:, t * P:(t + 1) * P], Sel[b][:, t, :, :], ident16)
                    for t in range(NT):
                        mm = pe.matmul(gate_ps, Sel[b][:, t, :, :], Gp[b][:, t, :, :],
                                       start=(t == 0), stop=(t == NT - 1))
                    mm.then_inc(st_tr, 1)

                pe.wait_ge(rounds_ready, 1)
                last = pe.value_load(last_pair2[0:1, 0:1], min_val=PAIRS // 2 - 1, max_val=ROUNDS * PAIRS // 2 - 1)
                pairs2 = last + 1
                pe.sem_inc(ht_tr, 1)
                pe.wait_ge(x_split, 1)
                pe.wait_ge(acc_done, ACC0)
                gather(0, 0)
                transposed_map(0, 0)
                with pe.Fori(0, pairs2) as j:
                    for b in range(2):
                        g = 2 * j + b
                        pe.wait_ge(gu_loaded[b], (base + j + 1) * 32)
                        pe.wait_ge(xg_act, g + 1)
                        pe.wait_ge(xg_dve, g + 1)
                        pe.wait_ge(h_done, g + 1)
                        for k in range(KD):
                            for e in range(2):
                                mm = pe.matmul(ps[0][64 * e:64 * e + CAP, :],
                                               XG[:, k, CAP * e:CAP * (e + 1)], wgu[b][:, e, :, k, :],
                                               start=(k == 0), stop=(k == KD - 1))
                        mm.then_inc(gu_used[b], 1)
                        gather(g + 1, 1 - b)
                        pe.wait_ge(h_done, g + 2)
                        pe.wait_ge(ht_done, g + 1)
                        pe.wait_ge(st_done, g + 2)
                        for k in range(2):
                            mm = pe.transpose(ps[7][:, k * P:(k + 1) * P],
                                              Hh.rearrange("p (f k) -> p k f", k=2)[:, k, :], ident)
                        mm.then_inc(ht_tr, 1)
                        scatter(g, b)
                        pe.wait_ge(ht_done, g + 2)
                        transposed_map(g + 1, 1 - b)
                        pe.wait_ge(dn_loaded[b], (base + j + 1) * 16)
                        for n in range(2):
                            for k in range(2):
                                for e in range(2):
                                    mm = pe.matmul(ps[3 + n][64 * e:64 * e + CAP, :], HT[:, k, CAP * e:CAP * (e + 1)],
                                                   wdn[b][:, e, k, n * 512:(n + 1) * 512],
                                                   start=(k == 0), stop=(k == 1))
                            mm.then_inc(dn_half if n == 0 else dn_used[b], 1)
                scatter(2 * pairs2, 0)
                pe.reg_add(before_dp, before_dp, pairs2)
                pe.sem_inc(layer_done, 1)
                pe.wait_ge(layer_open, l + 1)

        @block.scalar
        def _(act):
            own = [0]

            def link(ins):
                own[0] += 1
                ins.then_inc(act_own, 1)
                act.wait_ge(act_own, own[0])

            def copy(o, i):
                return act.activation(o, i, ACT.Copy)

            before_dp = act.alloc_register("act_before")
            act.reg_mov(before_dp, 0)
            act.wait_ge(cst_loaded, 32)
            with act.Fori(0, layers) as l:
                own[0] = 0
                base = act.snap(before_dp)
                def xt_half(n0):
                    for t in range(NT):
                        act.wait_ge(xt_done, n0 + 2 * t + 1)
                        if n0 + t:
                            act.wait_ge(xt_read, n0 + 2 * t)
                        copy(XT3[:, 0:4, t * P:(t + 1) * P],
                             ps[0].rearrange("p (k t) -> p k t", k=4)).then_inc(xt_read, 1)

                xt_half(0)
                act.wait_ge(cols_loaded, 16)
                act.wait_ge(proj_done, 1)
                link(act.activation(z, ps[0][:, 0:T], ACT.Identity, bias=colp[:, COL["bias"]]))
                act.sem_inc(proj_read, 1)
                act.sem_inc(gate_rows, 1)

                def log1p_exp(o, i):
                    link(act.activation(o, i, ACT.Abs))
                    link(act.activation(o, o, ACT.Exp, scale=-1.0))
                    link(act.activation(o, o, ACT.Ln, bias=1.0))

                log1p_exp(lt, z)
                link(act.activation(acol[64:64 + H, :], colp[64:64 + H, COL["a_log"]], ACT.Exp))
                act.sem_inc(logs_ready, 1)

                def unit(u, *moves):
                    act.wait_ge(proj_done, u + 1)
                    for o, c in moves:
                        n = o.ndim
                        src = ps[u % 2][:, c]
                        if n == 3:
                            src = src.rearrange("p (m t) -> p m t", m=o.shape[1])
                        ins = copy(o, src)
                    ins.then_inc(proj_read, 1)

                def decay(n, bias):
                    act.wait_ge(arg_ready, n + 1)
                    e = E[n % 2]
                    act.activation(e[:, 0:T], e[:, 0:T], ACT.Exp, bias=bias(0))
                    act.activation(e[:, T:SCORE], e[:, T:SCORE], ACT.Exp, bias=bias(1)).then_inc(exp_ready, 1)

                def ml_exp(h):
                    decay(h, lambda t: RC[:, t, h:h + 1])

                def ssm_exp(h):
                    decay(H + h, lambda t: nac[:, t, h:h + 1])

                def at_exp_of(h):
                    act.wait_ge(at_arg, h + 1)
                    e = E[h % 2]
                    act.activation(e[:, 0:P], e[:, 0:P], ACT.Exp, scale=-1.0, bias=rm[:, h % 2, 0:1])
                    act.activation(e[:, P:SCORE], e[:, P:SCORE], ACT.Exp, scale=-1.0,
                                   bias=rm[:, h % 2, 1:2]).then_inc(at_exp, 1)

                def at_copy(h):
                    act.wait_ge(at_tr, h + 1)
                    copy(PTa[:, h, :], ps[6 + h % 2][:, 0:SCORE]).then_inc(at_trc, 1)

                both = slice(0, 512)
                for i in range(2):
                    unit(FIRST["mlstm_qk"] + i, (mqkT[:, 2 * i:2 * i + 2, :], both))
                act.wait_ge(gla_gate, 1)
                link(act.activation(gdec, ps[2][:, 0:T], ACT.Identity, bias=colp[:, COL["gla_b"]]))
                log1p_exp(gl, gdec)
                act.sem_inc(gla_logs, 1)
                unit(FIRST["gla_qk"], (gqkT, both))
                act.wait_ge(cols_done, 1)
                link(act.activation(enm, ps[3].rearrange("p (t c) -> p t c", c=P)[:, 0:NT, 32:32 + H], ACT.Exp, scale=-1.0))
                act.sem_inc(cols_ready, 1)
                for t in range(NT):
                    unit(FIRST["att_qk"] + t, (aqk[:, t].rearrange("p h s e -> p (h s e)"), both))
                act.wait_ge(gla_arg, 1)
                act.activation(ge[:, 0, :], gd1, ACT.Exp)
                act.activation(ge[:, 1, :], gd1, ACT.Exp, scale=-1.0)
                act.activation(ge[:, 2, :], gd2, ACT.Exp)
                for j in range(1, NB):
                    k0 = BLK * (j * (j - 1) // 2)
                    ins = act.activation(kx[:, k0:k0 + BLK * j], gb[:, 0:BLK * j], ACT.Exp, scale=-1.0,
                                         bias=gb[:, BLK * j - 1:BLK * j])
                ins.then_inc(gla_exp, 1)
                act.wait_ge(cols_ready, 2)
                ml_exp(0)
                ml_exp(1)
                unit(FIRST["conv"], (convin[:, 0:2, 3:T + 3], both))
                ml_exp(2)
                ml_exp(3)
                unit(FIRST["conv"] + 1, (convin[:, 2:4, 3:T + 3], both))
                act.wait_ge(qkt_done, 1)
                for c in range(2):
                    ins = copy(aqkT[:, 2 * c:2 * c + 2, :], ps[6 + c].rearrange("p (m t) -> p m t", m=2))
                ins.then_inc(qkt_read, 1)
                halves = slice(0, 256), slice(256, 512)
                unit(8, (gv[:, 0, :], halves[0]), (gr[:, 0, :], halves[1]))
                at_exp_of(0)
                at_exp_of(1)
                unit(9, (gv[:, 1, :], halves[0]), (gr[:, 1, :], halves[1]))
                act.wait_ge(conv_raw, 1)
                for c in range(4):
                    ins = act.activation(convout[:, c, :], convout[:, c, :], ACT.Silu, bias=colp[:, 19 + c:20 + c])
                ins.then_inc(conv_ready, 1)
                at_copy(0)
                at_copy(1)
                at_exp_of(2)
                at_exp_of(3)
                act.wait_ge(dve_own, 1)
                unit(10, (mvx[:, 0, :, 0:DH], halves[0]), (mo[:, 0, :], halves[1]))
                at_copy(2)
                at_copy(3)
                unit(11, (mvx[:, 1, :, 0:DH], halves[0]), (mo[:, 1, :], halves[1]))
                unit(12, (av[:, 0, :], halves[0]), (sz[:, 0, :], halves[1]))
                ssm_exp(0)
                ssm_exp(1)
                unit(13, (av[:, 1, :], halves[0]), (sz[:, 1, :], halves[1]))
                ssm_exp(2)
                ssm_exp(3)
                link(act.activation(mo, mo, ACT.Sigmoid))
                link(act.activation(gr, gr, ACT.Silu))
                link(act.activation(sz, sz, ACT.Silu))
                act.sem_inc(gates_ready, 1)
                for i, (m, root) in enumerate(zip(YORDER, (st1, st2, None, st3))):
                    if root is not None:
                        n = (1, 2, None, 3)[i]
                        act.wait_ge(rms_in, n)
                        act.activation(root, root, ACT.Sqrt).then_inc(rms_out, 1)
                    act.wait_ge(yt_done, i + 1)
                    copy(XT3[:, 2 * m:2 * m + 2, :],
                         ps[(3, 0, 1, 2)[i]].rearrange("p (k t) -> p k t", k=2)).then_inc(yt_read, 1)
                for t in range(NT):
                    act.wait_ge(rms_in, 4 + t)
                    act.activation(rstd[:, t:t + 1], rstd[:, t:t + 1], ACT.Sqrt).then_inc(rms_out, 1)
                act.wait_ge(x1_ready, 2)
                copy(X3[0], Xv).then_inc(x_hi, 1)
                xt_half(4)
                act.wait_ge(rt_done, 1)
                act.activation(SC, ps[2][:, 0:NT * EXPERTS].rearrange("p (t e) -> p t e", t=NT),
                               ACT.Sigmoid).then_inc(score_sig, 1)
                for t in range(NT):
                    act.wait_ge(sh_done, t + 1)
                    act.activation(shh[:, t, :], ps[4 + t][:, 0:F], ACT.Silu).then_inc(sh_silu, 1)
                act.wait_ge(x_rest, 1)
                copy(X3[1], ACCv).then_inc(x_mid, 1)
                act.wait_ge(sht_done, 1)
                copy(shT, ps[7].rearrange("p (k t) -> p k t", k=2)).then_inc(sht_read, 1)
                act.wait_ge(rounds_ready, 1)
                last = act.value_load(last_pair2[0:1, 0:1], min_val=PAIRS // 2 - 1, max_val=ROUNDS * PAIRS // 2 - 1)
                pairs2 = last + 1

                def gathered_half(g):
                    act.wait_ge(gathered, 2 * g + 1)
                    copy(XG[:, 0:4, :], ps[1].rearrange("p (k s) -> p k s", k=4)).then_inc(xg_act, 1)

                act.sem_inc(ht_done, 1)
                gathered_half(0)
                with act.Fori(0, pairs2) as j:
                    for b in range(2):
                        g = 2 * j + b
                        act.wait_ge(gu_used[b], base + j + 2)
                        act.wait_ge(h_done, g + 1)
                        act.activation(HS, ps[0][:, 0:F], ACT.Silu).then_inc(silu_done, 1)
                        gathered_half(g + 1)
                        act.wait_ge(ht_tr, g + 2)
                        copy(HT, ps[7][:, 0:T].rearrange("p (k s) -> p k s", k=2)).then_inc(ht_done, 1)
                        act.wait_ge(sc_done, 4 * g + 4)
                        for n, s in enumerate((slice(0, 512), slice(512, D))):
                            if n == 0:
                                act.wait_ge(dn_half, g + 1)
                            else:
                                act.wait_ge(dn_used[b], base + j + 2)
                            copy(Y3[:, 0, s], ps[3 + n]).then_inc(ys_hi, 1)
                        for n, s in enumerate((slice(0, 512), slice(512, D))):
                            act.wait_ge(ys_rest, 2 * g + n + 1)
                            copy(Y3[:, 1, s], YR[:, s]).then_inc(ys_mid, 1)
                for t in range(NT):
                    act.wait_ge(rms_in, 6 + t)
                    act.activation(rstd[:, t:t + 1], rstd[:, t:t + 1], ACT.Sqrt).then_inc(rms_out, 1)
                act.reg_add(before_dp, before_dp, pairs2)
                act.sem_inc(layer_done, 1)
                act.wait_ge(layer_open, l + 1)

        @block.vector
        def _(dve):
            own = [0]

            def link(ins):
                own[0] += 1
                ins.then_inc(dve_own, 1)
                dve.wait_ge(dve_own, own[0])

            def tt(o, a, b, op):
                return dve.tensor_tensor(o, a, b, op)

            def mul(o, a, b):
                return tt(o, a, b, ALU.mult)

            def add(o, a, b):
                return tt(o, a, b, ALU.add)

            def heads(ap):
                return ap.rearrange("p t (h d) -> p t h d", h=H)

            def over(ap, n):
                return ap.unsqueeze(3).broadcast_to([P, ap.shape[1], ap.shape[2], n])

            def layer_norm(t, src, g, b, n):
                for h in range(2):
                    link(dve.bn_stats(bst[:, t, h, :], src[:, t, h * 512:(h + 1) * 512]))
                link(dve.bn_aggr(bag[:, t, :], bst[:, t, :, :].rearrange("p n s -> p (n s)")))
                link(dve.tensor_scalar(rstd[:, t:t + 1], bag[:, t, 1:2], EPS, None, ALU.add))
                dve.sem_inc(rms_in, 1)
                link(dve.scalar_tensor_tensor(src[:, t, :], src[:, t, :], bag[:, t, 0:1], rowp[:, ROW[g]],
                                              ALU.subtract, ALU.mult))
                dve.wait_ge(rms_out, n)
                link(dve.reciprocal(rstd[:, t:t + 1], rstd[:, t:t + 1]))
                link(dve.scalar_tensor_tensor(Xv[:, t, :], src[:, t, :], rstd[:, t:t + 1], rowp[:, ROW[b]],
                                              ALU.mult, ALU.add))

            before_dp = dve.alloc_register("dve_before")
            dve.reg_mov(before_dp, 0)
            dve.wait_ge(cst_loaded, 32)
            with dve.Fori(0, layers) as l:
                own[0] = 0
                base = dve.snap(before_dp)
                link(dve.memset(mvx[:, :, :, DH:DH + 1], 1.0))
                link(dve.memset(convin[:, :, 0:3], 0.0))
                link(dve.memset(R, 0.0))
                link(dve.memset(PT, 0.0))

                def xt_half(n0):
                    for t in range(NT):
                        dve.wait_ge(xt_done, n0 + 2 * t + 2)
                        dve.wait_ge(xt_read, n0 + 2 * t + 1)
                        dve.tensor_copy(XT3[:, 4:8, t * P:(t + 1) * P],
                                        ps[1].rearrange("p (k t) -> p k t", k=4)).then_inc(xt_read, 1)

                xt_half(0)
                dve.wait_ge(logs_ready, 1)
                fr, dr = slice(32, 32 + H), slice(64, 64 + H)
                link(dve.scalar_tensor_tensor(lsg[fr], z[fr], 0.0, lt[fr], ALU.min, ALU.subtract))
                link(dve.scalar_tensor_tensor(lsp[dr], z[dr], 0.0, lt[dr], ALU.max, ALU.add))
                link(dve.tensor_copy(R[96:96 + H], lsp[dr]))
                link(dve.tensor_scalar(lsp[dr], lsp[dr], acol[dr], -1.0, ALU.mult, ALU.mult))
                link(dve.tensor_tensor_scan(R[dr], ones[dr], lsp[dr], 0.0, ALU.mult, ALU.add))
                link(dve.tensor_tensor_scan(lsg[fr], ones[fr], lsg[fr], 0.0, ALU.mult, ALU.add))
                link(dve.tensor_copy(C0[0:H], lsg[fr]))
                link(tt(R[0:H], z[0:H], C0[0:H], ALU.subtract))
                link(dve.tensor_tensor_scan(MR[0:H], R[0:H], R[0:H], -3.0e38, ALU.max, ALU.max))
                link(add(C0[0:H], C0[0:H], MR[0:H]))
                link(dve.tensor_copy(R[fr], C0[0:H]))
                dve.sem_inc(rows_ready, 1)
                dve.wait_ge(gla_logs, 1)
                link(dve.scalar_tensor_tensor(gl, gdec, 0.0, gl, ALU.min, ALU.subtract))
                link(dve.tensor_scalar(gl, gl, 1.0 / TAU, None, ALU.mult))
                link(dve.tensor_tensor_scan(gb, ones, gl, 0.0, ALU.mult, ALU.add))
                b3 = gb.rearrange("p (j i) -> p j i", i=BLK)
                link(tt(gd1.rearrange("p (j i) -> p j i", i=BLK), b3,
                        b3[:, :, BLK // 2 - 1:BLK // 2].broadcast_to([P, NB, BLK]), ALU.subtract))
                link(dve.tensor_scalar(gd1, gd1, CLAMP, -CLAMP, ALU.min, ALU.max))
                link(dve.tensor_copy(gd2[:, 0:BLK], gb[:, 0:BLK]))
                link(tt(gd2[:, BLK:T].rearrange("p (j i) -> p j i", i=BLK), b3[:, 1:NB, :],
                        b3[:, 0:NB - 1, BLK - 1:BLK].broadcast_to([P, NB - 1, BLK]), ALU.subtract))
                dve.sem_inc(gla_arg, 1)
                dve.wait_ge(cols_done, 1)
                dve.wait_ge(cols_ready, 1)
                link(dve.tensor_copy(RC, ps[3][:, 0:T].rearrange("p (t c) -> p t c", c=P)))
                link(dve.tensor_scalar(nac, RC[:, :, 64:64 + H], -1.0, None, ALU.mult))
                dve.sem_inc(cols_ready, 1)

                def decay_arg(n, bank, sign):
                    dve.wait_ge(bc_done, n + 1)
                    e = E[n % 2]
                    cm = C("causal")
                    link(tt(e[:, 0:T], cm[:, 0:T], bank[:, 0:T], sign))
                    link(tt(e[:, T:SCORE], cm[:, T:SCORE], bank[:, P:T], sign))
                    dve.sem_inc(bc_read, 1)
                    dve.sem_inc(arg_ready, 1)

                def ml_arg(h):
                    decay_arg(h, ps[2 + h % 2], ALU.subtract)

                def ml_prob(h):
                    dve.wait_ge(exp_ready, h + 1)
                    dve.wait_ge(score_done, h + 1)
                    link(dve.scalar_tensor_tensor(pml[:, h, :], ps[4 + h % 2][:, 0:SCORE], DH ** -0.5, E[h % 2],
                                                  ALU.mult, ALU.mult))
                    dve.sem_inc(score_read, 1)
                    dve.sem_inc(prob_ready, 1)

                def ssm_arg(h):
                    decay_arg(H + h, ps[4 + h % 2], ALU.add)

                def ssm_prob(h):
                    dve.wait_ge(exp_ready, H + h + 1)
                    dve.wait_ge(score_done, 2 * H + 1)
                    link(mul(pss[:, h, :], ps[6 + h // 2][:, 0:SCORE], E[h % 2]))
                    dve.sem_inc(prob_ready, 1)

                def rotate(t):
                    cos = cst[:, CST["cos"]][:, 32 * t:32 * t + 32].unsqueeze(1).broadcast_to([P, 8, 32])
                    sin = cst[:, CST["sin"]][:, 32 * t:32 * t + 32].unsqueeze(1).broadcast_to([P, 8, 32])
                    x1, x2 = aqk[:, t, :, 0, :], aqk[:, t, :, 1, :]
                    link(mul(rot[:, t, :, 0, :], x1, cos))
                    link(mul(rtmp[:, t], x2, sin))
                    link(tt(rot[:, t, :, 0, :], rot[:, t, :, 0, :], rtmp[:, t], ALU.subtract))
                    link(mul(rot[:, t, :, 1, :], x2, cos))
                    link(mul(rtmp[:, t], x1, sin))
                    link(add(rot[:, t, :, 1, :], rot[:, t, :, 1, :], rtmp[:, t]))

                def convolve(c):
                    for i in range(4):
                        w = colp[:, 3 + 4 * c + i:4 + 4 * c + i]
                        if i == 0:
                            link(dve.tensor_scalar(convout[:, c, :], convin[:, c, 0:T], w, None, ALU.mult))
                        else:
                            link(dve.scalar_tensor_tensor(convout[:, c, :], convin[:, c, i:i + T], w,
                                                          convout[:, c, :], ALU.mult, ALU.add))

                def at_arg_of(h):
                    am = C("att_add")
                    dve.wait_ge(score_done, H + h + 1)
                    e, r, bank = E[h % 2], rm[:, h % 2, :], ps[4 + h % 2]
                    link(dve.tensor_tensor_reduce(e[:, 0:P], bank[:, 0:P], am[:, 0:P], -(DH ** -0.5), 3.0e38,
                                                  ALU.add, ALU.min, r[:, 0:1]))
                    link(dve.tensor_tensor_reduce(e[:, P:SCORE], bank[:, P:SCORE], am[:, P:SCORE],
                                                  -(DH ** -0.5), 3.0e38, ALU.add, ALU.min, r[:, 1:2]))
                    dve.sem_inc(score_read, 1)
                    dve.sem_inc(at_arg, 1)

                def at_weights(h):
                    dve.wait_ge(at_exp, h + 1)
                    if h >= 2:
                        dve.wait_ge(at_tr, h - 1)
                    p, e, mm = Pm[h % 2], E[h % 2], C("att_mul")
                    for t, s in ((0, slice(0, P)), (1, slice(P, SCORE))):
                        link(dve.tensor_tensor_reduce(p[:, s], e[:, s], mm[:, s], 1.0, 0.0, ALU.mult, ALU.add,
                                                      aden[:, t, h:h + 1]))
                    dve.sem_inc(at_prob, 1)

                def mean_square(o, src, sq, scale):
                    link(mul(sq, src, src))
                    link(dve.tensor_reduce(o.unsqueeze(3), heads(sq), AX, ALU.add))
                    link(dve.tensor_scalar(o, o, scale, EPS, ALU.mult, ALU.add))

                def row(name):
                    return rowp[:, ROW[name]].unsqueeze(1).broadcast_to([P, NT, 256])

                dve.wait_ge(rows_loaded, 16)
                yml, ysm, yat, ygl = (ACCv[:, :, 256 * i:256 * (i + 1)] for i in range(4))
                dve.wait_ge(proj_read, FIRST["att_qk"] + 2)
                ml_arg(0)
                ml_arg(1)
                rotate(0)
                ml_prob(0)
                ml_prob(1)
                rotate(1)
                dve.sem_inc(rope_ready, 1)
                ml_arg(2)
                ml_arg(3)
                ml_prob(2)
                ml_prob(3)
                dve.wait_ge(gla_exp, 1)
                q, k = gqkT[:, 0, :], gqkT[:, 1, :]
                dve.scalar_tensor_tensor(ge[:, 0, :], q, DK ** -0.5, ge[:, 0, :], ALU.mult, ALU.mult)
                mul(ge[:, 1, :], k, ge[:, 1, :])
                dve.scalar_tensor_tensor(ge[:, 2, :], q, DK ** -0.5, ge[:, 2, :], ALU.mult, ALU.mult)
                for j in range(1, NB):
                    k0 = BLK * (j * (j - 1) // 2)
                    ins = mul(kx[:, k0:k0 + BLK * j], k[:, 0:BLK * j], kx[:, k0:k0 + BLK * j])
                link(ins)
                dve.sem_inc(gla_qk, 1)
                dve.wait_ge(proj_read, FIRST["conv"] + 2)
                convolve(0)
                convolve(1)
                at_arg_of(0)
                at_arg_of(1)
                convolve(2)
                at_weights(0)
                at_weights(1)
                convolve(3)
                dve.sem_inc(conv_raw, 1)
                at_arg_of(2)
                at_arg_of(3)
                at_weights(2)
                at_weights(3)
                dve.wait_ge(sxt_done, 1)
                link(dve.tensor_copy(sx, ps[2].rearrange("p (t c) -> p t c", t=NT)))
                link(mul(heads(xdt), heads(sx), over(RC[:, :, 96:96 + H], DH)))
                dve.sem_inc(sx_ready, 1)
                link(mul(heads(sx), heads(sx), rowp[:, ROW["ssm_d"]].unsqueeze(1).unsqueeze(3)
                         .broadcast_to([P, NT, H, DH])))
                dve.wait_ge(gla_sc, 1)
                for j in range(NB):
                    jj, t = j % 4, j // 4
                    col = BLK * j if t == 0 else 2 * P + BLK * jj
                    r = slice(BLK * jj, BLK * (jj + 1))
                    mul(PT[r, :, col:col + BLK], psA[r, :, col:col + BLK],
                        cst[r, CST["tri"]].unsqueeze(1).broadcast_to([BLK, H, BLK]))
                    if jj > 0:
                        dve.tensor_copy(PT[0:BLK * jj, :, col:col + BLK], psA[0:BLK * jj, :, col:col + BLK])
                link(dve.tensor_copy(PT[:, :, P:2 * P], psA[:, :, P:2 * P]))
                dve.sem_inc(gla_pt, 1)
                ssm_arg(0)
                ssm_arg(1)
                dve.wait_ge(o_done, 1)
                for t in range(NT):
                    o = ps[2 + t][:, 0:H * (DH + 1)].rearrange("p (h d) -> p h d", h=H)
                    den = rden[:, t, :].unsqueeze(2)
                    link(dve.tensor_scalar(den, o[:, :, DH:DH + 1], -1.0, None, ALU.mult))
                    link(tt(den, den, o[:, :, DH:DH + 1], ALU.max))
                    link(tt(rden[:, t, :], rden[:, t, :], enm[:, t, :], ALU.max))
                    link(dve.reciprocal(rden[:, t, :], rden[:, t, :]))
                    link(mul(ACCv[:, t, 0:256].rearrange("p (h d) -> p h d", h=H), o[:, :, 0:DH],
                             den.broadcast_to([P, H, DH])))
                dve.sem_inc(o_read, 1)
                ssm_prob(0)
                ssm_prob(1)
                link(dve.tensor_reduce(st2.unsqueeze(3), heads(yml), AX, ALU.add))
                link(dve.tensor_scalar(st2, st2, 1.0 / DH, None, ALU.mult))
                link(tt(heads(yml), heads(yml), over(st2, DH), ALU.subtract))
                mean_square(st1, yml, tmp, 1.0 / DH)
                ssm_arg(2)
                ssm_arg(3)
                ssm_prob(2)
                ssm_prob(3)
                dve.sem_inc(rms_in, 1)
                dve.wait_ge(gates_ready, 1)
                link(mul(yml, yml, row("ml_norm")))
                link(mul(yml, yml, mo))
                dve.wait_ge(rms_out, 1)
                link(dve.reciprocal(st1, st1))
                link(mul(heads(yml), heads(yml), over(st1, DH)))
                dve.sem_inc(y_ready, 1)
                dve.wait_ge(o_done, 2)
                link(dve.tensor_copy(ygl, ps[0].rearrange("p (t c) -> p t c", t=NT)))
                mean_square(st2, ygl, tmp, 1.0 / DH)
                dve.sem_inc(rms_in, 1)
                link(mul(ygl, ygl, row("gla_norm")))
                link(mul(ygl, ygl, gr))
                dve.wait_ge(rms_out, 2)
                link(dve.reciprocal(st2, st2))
                link(mul(heads(ygl), heads(ygl), over(st2, DH)))
                dve.sem_inc(y_ready, 1)
                dve.wait_ge(o_done, 3)
                link(dve.reciprocal(aden, aden))
                link(mul(heads(yat), ps[1].rearrange("p (t h d) -> p t h d", t=NT, h=H), over(aden, DH)))
                dve.sem_inc(y_ready, 1)
                dve.wait_ge(o_done, 4)
                link(add(ysm, sx, ps[2].rearrange("p (t c) -> p t c", t=NT)))
                link(mul(ysm, ysm, sz))
                link(mul(tmp, ysm, ysm))
                link(dve.memset(st3, 1.0))
                link(dve.tensor_reduce(st3[:, :, 0:1], tmp, AX, ALU.add))
                link(dve.tensor_scalar(st3, st3, 1.0 / 256, EPS, ALU.mult, ALU.add))
                dve.sem_inc(rms_in, 1)
                dve.sem_inc(mixers_done, 1)
                link(mul(ysm, ysm, row("ssm_norm")))
                dve.wait_ge(rms_out, 3)
                link(dve.reciprocal(st3, st3))
                link(mul(ysm, ysm, st3[:, :, 0:1].broadcast_to([P, NT, 256])))
                dve.sem_inc(y_ready, 1)
                for t in range(NT):
                    for n in range(2):
                        dve.wait_ge(op_done, 2 * t + n + 1)
                        xs = Xv[:, t, n * 512:(n + 1) * 512]
                        link(dve.scalar_tensor_tensor(xs, xs, ALPHA, ps[4 + 2 * t + n], ALU.mult, ALU.add))
                    layer_norm(t, Xv, "ln1_g", "ln1_b", 4 + t)
                    dve.sem_inc(x1_ready, 1)
                xt_half(4)
                dve.wait_ge(x_hi, 1)
                link(tt(ACCv, Xv, X3[0], ALU.subtract))
                dve.wait_ge(score_sig, 1)
                rb = rowp[:, ROW["router_bias"]].unsqueeze(1).broadcast_to([P, NT, EXPERTS])
                link(add(selm, SC, rb))
                for t in range(NT):
                    for g in range(GROUPS):
                        ins = dve.max(m8[:, t, g, :], selm[:, t, 8 * g:8 * g + 8])
                link(ins)
                link(add(grp.unsqueeze(3), m8[:, :, :, 0:1], m8[:, :, :, 1:2]))
                theirs = grp.unsqueeze(2).broadcast_to([P, NT, GROUPS, GROUPS])
                mine = grp.unsqueeze(3).broadcast_to([P, NT, GROUPS, GROUPS])
                link(tt(cmp1, theirs, mine, ALU.is_gt))
                link(tt(cmp2, theirs, mine, ALU.is_equal))
                earlier = C("earlier").rearrange("p (a b) -> p a b", a=GROUPS).unsqueeze(1)\
                    .broadcast_to([P, NT, GROUPS, GROUPS])
                link(mul(cmp2, cmp2, earlier))
                link(add(cmp1, cmp1, cmp2))
                link(dve.tensor_reduce(gmask.unsqueeze(3), cmp1, AX, ALU.add))
                link(dve.tensor_scalar(gmask, gmask, float(GROUPS // 2), None, ALU.is_lt))
                gm = over(gmask, 8)
                s4 = selm.rearrange("p t (g e) -> p t g e", g=GROUPS)
                link(mul(s4, s4, gm))
                link(dve.tensor_scalar(gmask, gmask, -1.0, 1.0e30, ALU.add, ALU.mult))
                link(add(s4, s4, gm))
                for t in range(NT):
                    link(dve.max(t8[:, t, :], selm[:, t, :]))
                    link(dve.match_replace(selr[:, t, :], t8[:, t, :], selm[:, t, :], -3.0e38))
                link(dve.tensor_scalar(Mk, selr, -2.0e38, None, ALU.is_lt))
                dve.sem_inc(mask_ready, 1)
                link(mul(G, SC, Mk))
                link(dve.tensor_reduce(gs.unsqueeze(2), G, AX, ALU.add))
                link(dve.reciprocal(gs, gs))
                link(dve.tensor_scalar(gs, gs, 2.5, None, ALU.mult))
                link(mul(G, G, gs.unsqueeze(2).broadcast_to([P, NT, EXPERTS])))
                dve.wait_ge(rank_done, 1)
                rk = ps[3][:, 0:NT * EXPERTS].rearrange("p (t e) -> p t e", t=NT)
                link(dve.scalar_tensor_tensor(rank, rk, 1.0, Mk, ALU.add, ALU.mult))
                link(dve.tensor_scalar(rank, rank, -1.0, None, ALU.add))
                link(dve.tensor_reduce(cnt[:, 0:1], ps[3][:, 2 * EXPERTS:3 * EXPERTS], AX, ALU.max))
                link(dve.memset(cnt[:, 1:2], 1.0))
                for r in range(1, ROUNDS):
                    link(dve.scalar_tensor_tensor(cnt[:, 1:2], cnt[:, 0:1], float(CAP * r), cnt[:, 1:2],
                                                  ALU.is_gt, ALU.add))
                link(dve.tensor_scalar(last_pair2[:, :], cnt[:, 1:2], float(PAIRS // 2), -1.0, ALU.mult, ALU.add))
                dve.sem_inc(rounds_ready, 1)
                link(dve.memset(Gs, 0.0))
                link(dve.tensor_copy(ident16, ident))
                link(dve.tensor_copy(Gs[:, :, :, 0:1], G.unsqueeze(3)))
                link(tt(G.unsqueeze(3), G.unsqueeze(3), Gs[:, :, :, 0:1], ALU.subtract))
                link(dve.tensor_copy(Gs[:, :, :, 1:2], G.unsqueeze(3)))
                link(tt(Gs[:, :, :, 2:3], G.unsqueeze(3), Gs[:, :, :, 1:2], ALU.subtract))
                for t in range(NT):
                    dve.wait_ge(sh_silu, t + 1)
                    mul(shh[:, t, :], shh[:, t, :], ps[4 + t][:, F:2 * F]).then_inc(sh_hid, 1)
                dve.sem_inc(x_rest, 1)
                dve.wait_ge(x_mid, 1)
                tt(X3[2], ACCv, X3[1], ALU.subtract).then_inc(x_split, 1)
                dve.wait_ge(x_split, 1)
                for t in range(NT):
                    for n in range(2):
                        dve.wait_ge(sho_done, 2 * t + n + 1)
                        s = slice(n * 512, (n + 1) * 512)
                        dve.scalar_tensor_tensor(ACCv[:, t, s], Xv[:, t, s], ALPHA, ps[4 + 2 * t + n],
                                                 ALU.mult, ALU.add).then_inc(acc_done, 1)

                slot = C("slot").unsqueeze(1).unsqueeze(1).broadcast_to([P, NT, 2, CAP])

                def selection(g, b):
                    e0 = (g % PAIRS) * 2
                    mine = rank[:, :, bass.ds(e0, 2)]
                    tt(Sel[b], slot, over(mine, CAP), ALU.is_equal).then_inc(sel_ready, 1)
                    dve.tensor_copy(Gp[b], Gs[:, :, bass.ds(e0, 2), :]).then_inc(selg_ready, 1)
                    dve.wait_ge(sel_ready, g + 1)
                    dve.tensor_scalar(mine, mine, -float(CAP), None, ALU.add).then_inc(rank_next, 1)
                    dve.wait_ge(rank_next, g + 1)

                def map_columns(g, b):
                    dve.wait_ge(st_tr, g + 1)
                    dve.tensor_copy(SelT[b], selT_ps)
                    for e in range(2):
                        r = slice(CAP * e, CAP * (e + 1))
                        ins = dve.tensor_reduce(gslot[r, :], gate_ps[r, 4 * e:4 * e + 4], AX, ALU.add)
                    ins.then_inc(st_done, 1)

                def gathered_half(g):
                    dve.wait_ge(gathered, 2 * g + 2)
                    dve.tensor_copy(XG[:, 4:8, :], ps[2].rearrange("p (k s) -> p k s", k=4)).then_inc(xg_dve, 1)

                def add_rows(g):
                    for t in range(NT):
                        for n in range(2):
                            q = 2 * t + n
                            dve.wait_ge(sc_done, 4 * g + q + 1)
                            dve.wait_ge(acc_done, 4 * g + q + ACC0 - 3)
                            a = ACCv[:, t, n * 512:(n + 1) * 512]
                            add(a, a, ps[5 + q % 2]).then_inc(acc_done, 1)

                last = dve.value_load(last_pair2[0:1, 0:1], min_val=PAIRS // 2 - 1, max_val=ROUNDS * PAIRS // 2 - 1)
                pairs2 = last + 1
                dve.sem_inc(h_done, 1)
                dve.wait_ge(sh_hid, 2)
                dve.wait_ge(sht_done, 1)
                link(dve.memset(SelT[1], 0.0))
                link(dve.memset(Y3, 0.0))
                dve.sem_inc(ys_lo, 2)
                dve.sem_inc(st_done, 1)
                selection(0, 0)
                selection(1, 1)
                gathered_half(0)
                map_columns(0, 0)
                with dve.Fori(0, pairs2) as j:
                    for b in range(2):
                        g = 2 * j + b
                        dve.wait_ge(silu_done, g + 1)
                        dve.wait_ge(ht_tr, g + 1)
                        dve.wait_ge(st_done, g + 2)
                        dve.scalar_tensor_tensor(Hh, HS, gslot, ps[0][:, F:2 * F], ALU.mult, ALU.mult)\
                           .then_inc(h_done, 1)
                        gathered_half(g + 1)
                        add_rows(g)
                        map_columns(g + 1, 1 - b)
                        selection(g + 2, b)
                        for n, s in enumerate((slice(0, 512), slice(512, D))):
                            dve.wait_ge(ys_hi, 2 * g + n + 1)
                            tt(YR[:, s], ps[3 + n], Y3[:, 0, s], ALU.subtract).then_inc(ys_rest, 1)
                        for n, s in enumerate((slice(0, 512), slice(512, D))):
                            dve.wait_ge(ys_mid, 2 * g + n + 1)
                            tt(Y3[:, 2, s], YR[:, s], Y3[:, 1, s], ALU.subtract).then_inc(ys_lo, 1)
                add_rows(2 * pairs2)
                dve.wait_ge(acc_done, 8 * pairs2 + 4 + ACC0)
                for t in range(NT):
                    layer_norm(t, ACCv, "ln2_g", "ln2_b", 6 + t)
                dve.reg_add(before_dp, before_dp, pairs2)
                dve.sem_inc(layer_done, 1)
                dve.wait_ge(layer_open, l + 1)


IN_AT = {"mlstm_qk": (0,), "conv": (1288,), "gla_qk": (2572,), "mlstm_vo": (512,), "gla_vr": (2828,),
         "att_qk": (1804,)}


def constants():
    import numpy as np
    c = np.zeros((P, CSTS), np.float32)
    i = np.arange(P)
    c[:, CST["ident"]] = np.eye(P)
    c[:, CST["before"]] = i[:, None] < i[None, :]
    c[:, CST["ones"]] = 1.0
    causal = np.where(i[:, None] <= i[None, :], 0.0, -1.0e30)
    c[:, CST["causal"]] = np.concatenate([causal, np.zeros((P, P)), causal], 1)
    t, s = np.arange(T)[:, None], np.arange(T)[None, :]
    n = ((t >= s) & (t - s <= 128)).astype(np.float32)
    for window, dilation in ((512, 4), (2048, 16)):
        n += (t >= s) & ((t - s) % dilation == 0) & ((t - s) // dilation <= window // dilation)
    n = np.concatenate([n[:P, :P], n[P:, :]], 1)
    c[:, CST["att_mul"]] = n
    c[:, CST["att_add"]] = np.where(n > 0, 0.0, -1.0e30)
    inv = np.float32(10000.0) ** (-np.arange(32, dtype=np.float32) / np.float32(32))
    ang = np.arange(T, dtype=np.float32)[:, None] * inv.astype(np.float32)
    for name, f in (("cos", np.cos), ("sin", np.sin)):
        c[:, CST[name]] = f(ang).astype(np.float32).reshape(NT, P, 32).transpose(1, 0, 2).reshape(P, -1)
    c[:, CST["slot"]] = np.arange(CAP)
    for r in (0, 64):
        for h in range(H):
            c[r + h, CST["head"].start + h * P:CST["head"].start + (h + 1) * P] = 1.0
    c[:, CST["tri"]] = (i % BLK)[:, None] <= np.arange(BLK)[None, :]
    g = np.arange(GROUPS)
    c[:, CST["earlier"]] = (g[None, :] < g[:, None]).reshape(1, -1)
    return c


def layout(w):
    import numpy as np
    w = {k: np.asarray(v) for k, v in w.items()}
    win = w["w_in"].reshape(DEPTH, P, KD, -1)
    small = np.zeros((DEPTH, P, KD, P), np.float32)
    small[..., 0:H] = win[..., 1024:1028]
    small[..., 32:32 + H] = win[..., 1028:1032]
    small[..., 64:64 + H] = win[..., 1800:1804]
    small[..., 96:112] = win[..., 3340:3356]
    parts = [small]
    for name, n, _ in GROUPS_IN[1:]:
        if name == "att_v_ssm_z":
            parts.append(np.concatenate([win[..., 2316:2572], win[..., 1032:1288]], -1))
        else:
            parts.append(win[..., IN_AT[name][0]:IN_AT[name][0] + n])
    w_in = np.concatenate([p.reshape(DEPTH, P, -1) for p in parts], -1)
    rows = np.concatenate([w["ln1_g"], w["ln1_b"], w["ln2_g"], w["ln2_b"], w["ml_norm_w"], w["ssm_norm_w"],
                           w["gla_norm_w"], w["ssm_d"], w["router_bias"]], -1)
    cols = np.zeros((DEPTH, P, COLS), np.float32)
    cols[:, 0:H, 0] = w["ml_i_bias"]
    cols[:, 32:32 + H, 0] = w["ml_f_bias"]
    cols[:, 64:64 + H, 0] = w["ssm_dt_bias"]
    cols[:, 64:64 + H, 1] = w["ssm_a_log"]
    cols[:, :, 2] = w["gla_gate_b"]
    cols[:, :, COL["taps"]] = w["ssm_conv_w"].reshape(DEPTH, 4, 4, P).transpose(0, 3, 2, 1).reshape(DEPTH, P, 16)
    cols[:, :, COL["conv_b"]] = w["ssm_conv_b"].reshape(DEPTH, 4, P).transpose(0, 2, 1)
    cols[:, 96:112, COL["gate_w2"]] = w["gla_gate_w2"]
    return {"x": w["x"][0], "w_in": w_in, "cols": cols, "rows": rows, "cst": constants(), "w_out": w["w_out"],
            "router_w": w["router_w"], "exp_w_gate": w["exp_w_gate"], "exp_w_up": w["exp_w_up"],
            "exp_w_down": w["exp_w_down"], "sh_w_gate": w["sh_w_gate"], "sh_w_up": w["sh_w_up"],
            "sh_w_down": w["sh_w_down"]}


def build(nc, arrays, **more):
    import numpy as np
    a = {}
    for name, v in arrays.items():
        a[name] = nc.dram_tensor(f"in_{name}", v.shape, mybir.dt.from_np(v.dtype), kind="ExternalInput").ap()
    out = nc.dram_tensor("out_0", (T, D), F32, kind="ExternalOutput").ap()
    hybrid_kernel(nc, a["x"], a["w_in"], a["cols"], a["rows"], a["cst"], a["w_out"], a["router_w"],
                  a["exp_w_gate"].rearrange("l (g e) (p k) f -> l g p e k f", e=2, k=KD),
                  a["exp_w_up"].rearrange("l (g e) (p k) f -> l g p e k f", e=2, k=KD),
                  a["exp_w_down"].rearrange("l (g e) (p k) d -> l g p e k d", e=2, k=2),
                  a["sh_w_gate"], a["sh_w_up"], a["sh_w_down"], out, **more)


def kernel(**inputs):
    import numpy as np
    from concourse import bacc
    from concourse.bass_utils import run_bass_kernel_spmd

    arrays = {k: np.ascontiguousarray(v) for k, v in layout(inputs).items()}
    nc = bacc.Bacc("TRN2", target_bir_lowering=False, num_devices=1)
    build(nc, arrays)
    r = run_bass_kernel_spmd(nc, [{f"in_{k}": v for k, v in arrays.items()}], core_ids=[0])
    return r.results[0]["out_0"].reshape(1, T, D)
```

```python
from contextlib import ExitStack

import concourse.bass as bass
from concourse import mybir

F32 = mybir.dt.float32
I32 = mybir.dt.int32
BF16 = mybir.dt.bfloat16
ALU = mybir.AluOpType
ACT = mybir.ActivationFunctionType
AX = mybir.AxisListType.X

P = 128
T = 256
NT = T // P
D = 1024
KD = D // P
DEPTH = 2
H = 4
DH = 64
DK = 32
EXPERTS = 64
PAIRS = EXPERTS // 2
TOP_K = 8
GROUPS = 8
F = 256
CAP = 64
ROUNDS = T // CAP
ALPHA = (2 * DEPTH) ** 0.25
EPS = 1e-5
TAU = 16.0
BLK = 32
NB = T // BLK
SCORE = 3 * P
CLAMP = 80.0

GROUPS_IN = [
    ("small", P, True), ("mlstm_qk", 512, True), ("gla_qk", 256, True), ("att_qk", 512, False),
    ("conv", 512, True), ("gla_vr", 512, False), ("mlstm_vo", 512, False), ("att_v_ssm_z", 512, False),
]
UNITS = [max(g[1] // 256, 1) for g in GROUPS_IN]
FIRST = {g[0]: sum(UNITS[:i]) for i, g in enumerate(GROUPS_IN)}
YORDER = (0, 3, 2, 1)

ROW = {}
_at = 0
for _name, _n in (("ln1_g", D), ("ln1_b", D), ("ln2_g", D), ("ln2_b", D), ("ml_norm", 256), ("ssm_norm", 256),
                  ("gla_norm", 256), ("ssm_d", H), ("router_bias", EXPERTS)):
    ROW[_name] = slice(_at, _at + _n)
    _at += _n
ROWS = _at
COL = {"bias": slice(0, 1), "a_log": slice(1, 2), "gla_b": slice(2, 3), "taps": slice(3, 19),
       "conv_b": slice(19, 23), "gate_w2": slice(23, 151)}
COLS = 151
CST = {}
_at = 0
for _name, _n in (("ident", P), ("before", P), ("ones", T), ("causal", SCORE), ("att_add", SCORE),
                  ("att_mul", SCORE), ("cos", NT * 32), ("sin", NT * 32), ("slot", CAP), ("head", H * P),
                  ("tri", BLK), ("earlier", GROUPS * GROUPS)):
    CST[_name] = slice(_at, _at + _n)
    _at += _n
CSTS = _at


def hybrid_kernel(nc, x_in, w_in, cols_in, rows_in, cst_in, w_out, router_w, e_gate, e_up, e_down,
                  sh_gate, sh_up, sh_down, out, debug=None, layers=DEPTH):
    with ExitStack() as ctx:
        def sb(name, n, dt=F32):
            return ctx.enter_context(nc.sbuf_tensor(name, [P, n], dt))

        def sem(name):
            return ctx.enter_context(nc.semaphore(name))

        wbuf = sb("wbuf", 24576)
        stage = sb("stage", 8192)
        X = sb("X", NT * D)
        XT = sb("XT", KD * T)
        ACC = sb("ACC", NT * D)
        rowp = sb("rowp", ROWS)
        colp = sb("colp", COLS)
        cst = sb("cst", CSTS)
        misc = sb("misc", 5632)
        last_pair2 = sb("last_pair2", 1, I32)

        def view(t, at, *dims):
            n = 1
            for d in dims:
                n *= d
            ap = t[:, at:at + n]
            if len(dims) == 1:
                return ap
            names = "abcd"[:len(dims)]
            return ap.rearrange("p (" + " ".join(names) + ") -> p " + " ".join(names),
                                **{c: d for c, d in zip(names, dims)})

        Xv = view(X, 0, NT, D)
        XT3 = view(XT, 0, KD, T)
        ACCv = view(ACC, 0, NT, D)
        wgu = [view(wbuf, 8192 * b, 2, 2, KD, F) for b in range(2)]
        wdn = [view(wbuf, 16384 + 4096 * b, 2, 2, D) for b in range(2)]

        pos = [8192]

        def scr(*dims):
            n = 1
            for d in dims:
                n *= d
            at = pos[0]
            pos[0] += n
            assert pos[0] <= 24576
            return view(wbuf, at, *dims)

        mqkT = scr(4, T)
        mvx = scr(NT, H, DH + 1)
        mo = scr(NT, 256)
        convin = scr(4, T + 3)
        convout = scr(4, T)
        gqkT = scr(2, T)
        gv = scr(NT, 256)
        gr = scr(NT, 256)
        aqk = scr(NT, 8, 2, 32)
        rtmp = scr(NT, 8, 32)
        pss = view(wbuf, pos[0] - 1536, H, SCORE)
        rot = view(ACC, 0, NT, 8, 2, 32)
        kx = view(ACC, 1024, 28 * BLK)
        aqkT = scr(4, T)
        av = scr(NT, 256)
        sz = scr(NT, 256)
        sx = scr(NT, 256)
        xdt = scr(NT, 256)
        gdec = scr(T)
        gb = scr(T)
        gd1 = scr(T)
        gd2 = scr(T)
        gl = scr(T)
        ge = scr(3, T)
        PT = scr(H, SCORE)
        PTa = scr(H, SCORE)
        mpos = [0]

        def mscr(*dims):
            n = 1
            for d in dims:
                n *= d
            at = mpos[0]
            mpos[0] += n
            assert mpos[0] <= 5632, mpos
            return view(misc, at, *dims)

        z = mscr(T)
        lt = mscr(T)
        lsg = mscr(T)
        lsp = mscr(T)
        R = mscr(T)
        C0 = mscr(T)
        MR = mscr(T)
        RC = mscr(NT, P)
        nac = mscr(NT, H)
        enm = mscr(NT, H)
        acol = mscr(1)
        rm = mscr(2, 2)
        rden = mscr(NT, H)
        aden = mscr(NT, H)
        st1 = mscr(NT, H)
        st2 = mscr(NT, H)
        st3 = mscr(NT, H)
        E = [mscr(SCORE) for _ in range(2)]
        Pm = [mscr(SCORE) for _ in range(2)]
        pml = mscr(H, SCORE)
        tmp = view(misc, 0, NT, 256)
        mpos[0] = 0
        def mscr16(*dims):
            n = 1
            for d in dims:
                n *= d
            ap = mscr(n // 2).bitcast(BF16)
            names = "abcd"[:len(dims)]
            return ap if len(dims) == 1 else ap.rearrange(
                "p (" + " ".join(names) + ") -> p " + " ".join(names), **{c: d for c, d in zip(names, dims)})

        Sel = [mscr16(NT, 2, CAP) for _ in range(2)]
        SelT = [mscr16(T) for _ in range(2)]
        Gp = [mscr16(NT, 2, 4) for _ in range(2)]
        gslot = mscr(4)[:, 0:1]
        XG = mscr(KD, 2 * CAP)
        HS = mscr(F)
        Hh = mscr(F)
        HT = mscr(2, 2 * CAP)
        Y3 = mscr16(3, D)
        YR = mscr(D)
        G = mscr(NT, EXPERTS)
        rank = mscr(NT, EXPERTS)
        SC = mscr(NT, EXPERTS)
        Gs = mscr16(NT, EXPERTS, 4)
        ident16 = mscr16(P)
        X3 = [stage[:, 2048 + D * i:2048 + D * (i + 1)].bitcast(BF16).rearrange("p (t d) -> p t d", t=NT)
              for i in range(3)]
        r0 = 512
        selm = view(misc, r0, NT, EXPERTS)
        selr = view(misc, r0 + 128, NT, EXPERTS)
        m8 = view(misc, r0 + 256, NT, GROUPS, 8)
        grp = view(misc, r0 + 384, NT, GROUPS)
        cmp1 = view(misc, r0 + 400, NT, GROUPS, GROUPS)
        cmp2 = view(misc, r0 + 528, NT, GROUPS, GROUPS)
        gmask = view(misc, r0 + 656, NT, GROUPS)
        t8 = view(misc, r0 + 672, NT, 8)
        Mk = view(misc, r0 + 688, NT, EXPERTS)
        gs = view(misc, r0 + 816, NT)
        cnt = view(misc, r0 + 818, 2)
        shh = view(misc, 3872, NT, F)
        lnb = sb("lnb", 64)
        bst = view(lnb, 0, NT, 2, 6)
        bag = view(lnb, 24, NT, 2)
        rstd = view(lnb, 28, NT)
        spare = view(lnb, 30, 1)

        def C(name):
            return cst[:, CST[name]]

        ident = C("ident")
        before = C("before")
        ones = C("ones")
        sh_w = view(wbuf, 16384, 2, KD, F)
        sh_d = view(stage, 0, 2, D)
        rw = view(stage, 6144, KD, EXPERTS)
        wo = view(stage, 0, KD, D)
        shT = view(stage, 6656, 2, T)

        ps = [ctx.enter_context(nc.psum_tensor(f"ps{i}", [P, 512], F32)) for i in range(4)]
        psA = ctx.enter_context(nc.psum_tensor("psA", [P, 4, 512], F32))
        ps = [t[:, :] for t in ps] + [psA[:, i, :] for i in range(4)]

        ident_loaded = sem("ident_loaded")
        x_loaded = [sem(f"x_loaded{t}") for t in range(NT)]
        cst_loaded = sem("cst_loaded")
        cols_loaded = sem("cols_loaded")
        in_loaded = [sem(f"in_loaded{b}") for b in range(2)]
        gu_loaded = [[sem(f"gu_loaded{b}{h}") for h in range(2)] for b in range(2)]
        dn_loaded = [sem(f"dn_loaded{b}") for b in range(2)]
        gu_used = [[sem(f"gu_used{b}{h}") for h in range(2)] for b in range(2)]
        dn_used = [sem(f"dn_used{b}") for b in range(2)]
        in_experts = sem("in_experts")
        layer_done = sem("layer_done")
        layer_open = sem("layer_open")
        out_stored = sem("out_stored")
        sp_held = sem("sp_held")
        pool_held = sem("pool_held")
        cleared = []
        cleared_early = []

        def lsem(name):
            s = sem(name)
            cleared.append(s)
            return s

        def msem(name):
            s = sem(name)
            cleared_early.append(s)
            return s

        rows_loaded = msem("rows_loaded")
        wo_loaded = [msem(f"wo_loaded{b}") for b in range(2)]
        router_loaded = msem("router_loaded")
        shared_loaded = msem("shared_loaded")
        shared_down_loaded = msem("shared_down_loaded")
        mixers_done = msem("mixers_done")
        proj_done = msem("proj_done")
        proj_read = msem("proj_read")
        xt_done = msem("xt_done")
        xt_read = msem("xt_read")
        gate_rows = msem("gate_rows")
        gla_gate = msem("gla_gate")
        logs_ready = msem("logs_ready")
        gla_logs = msem("gla_logs")
        rows_ready = msem("rows_ready")
        cols_done = msem("cols_done")
        cols_ready = msem("cols_ready")
        conv_raw = msem("conv_raw")
        conv_ready = msem("conv_ready")
        sxt_done = msem("sxt_done")
        sx_ready = msem("sx_ready")
        rope_ready = msem("rope_ready")
        qkt_done = msem("qkt_done")
        qkt_read = msem("qkt_read")
        score_done = msem("score_done")
        score_read = msem("score_read")
        bc_done = msem("bc_done")
        bc_read = msem("bc_read")
        arg_ready = msem("arg_ready")
        exp_ready = msem("exp_ready")
        prob_ready = msem("prob_ready")
        at_arg = msem("at_arg")
        at_exp = msem("at_exp")
        at_prob = msem("at_prob")
        at_tr = msem("at_tr")
        at_trc = msem("at_trc")
        o_done = msem("o_done")
        o_read = msem("o_read")
        gla_arg = msem("gla_arg")
        gla_exp = msem("gla_exp")
        gla_qk = msem("gla_qk")
        gla_sc = msem("gla_sc")
        gla_pt = msem("gla_pt")
        rms_in = lsem("rms_in")
        rms_out = lsem("rms_out")
        gates_ready = msem("gates_ready")
        y_ready = msem("y_ready")
        yt_done = msem("yt_done")
        yt_read = msem("yt_read")
        wo_used = msem("wo_used")
        op_done = msem("op_done")
        x1_ready = msem("x1_ready")
        rt_done = msem("rt_done")
        score_sig = msem("score_sig")
        mask_ready = msem("mask_ready")
        rank_done = msem("rank_done")
        rounds_ready = msem("rounds_ready")
        sh_done = msem("sh_done")
        sh_silu = msem("sh_silu")
        sh_hid = msem("sh_hid")
        sht_done = msem("sht_done")
        sht_read = msem("sht_read")
        sho_done = msem("sho_done")
        dve_own = lsem("dve_own")
        act_own = lsem("act_own")
        sel_ready = lsem("sel_ready")
        selg_ready = lsem("selg_ready")
        rank_next = lsem("rank_next")
        gathered = lsem("gathered")
        xg_act = lsem("xg_act")
        xg_dve = lsem("xg_dve")
        silu_done = lsem("silu_done")
        h_done = lsem("h_done")
        ht_tr = lsem("ht_tr")
        ht_done = lsem("ht_done")
        st_tr = lsem("st_tr")
        st_done = lsem("st_done")
        dn_half = lsem("dn_half")
        ys_hi = lsem("ys_hi")
        ys_rest = lsem("ys_rest")
        ys_mid = lsem("ys_mid")
        ys_lo = lsem("ys_lo")
        x_hi = msem("x_hi")
        x_rest = msem("x_rest")
        x_mid = msem("x_mid")
        x_split = msem("x_split")
        sc_done = lsem("sc_done")
        acc_done = lsem("acc_done")

        selT_ps = ps[7][:, T:T + P].bitcast(BF16)
        gate_ps = ps[7][:, 3 * P:3 * P + 8]
        SHARED_BANK = (4, 5, 6, 3)
        SCATTER_BANK = (5, 6, 0, 5)
        ACC0 = 8
        block = ctx.enter_context(nc.Block())

        def head_rows(h):
            return slice(DH * (h % 2), DH * (h % 2) + DH)

        @block.sync
        def _(sp):
            sp.dma_start(ident, cst_in[:, CST["ident"]]).then_inc(ident_loaded, 16)
            for t in range(NT):
                sp.dma_start(Xv[:, t, :], x_in[t * P:(t + 1) * P]).then_inc(x_loaded[t], 16)
            before_dp = sp.alloc_register("sp_before")
            sp.reg_mov(before_dp, 0)


            def load_in(l, gi):
                at = KD * sum(g[1] for g in GROUPS_IN[:gi])
                n = KD * GROUPS_IN[gi][1]
                b = gi % 2
                if gi == 0:
                    sp.dma_start(colp[:, :], cols_in[l]).then_inc(cols_loaded, 16)
                sp.dma_start(stage[:, 4096 * b:4096 * b + n], w_in[l][:, at:at + n]).then_inc(in_loaded[b], 16)

            def load_gate_up(l, base, j, b, halves=(0, 1)):
                for h in halves:
                    k = slice(KD // 2 * h, KD // 2 * (h + 1))
                    sp.wait_ge(gu_used[b][h], base + j + 1)
                    sp.sem_inc(sp_held, 1)
                    sp.dma_start(wgu[b][:, :, 0, k, :], e_gate[l][(j * 2 + b) % PAIRS][:, :, k, :])\
                      .then_inc(gu_loaded[b][h], 16)
                    sp.dma_start(wgu[b][:, :, 1, k, :], e_up[l][(j * 2 + b) % PAIRS][:, :, k, :])\
                      .then_inc(gu_loaded[b][h], 16)

            load_in(0, 0)
            load_in(0, 1)
            sp.dma_start(cst[:, P:CSTS], cst_in[:, P:CSTS]).then_inc(cst_loaded, 16)
            with sp.Fori(0, layers) as l:
                base = sp.snap(before_dp)
                for gi in range(1, len(GROUPS_IN)):
                    if gi >= 2:
                        sp.wait_ge(proj_done, sum(UNITS[:gi - 1]))
                        load_in(l, gi)
                    if gi == 2:
                        sp.dma_start(rowp[:, :], rows_in[l].partition_broadcast(P)).then_inc(rows_loaded, 16)
                    if gi in (4, 5):
                        load_gate_up(l, base, 0, 0, halves=(gi - 4,))
                for b in range(2):
                    sp.wait_ge(proj_done, sum(UNITS[:len(UNITS) - 1 + b]))
                    sp.dma_start(wo[:, 4 * b:4 * b + 4, :], w_out[l][512 * b:512 * b + 512]
                                 .rearrange("(k p) d -> p k d", p=P)).then_inc(wo_loaded[b], 16)
                sp.wait_ge(mixers_done, 1)
                sp.dma_start(sh_w[:, 0], sh_gate[l].rearrange("(p k) f -> p k f", k=KD)).then_inc(shared_loaded, 16)
                sp.dma_start(sh_w[:, 1], sh_up[l].rearrange("(p k) f -> p k f", k=KD)).then_inc(shared_loaded, 16)
                load_gate_up(l, base, 0, 1)
                sp.wait_ge(wo_used, 2)
                sp.dma_start(rw, router_w[l].rearrange("(p k) e -> p k e", k=KD)).then_inc(router_loaded, 16)
                sp.dma_start(sh_d, sh_down[l].rearrange("(p k) d -> p k d", k=2)).then_inc(shared_down_loaded, 16)

                def load_down(j, b):
                    sp.wait_ge(dn_used[b], base + j + 1)
                    sp.sem_inc(sp_held, 1)
                    sp.dma_start(wdn[b], e_down[l][(j * 2 + b) % PAIRS]).then_inc(dn_loaded[b], 16)

                load_down(0, 1)
                sp.wait_ge(sh_done, 2)
                load_down(0, 0)
                sp.wait_ge(rounds_ready, 1)
                last = sp.value_load(last_pair2[0:1, 0:1], min_val=PAIRS // 2 - 1, max_val=ROUNDS * PAIRS // 2 - 1)
                pairs2 = last + 1
                sp.sem_inc(in_experts, 1)
                with sp.Fori(0, last) as j:
                    for b in range(2):
                        load_gate_up(l, base, j + 1, b)
                        load_down(j + 1, b)
                sp.wait_ge(dn_used[1], base + last + 2)
                sp.sem_inc(sp_held, 1)
                for gi in range(2):
                    load_in((l + 1) % DEPTH, gi)
                sp.reg_add(before_dp, before_dp, pairs2)
                sp.sem_inc(layer_done, 1)
                sp.wait_ge(layer_open, l + 1)
                sp.sem_inc(sp_held, 1)
            sp.wait_ge(cols_loaded, 16 * (layers + 1))
            for b in range(2):
                sp.wait_ge(in_loaded[b], 16 * (layers * len(GROUPS_IN) // 2 + 1))
            sp.dma_start(out.rearrange("(t p) d -> p t d", p=P), Xv).then_inc(out_stored, 16)
            sp.wait_ge(out_stored, 16)

        @block.gpsimd
        def _(pool):
            with pool.Fori(0, layers) as l:
                pool.wait_ge(in_experts, 4 * (l + 1))
                pool.sem_inc(pool_held, 1)
                for s in cleared_early:
                    pool.sem_clear(s)
                pool.wait_ge(layer_done, 4 * (l + 1))
                pool.sem_inc(pool_held, 1)
                for s in cleared:
                    pool.sem_clear(s)
                pool.sem_inc(layer_open, 1)

        @block.tensor
        def _(pe):
            before_dp = pe.alloc_register("pe_before")
            pe.reg_mov(before_dp, 0)
            for b in range(2):
                for h in range(2):
                    pe.sem_inc(gu_used[b][h], 1)
                pe.sem_inc(dn_used[b], 1)
            pe.wait_ge(ident_loaded, 16)

            def transpose_x(u, n0=0):
                xs = Xv.rearrange("p t (q k) -> p t k q", k=KD)
                if u >= 2:
                    pe.wait_ge(xt_read, n0 + u - 1)
                for kk in range(4):
                    mm = pe.transpose(ps[u % 2][:, kk * P:(kk + 1) * P], xs[:, u // 2, 4 * (u % 2) + kk, :], ident)
                mm.then_inc(xt_done, 1)

            def transposed_scores(bank, keys, queries):
                pe.matmul(bank[:, 0:T], keys[:, 0:P], queries[:, 0:T], start=True, stop=True)
                return pe.matmul(bank[:, T:T + P], keys[:, P:T], queries[:, P:T], start=True, stop=True)

            def apply(out0, out1, p, values):
                pe.matmul(out0, p[:, 0:P], values(0), start=True, stop=True)
                pe.matmul(out1, p[:, P:2 * P], values(0), start=True, stop=False)
                return pe.matmul(out1, p[:, 2 * P:3 * P], values(1), start=False, stop=True)

            def head_row(bank, rows, h):
                r = slice(rows.start, rows.start + H)
                src = MR if rows.start == 0 else R
                pe.matmul(bank[:, 0:T], cst[r, CST["head"]][:, h * P:(h + 1) * P], src[r, :],
                          start=True, stop=True).then_inc(bc_done, 1)

            def gla_gate_rows():
                pe.wait_ge(gate_rows, 1)
                pe.matmul(ps[2][:, 0:T], colp[96:112, COL["gate_w2"]], z[96:112, :],
                          start=True, stop=True).then_inc(gla_gate, 1)

            def gate_columns():
                pe.wait_ge(rows_ready, 1)
                for t in range(NT):
                    mm = pe.transpose(ps[3][:, t * P:(t + 1) * P], R[:, t * P:(t + 1) * P], ident)
                mm.then_inc(cols_done, 1)

            def ml_scores(h):
                if h == 0:
                    pe.wait_ge(proj_read, FIRST["mlstm_qk"] + 2)
                    pe.wait_ge(cols_ready, 2)
                    pe.wait_ge(cst_loaded, 16)
                else:
                    pe.wait_ge(score_read, max(h - 1, 0))
                    pe.wait_ge(bc_read, max(h - 1, 0))
                r = head_rows(h)
                transposed_scores(ps[4 + h % 2], mqkT[r, 2 + h // 2, :], mqkT[r, h // 2, :]).then_inc(score_done, 1)
                head_row(ps[2 + h % 2], slice(0, H), h)

            def rotated_columns():
                pe.wait_ge(rope_ready, 1)
                rf = rot.rearrange("p t h s e -> p t (h s e)")
                for c in range(4):
                    for t in range(NT):
                        mm = pe.transpose(ps[6 + c // 2][:, (c % 2) * T + t * P:(c % 2) * T + (t + 1) * P],
                                          rf[:, t, c * P:(c + 1) * P], ident)
                mm.then_inc(qkt_done, 1)

            def at_scores(h):
                pe.wait_ge(score_read, H + h - 1)
                if h == 0:
                    pe.wait_ge(qkt_read, 1)
                r = head_rows(h)
                q, k = aqkT[r, h // 2, :], aqkT[r, 2 + h // 2, :]
                bank = ps[4 + h % 2]
                pe.matmul(bank[:, 0:P], q[:, 0:P], k[:, 0:P], start=True, stop=True)
                pe.matmul(bank[:, P:SCORE], q[:, P:T], k, start=True, stop=True).then_inc(score_done, 1)

            def at_transposes(h):
                pe.wait_ge(at_prob, h + 1)
                if h >= 2:
                    pe.wait_ge(at_trc, h - 1)
                for i in range(3):
                    mm = pe.transpose(ps[6 + h % 2][:, i * P:(i + 1) * P], Pm[h % 2][:, i * P:(i + 1) * P], ident)
                mm.then_inc(at_tr, 1)

            def ssm_columns():
                pe.wait_ge(conv_ready, 1)
                pe.wait_ge(bc_read, H)
                for t in range(NT):
                    for c in range(2):
                        mm = pe.transpose(ps[2][:, t * 256 + c * P:t * 256 + (c + 1) * P],
                                          convout[:, c, t * P:(t + 1) * P], ident)
                mm.then_inc(sxt_done, 1)

            def gla_scores():
                pe.wait_ge(score_read, 2 * H)
                pe.wait_ge(at_trc, H)
                pe.wait_ge(gla_qk, 1)
                for j in range(NB):
                    js = slice(BLK * j, BLK * (j + 1))
                    jj, t = j % 4, j // 4
                    col = BLK * j if t == 0 else 2 * P + BLK * jj
                    k0 = BLK * (j * (j - 1) // 2)
                    for h in range(H):
                        r = slice(DK * h, DK * (h + 1))
                        mm = pe.matmul(psA[BLK * jj:BLK * (jj + 1), h, col:col + BLK], ge[r, 1, js], ge[r, 0, js],
                                       start=True, stop=True)
                        if t == 0 and j > 0:
                            mm = pe.matmul(psA[0:BLK * j, h, col:col + BLK], kx[r, k0:k0 + BLK * j], ge[r, 2, js],
                                           start=True, stop=True)
                        if t == 1:
                            mm = pe.matmul(psA[:, h, BLK * j:BLK * j + BLK], kx[r, k0:k0 + P], ge[r, 2, js],
                                           start=True, stop=True)
                            if jj > 0:
                                mm = pe.matmul(psA[0:BLK * jj, h, col:col + BLK],
                                               kx[r, k0 + P:k0 + P + BLK * jj], ge[r, 2, js], start=True, stop=True)
                mm.then_inc(gla_sc, 1)

            def ssm_maps():
                pe.wait_ge(gla_pt, 1)
                for g in range(2):
                    r = slice(64 * g, 64 * g + 64)
                    mm = transposed_scores(ps[6 + g], convout[r, 2, :], convout[r, 3, :])
                mm.then_inc(score_done, 1)

            def ssm_decay(h):
                if h >= 2:
                    pe.wait_ge(bc_read, H + h - 1)
                head_row(ps[4 + h % 2], slice(64, 64 + H), h)

            def ml_apply():
                pe.wait_ge(proj_read, FIRST["mlstm_vo"] + 2)
                pe.wait_ge(sx_ready, 1)
                pe.wait_ge(prob_ready, H)
                for h in range(H):
                    c = h * (DH + 1)
                    mm = apply(ps[2][:, c:c + DH + 1], ps[3][:, c:c + DH + 1], pml[:, h, :], lambda t: mvx[:, t, h, :])
                mm.then_inc(o_done, 1)

            def rows_of(bank, maps, values):
                for h in range(H):
                    mm = apply(bank[:, h * DH:(h + 1) * DH], bank[:, 256 + h * DH:256 + (h + 1) * DH], maps[:, h, :],
                               lambda t: values[:, t, h * DH:(h + 1) * DH])
                mm.then_inc(o_done, 1)

            BETWEEN = {
                2: [gla_gate_rows],
                3: [gate_columns],
                5: [lambda: ml_scores(0), lambda: ml_scores(1)],
                6: [lambda: ml_scores(2), lambda: ml_scores(3)],
                7: [rotated_columns],
                8: [lambda: at_scores(0), lambda: at_scores(1)],
                9: [lambda: at_transposes(0), lambda: at_transposes(1), lambda: at_scores(2), lambda: at_scores(3)],
                10: [lambda: at_transposes(2), lambda: at_transposes(3), ssm_columns],
                11: [gla_scores],
                12: [ssm_maps, lambda: ssm_decay(0), lambda: ssm_decay(1), ml_apply],
                13: [lambda: ssm_decay(2), lambda: ssm_decay(3)],
            }

            with pe.Fori(0, layers) as l:
                base = pe.snap(before_dp)
                for u in range(4):
                    pe.wait_ge(x_loaded[u // 2], 16)
                    transpose_x(u)
                pe.wait_ge(xt_read, 4)
                u = 0
                count = [0, 0]
                for gi, (name, n, chan) in enumerate(GROUPS_IN):
                    b = gi % 2
                    count[b] += 16
                    pe.wait_ge(in_loaded[b], l * (8 * len(GROUPS_IN)) + count[b])
                    w = view(stage, 4096 * b, KD, n)
                    for h in range(UNITS[gi]):
                        if u >= 2:
                            pe.wait_ge(proj_read, u - 1)
                        bank = ps[u % 2]
                        if chan:
                            for m in range(min(2, n // P)):
                                for k in range(KD):
                                    c = (2 * h + m) * P
                                    mm = pe.matmul(bank[:, m * T:(m + 1) * T], w[:, k, c:c + P], XT3[:, k, :],
                                                   start=(k == 0), stop=(k == KD - 1))
                        else:
                            for k in range(KD):
                                mm = pe.matmul(bank, XT3[:, k, h * P:(h + 1) * P], w[:, k, :],
                                               start=(k == 0), stop=(k == KD - 1))
                        mm.then_inc(proj_done, 1)
                        for step in BETWEEN.get(u, []):
                            step()
                        u += 1
                pe.wait_ge(proj_read, 14)
                rows_of(ps[0], PT, gv)
                pe.wait_ge(at_trc, H)
                rows_of(ps[1], PTa, av)
                pe.wait_ge(prob_ready, 2 * H)
                pe.wait_ge(o_read, 1)
                rows_of(ps[2], pss, xdt)
                def y_columns(i):
                    pe.wait_ge(y_ready, i + 1)
                    for kk in range(2):
                        k = 2 * YORDER[i] + kk
                        for t in range(NT):
                            mm = pe.transpose(ps[(3, 0, 1, 2)[i]][:, kk * T + t * P:kk * T + (t + 1) * P],
                                              ACCv[:, t, k * P:(k + 1) * P], ident)
                    mm.then_inc(yt_done, 1)

                y_columns(0)
                for i, m in enumerate(YORDER):
                    pe.wait_ge(yt_read, i + 1)
                    pe.wait_ge(wo_loaded[m // 2], 16)
                    for t in range(NT):
                        for n in range(2):
                            for k in range(2 * m, 2 * m + 2):
                                mm = pe.matmul(ps[4 + 2 * t + n], XT3[:, k, t * P:(t + 1) * P],
                                               wo[:, k, n * 512:(n + 1) * 512], start=(i == 0 and k == 2 * m),
                                               stop=(i == 3 and k == 2 * m + 1))
                            if i == 3:
                                mm.then_inc(op_done, 1)
                        if t == 0 and i < 3:
                            y_columns(i + 1)
                    if i < 3:
                        mm.then_inc(wo_used, 1)

                def shared_gate_up(t):
                    for k in range(KD):
                        if k % 4 == 0:
                            pe.wait_ge(xt_read, 4 + 2 * t + k // 4 + 1)
                        mm = pe.matmul(ps[4 + t], XT3[:, k, t * P:(t + 1) * P], sh_w[:, :, k, :],
                                       start=(k == 0), stop=(k == KD - 1))
                    mm.then_inc(sh_done, 1)

                def shared_down(q):
                    t, n = q // 2, q % 2
                    for k in range(2):
                        mm = pe.matmul(ps[SHARED_BANK[q]], shT[:, k, t * P:(t + 1) * P],
                                       sh_d[:, k, n * 512:(n + 1) * 512], start=(k == 0), stop=(k == 1))
                    mm.then_inc(sho_done, 1)

                pe.wait_ge(x1_ready, 1)
                transpose_x(0, 4)
                transpose_x(1, 4)
                pe.wait_ge(shared_loaded, 32)
                shared_gate_up(0)
                pe.wait_ge(x1_ready, 2)
                transpose_x(2, 4)
                transpose_x(3, 4)
                pe.wait_ge(router_loaded, 16)
                for t in range(NT):
                    pe.wait_ge(xt_read, 6 + 2 * t)
                    for k in range(KD):
                        mm = pe.matmul(ps[2][:, t * EXPERTS:(t + 1) * EXPERTS], XT3[:, k, t * P:(t + 1) * P],
                                       rw[:, k, :], start=(k == 0), stop=(k == KD - 1))
                mm.then_inc(rt_done, 1)
                shared_gate_up(1)
                pe.wait_ge(mask_ready, 1)
                pe.matmul(ps[3][:, 0:EXPERTS], before, Mk[:, 0, :], start=True, stop=True)
                pe.matmul(ps[3][:, EXPERTS:2 * EXPERTS], ones[:, 0:P], Mk[:, 0, :], start=True, stop=False)
                pe.matmul(ps[3][:, EXPERTS:2 * EXPERTS], before, Mk[:, 1, :], start=False, stop=True)
                pe.matmul(ps[3][:, 2 * EXPERTS:3 * EXPERTS], ones[:, 0:P], Mk[:, 0, :], start=True, stop=False)
                pe.matmul(ps[3][:, 2 * EXPERTS:3 * EXPERTS], ones[:, 0:P], Mk[:, 1, :],
                          start=False, stop=True).then_inc(rank_done, 1)
                pe.wait_ge(sh_hid, 2)
                for t in range(NT):
                    for k in range(2):
                        mm = pe.transpose(ps[7][:, k * T + t * P:k * T + (t + 1) * P],
                                          shh[:, t, :].rearrange("p (f k) -> p k f", k=2)[:, k, :], ident)
                mm.then_inc(sht_done, 1)
                pe.wait_ge(sht_read, 1)
                pe.wait_ge(shared_down_loaded, 16)
                for q in range(2):
                    shared_down(q)

                xs = [x.rearrange("p t (q k) -> p t k q", k=KD) for x in X3]

                def gather(g, b):
                    pe.wait_ge(sel_ready, g + 1)
                    for q in range(2):
                        for k in range(4 * q, 4 * q + 4):
                            for i in range(3 * NT):
                                mm = pe.matmul(ps[1 + q][:, (k % 4) * P:(k % 4 + 1) * P], xs[i // NT][:, i % NT, k, :],
                                               Sel[b][:, i % NT, :, :], start=(i == 0), stop=(i == 3 * NT - 1))
                        mm.then_inc(gathered, 1)

                def scatter(g, b, hidden):
                    for n in range(2):
                        pe.wait_ge(ys_lo, 2 * g + n + 1)
                        for t in range(NT):
                            q = 2 * n + t
                            if SCATTER_BANK[q] == 0:
                                pe.wait_ge(h_done, hidden)
                            else:
                                pe.wait_ge(acc_done, 4 * g + (q - 1 if q < 2 else q - 2) + ACC0 - 4)
                            for i in range(3):
                                mm = pe.matmul(ps[SCATTER_BANK[q]], SelT[1 - b][:, t * P:(t + 1) * P],
                                               Y3[:, i, n * 512:(n + 1) * 512], start=(i == 0), stop=(i == 2))
                            mm.then_inc(sc_done, 1)

                def transposed_map(g, b):
                    pe.wait_ge(selg_ready, g + 1)
                    for t in range(NT):
                        pe.transpose(selT_ps[:, t * P:(t + 1) * P], Sel[b][:, t, :, :], ident16)
                    for t in range(NT):
                        mm = pe.matmul(gate_ps, Sel[b][:, t, :, :], Gp[b][:, t, :, :],
                                       start=(t == 0), stop=(t == NT - 1))
                    mm.then_inc(st_tr, 1)

                pe.wait_ge(rounds_ready, 1)
                last = pe.value_load(last_pair2[0:1, 0:1], min_val=PAIRS // 2 - 1, max_val=ROUNDS * PAIRS // 2 - 1)
                pairs2 = last + 1
                pe.sem_inc(ht_tr, 1)
                pe.sem_inc(sc_done, 4)
                pe.wait_ge(x_split, 2)
                shared_down(2)
                gather(0, 0)
                transposed_map(0, 0)
                shared_down(3)

                def pair(j, b, first=False, final=False, opening=False):
                    g = 2 * j + b
                    pe.wait_ge(xg_act, g + 1)
                    pe.wait_ge(xg_dve, g + 1)
                    pe.wait_ge(h_done, g + 1)
                    if not opening:
                        pe.wait_ge(acc_done, 4 * g + 3 + ACC0 - 8)
                    for h in range(2):
                        pe.wait_ge(gu_loaded[b][h], (base + j + 1) * 32)
                        for k in range(KD // 2 * h, KD // 2 * (h + 1)):
                            for e in range(2):
                                mm = pe.matmul(ps[0][64 * e:64 * e + CAP, :],
                                               XG[:, k, CAP * e:CAP * (e + 1)], wgu[b][:, e, :, k, :],
                                               start=(k == 0), stop=(k == KD - 1))
                        mm.then_inc(gu_used[b][h], 1)
                    if final:
                        scatter(g, b, g + 2)
                    else:
                        gather(g + 1, 1 - b)
                    pe.wait_ge(h_done, g + 2)
                    pe.wait_ge(ht_done, g + 1)
                    pe.wait_ge(st_done, g + 1)
                    for k in range(2):
                        mm = pe.transpose(ps[7][:, k * P:(k + 1) * P],
                                          Hh.rearrange("p (f k) -> p k f", k=2)[:, k, :], ident)
                    mm.then_inc(ht_tr, 1)
                    if not (first or final):
                        scatter(g, b, g + 2)
                    pe.wait_ge(ht_done, g + 2)
                    if not final:
                        transposed_map(g + 1, 1 - b)
                    pe.wait_ge(dn_loaded[b], (base + j + 1) * 16)
                    if first:
                        pe.wait_ge(acc_done, ACC0)
                    for n in range(2):
                        for k in range(2):
                            for e in range(2):
                                mm = pe.matmul(ps[3 + n][64 * e:64 * e + CAP, :], HT[:, k, CAP * e:CAP * (e + 1)],
                                               wdn[b][:, e, k, n * 512:(n + 1) * 512],
                                               start=(k == 0), stop=(k == 1))
                        mm.then_inc(dn_half if n == 0 else dn_used[b], 1)

                pe.sem_inc(in_experts, 1)
                pair(0, 0, first=True, opening=True)
                pair(0, 1, opening=True)
                with pe.Fori(1, last) as j:
                    for b in range(2):
                        pair(j, b)
                pair(last, 0)
                pair(last, 1, final=True)
                scatter(2 * pairs2, 0, 2 * pairs2 + 1)
                pe.reg_add(before_dp, before_dp, pairs2)
                pe.sem_inc(layer_done, 1)
                pe.wait_ge(layer_open, l + 1)

        @block.scalar
        def _(act):
            own = [0]

            def link(ins):
                own[0] += 1
                ins.then_inc(act_own, 1)
                act.wait_ge(act_own, own[0])

            def copy(o, i):
                return act.activation(o, i, ACT.Copy)

            before_dp = act.alloc_register("act_before")
            act.reg_mov(before_dp, 0)
            with act.Fori(0, layers) as l:
                own[0] = 0
                base = act.snap(before_dp)
                def xt_half(n0):
                    for t in range(NT):
                        act.wait_ge(xt_done, n0 + 2 * t + 1)
                        if n0 + t:
                            act.wait_ge(xt_read, n0 + 2 * t)
                        copy(XT3[:, 0:4, t * P:(t + 1) * P],
                             ps[0].rearrange("p (k t) -> p k t", k=4)).then_inc(xt_read, 1)

                xt_half(0)
                act.wait_ge(cols_loaded, (l + 1) * 16)
                act.wait_ge(proj_done, 1)
                link(act.activation(z, ps[0][:, 0:T], ACT.Identity, bias=colp[:, COL["bias"]]))
                act.sem_inc(proj_read, 1)
                act.sem_inc(gate_rows, 1)

                def log1p_exp(o, i):
                    link(act.activation(o, i, ACT.Abs))
                    link(act.activation(o, o, ACT.Exp, scale=-1.0))
                    link(act.activation(o, o, ACT.Ln, bias=1.0))

                log1p_exp(lt, z)
                link(act.activation(acol[64:64 + H, :], colp[64:64 + H, COL["a_log"]], ACT.Exp))
                act.sem_inc(logs_ready, 1)

                def unit(u, *moves):
                    act.wait_ge(proj_done, u + 1)
                    for o, c in moves:
                        n = o.ndim
                        src = ps[u % 2][:, c]
                        if n == 3:
                            src = src.rearrange("p (m t) -> p m t", m=o.shape[1])
                        ins = copy(o, src)
                    ins.then_inc(proj_read, 1)

                def decay(n, bias):
                    act.wait_ge(arg_ready, n + 1)
                    e = E[n % 2]
                    act.activation(e[:, 0:T], e[:, 0:T], ACT.Exp, bias=bias(0))
                    act.activation(e[:, T:SCORE], e[:, T:SCORE], ACT.Exp, bias=bias(1)).then_inc(exp_ready, 1)

                def ml_exp(h):
                    decay(h, lambda t: RC[:, t, h:h + 1])

                def ssm_exp(h):
                    decay(H + h, lambda t: nac[:, t, h:h + 1])

                def at_exp_of(h):
                    act.wait_ge(at_arg, h + 1)
                    e = E[h % 2]
                    act.activation(e[:, 0:P], e[:, 0:P], ACT.Exp, scale=-1.0, bias=rm[:, h % 2, 0:1])
                    act.activation(e[:, P:SCORE], e[:, P:SCORE], ACT.Exp, scale=-1.0,
                                   bias=rm[:, h % 2, 1:2]).then_inc(at_exp, 1)

                def at_copy(h):
                    act.wait_ge(at_tr, h + 1)
                    copy(PTa[:, h, :], ps[6 + h % 2][:, 0:SCORE]).then_inc(at_trc, 1)

                both = slice(0, 512)
                for i in range(2):
                    unit(FIRST["mlstm_qk"] + i, (mqkT[:, 2 * i:2 * i + 2, :], both))
                act.wait_ge(gla_gate, 1)
                link(act.activation(gdec, ps[2][:, 0:T], ACT.Identity, bias=colp[:, COL["gla_b"]]))
                log1p_exp(gl, gdec)
                act.sem_inc(gla_logs, 1)
                unit(FIRST["gla_qk"], (gqkT, both))
                act.wait_ge(cols_done, 1)
                link(act.activation(enm, ps[3].rearrange("p (t c) -> p t c", c=P)[:, 0:NT, 32:32 + H], ACT.Exp, scale=-1.0))
                act.sem_inc(cols_ready, 1)
                for t in range(NT):
                    unit(FIRST["att_qk"] + t, (aqk[:, t].rearrange("p h s e -> p (h s e)"), both))
                act.wait_ge(gla_arg, 1)
                act.activation(ge[:, 0, :], gd1, ACT.Exp)
                act.activation(ge[:, 1, :], gd1, ACT.Exp, scale=-1.0)
                act.activation(ge[:, 2, :], gd2, ACT.Exp)
                for j in range(1, NB):
                    k0 = BLK * (j * (j - 1) // 2)
                    ins = act.activation(kx[:, k0:k0 + BLK * j], gb[:, 0:BLK * j], ACT.Exp, scale=-1.0,
                                         bias=gb[:, BLK * j - 1:BLK * j])
                ins.then_inc(gla_exp, 1)
                act.wait_ge(cols_ready, 2)
                ml_exp(0)
                ml_exp(1)
                unit(FIRST["conv"], (convin[:, 0:2, 3:T + 3], both))
                ml_exp(2)
                ml_exp(3)
                unit(FIRST["conv"] + 1, (convin[:, 2:4, 3:T + 3], both))
                act.wait_ge(qkt_done, 1)
                for c in range(2):
                    ins = copy(aqkT[:, 2 * c:2 * c + 2, :], ps[6 + c].rearrange("p (m t) -> p m t", m=2))
                ins.then_inc(qkt_read, 1)
                halves = slice(0, 256), slice(256, 512)
                unit(8, (gv[:, 0, :], halves[0]), (gr[:, 0, :], halves[1]))
                at_exp_of(0)
                at_exp_of(1)
                unit(9, (gv[:, 1, :], halves[0]), (gr[:, 1, :], halves[1]))
                act.wait_ge(conv_raw, 1)
                for c in range(4):
                    ins = act.activation(convout[:, c, :], convout[:, c, :], ACT.Silu, bias=colp[:, 19 + c:20 + c])
                ins.then_inc(conv_ready, 1)
                at_copy(0)
                at_copy(1)
                at_exp_of(2)
                at_exp_of(3)
                act.wait_ge(dve_own, 1)
                unit(10, (mvx[:, 0, :, 0:DH], halves[0]), (mo[:, 0, :], halves[1]))
                at_copy(2)
                at_copy(3)
                unit(11, (mvx[:, 1, :, 0:DH], halves[0]), (mo[:, 1, :], halves[1]))
                unit(12, (av[:, 0, :], halves[0]), (sz[:, 0, :], halves[1]))
                ssm_exp(0)
                ssm_exp(1)
                unit(13, (av[:, 1, :], halves[0]), (sz[:, 1, :], halves[1]))
                ssm_exp(2)
                ssm_exp(3)
                link(act.activation(mo, mo, ACT.Sigmoid))
                act.sem_inc(gates_ready, 1)

                def head_root(n, root):
                    act.wait_ge(rms_in, n)
                    act.activation(root, root, ACT.Sqrt).then_inc(rms_out, 1)

                head_root(1, st1)
                link(act.activation(gr, gr, ACT.Silu))
                link(act.activation(sz, sz, ACT.Silu))
                act.sem_inc(gates_ready, 1)
                for i, m in enumerate(YORDER):
                    if i == 1:
                        head_root(2, st2)
                    elif i == 3:
                        head_root(3, st3)
                    act.wait_ge(yt_done, i + 1)
                    copy(XT3[:, 2 * m:2 * m + 2, :],
                         ps[(3, 0, 1, 2)[i]].rearrange("p (k t) -> p k t", k=2)).then_inc(yt_read, 1)
                def root(t):
                    act.wait_ge(rms_in, 4 + t)
                    act.activation(rstd[:, t:t + 1], rstd[:, t:t + 1], ACT.Sqrt).then_inc(rms_out, 1)

                def xt_unit(u):
                    act.wait_ge(xt_done, 4 + u + 1)
                    copy(XT3[:, 4 * (u % 2):4 * (u % 2) + 4, (u // 2) * P:(u // 2 + 1) * P],
                         ps[u % 2].rearrange("p (k t) -> p k t", k=4)).then_inc(xt_read, 1)

                def gate_of(t):
                    act.wait_ge(sh_done, t + 1)
                    act.activation(shh[:, t, :], ps[4 + t][:, 0:F], ACT.Sigmoid).then_inc(sh_silu, 1)

                root(0)
                xt_unit(0)
                xt_unit(1)
                act.wait_ge(op_done, 4)
                copy(X3[0][:, 0, :], Xv[:, 0, :]).then_inc(x_hi, 1)
                root(1)
                act.wait_ge(x1_ready, 2)
                copy(X3[0][:, 1, :], Xv[:, 1, :]).then_inc(x_hi, 1)
                for t in range(NT):
                    act.wait_ge(x_rest, t + 1)
                    copy(X3[1][:, t, :], ACCv[:, t, :]).then_inc(x_mid, 1)
                xt_unit(2)
                gate_of(0)
                act.wait_ge(rt_done, 1)
                act.activation(SC, ps[2][:, 0:NT * EXPERTS].rearrange("p (t e) -> p t e", t=NT),
                               ACT.Sigmoid).then_inc(score_sig, 1)
                gate_of(1)
                act.wait_ge(sht_done, 1)
                copy(shT, ps[7].rearrange("p (k t) -> p k t", k=2)).then_inc(sht_read, 1)
                act.wait_ge(rounds_ready, 1)
                last = act.value_load(last_pair2[0:1, 0:1], min_val=PAIRS // 2 - 1, max_val=ROUNDS * PAIRS // 2 - 1)
                pairs2 = last + 1

                def gathered_half(g):
                    act.wait_ge(gathered, 2 * g + 1)
                    copy(XG[:, 0:4, :], ps[1].rearrange("p (k s) -> p k s", k=4)).then_inc(xg_act, 1)

                act.wait_ge(cst_loaded, 16)
                act.activation(spare, ones[:, 0:1], ACT.Silu)
                act.sem_inc(ht_done, 1)
                gathered_half(0)

                def pair(j, b, first=False, final=False):
                    g = 2 * j + b
                    act.wait_ge(gu_used[b][1], base + j + 2)
                    act.wait_ge(h_done, g + 1)
                    act.activation(HS, ps[0][:, 0:F], ACT.Silu).then_inc(silu_done, 1)
                    if not final:
                        gathered_half(g + 1)
                    act.wait_ge(ht_tr, g + 2)
                    copy(HT, ps[7][:, 0:T].rearrange("p (k s) -> p k s", k=2)).then_inc(ht_done, 1)
                    if not first:
                        act.wait_ge(sc_done, 4 * g + 4)
                    for n, s in enumerate((slice(0, 512), slice(512, D))):
                        if n == 0:
                            act.wait_ge(dn_half, g + 1)
                        else:
                            act.wait_ge(dn_used[b], base + j + 2)
                        copy(Y3[:, 0, s], ps[3 + n]).then_inc(ys_hi, 1)
                        act.wait_ge(ys_rest, 2 * g + n + 1)
                        copy(Y3[:, 1, s], YR[:, s]).then_inc(ys_mid, 1)

                act.sem_inc(in_experts, 1)
                pair(0, 0, first=True)
                pair(0, 1)
                with act.Fori(1, last) as j:
                    for b in range(2):
                        pair(j, b)
                pair(last, 0)
                pair(last, 1, final=True)
                act.activation(spare, ones[:, 0:1], ACT.Sqrt)
                for t in range(NT):
                    act.wait_ge(rms_in, 6 + t)
                    act.activation(rstd[:, t:t + 1], rstd[:, t:t + 1], ACT.Sqrt).then_inc(rms_out, 1)
                act.reg_add(before_dp, before_dp, pairs2)
                act.sem_inc(layer_done, 1)
                act.wait_ge(layer_open, l + 1)

        @block.vector
        def _(dve):
            own = [0]

            def link(ins):
                own[0] += 1
                ins.then_inc(dve_own, 1)
                dve.wait_ge(dve_own, own[0])

            def tt(o, a, b, op):
                return dve.tensor_tensor(o, a, b, op)

            def mul(o, a, b):
                return tt(o, a, b, ALU.mult)

            def add(o, a, b):
                return tt(o, a, b, ALU.add)

            def heads(ap):
                return ap.rearrange("p t (h d) -> p t h d", h=H)

            def over(ap, n):
                return ap.unsqueeze(3).broadcast_to([P, ap.shape[1], ap.shape[2], n])

            def half_stats(t, h, src):
                link(dve.bn_stats(bst[:, t, h, :], src[:, t, h * 512:(h + 1) * 512]))

            def layer_norm(t, src, g, b, n):
                link(dve.bn_aggr(bag[:, t, :], bst[:, t, :, :].rearrange("p n s -> p (n s)")))
                link(dve.tensor_scalar(rstd[:, t:t + 1], bag[:, t, 1:2], EPS, None, ALU.add))
                dve.sem_inc(rms_in, 1)
                link(dve.scalar_tensor_tensor(src[:, t, :], src[:, t, :], bag[:, t, 0:1], rowp[:, ROW[g]],
                                              ALU.subtract, ALU.mult))
                dve.wait_ge(rms_out, n)
                link(dve.reciprocal(rstd[:, t:t + 1], rstd[:, t:t + 1]))
                link(dve.scalar_tensor_tensor(Xv[:, t, :], src[:, t, :], rstd[:, t:t + 1], rowp[:, ROW[b]],
                                              ALU.mult, ALU.add))

            before_dp = dve.alloc_register("dve_before")
            dve.reg_mov(before_dp, 0)
            with dve.Fori(0, layers) as l:
                own[0] = 0
                base = dve.snap(before_dp)
                link(dve.memset(mvx[:, :, :, DH:DH + 1], 1.0))
                link(dve.memset(convin[:, :, 0:3], 0.0))
                link(dve.memset(R, 0.0))

                def xt_half(n0):
                    for t in range(NT):
                        dve.wait_ge(xt_done, n0 + 2 * t + 2)
                        dve.wait_ge(xt_read, n0 + 2 * t + 1)
                        dve.tensor_copy(XT3[:, 4:8, t * P:(t + 1) * P],
                                        ps[1].rearrange("p (k t) -> p k t", k=4)).then_inc(xt_read, 1)

                xt_half(0)
                link(dve.memset(PT, 0.0))
                dve.wait_ge(logs_ready, 1)
                fr, dr = slice(32, 32 + H), slice(64, 64 + H)
                link(dve.scalar_tensor_tensor(lsg[fr], z[fr], 0.0, lt[fr], ALU.min, ALU.subtract))
                link(dve.scalar_tensor_tensor(lsp[dr], z[dr], 0.0, lt[dr], ALU.max, ALU.add))
                link(dve.tensor_copy(R[96:96 + H], lsp[dr]))
                dve.wait_ge(cst_loaded, 16)
                link(dve.tensor_scalar(lsp[dr], lsp[dr], acol[dr], -1.0, ALU.mult, ALU.mult))
                link(dve.tensor_tensor_scan(R[dr], ones[dr], lsp[dr], 0.0, ALU.mult, ALU.add))
                link(dve.tensor_tensor_scan(lsg[fr], ones[fr], lsg[fr], 0.0, ALU.mult, ALU.add))
                link(dve.tensor_copy(C0[0:H], lsg[fr]))
                link(tt(R[0:H], z[0:H], C0[0:H], ALU.subtract))
                link(dve.tensor_tensor_scan(MR[0:H], R[0:H], R[0:H], -3.0e38, ALU.max, ALU.max))
                link(add(C0[0:H], C0[0:H], MR[0:H]))
                link(dve.tensor_copy(R[fr], C0[0:H]))
                dve.sem_inc(rows_ready, 1)
                dve.wait_ge(gla_logs, 1)
                link(dve.scalar_tensor_tensor(gl, gdec, 0.0, gl, ALU.min, ALU.subtract))
                link(dve.tensor_scalar(gl, gl, 1.0 / TAU, None, ALU.mult))
                link(dve.tensor_tensor_scan(gb, ones, gl, 0.0, ALU.mult, ALU.add))
                b3 = gb.rearrange("p (j i) -> p j i", i=BLK)
                link(tt(gd1.rearrange("p (j i) -> p j i", i=BLK), b3,
                        b3[:, :, BLK // 2 - 1:BLK // 2].broadcast_to([P, NB, BLK]), ALU.subtract))
                link(dve.tensor_scalar(gd1, gd1, CLAMP, -CLAMP, ALU.min, ALU.max))
                link(dve.tensor_copy(gd2[:, 0:BLK], gb[:, 0:BLK]))
                link(tt(gd2[:, BLK:T].rearrange("p (j i) -> p j i", i=BLK), b3[:, 1:NB, :],
                        b3[:, 0:NB - 1, BLK - 1:BLK].broadcast_to([P, NB - 1, BLK]), ALU.subtract))
                dve.sem_inc(gla_arg, 1)
                dve.wait_ge(cols_done, 1)
                dve.wait_ge(cols_ready, 1)
                link(dve.tensor_copy(RC, ps[3][:, 0:T].rearrange("p (t c) -> p t c", c=P)))
                link(dve.tensor_scalar(nac, RC[:, :, 64:64 + H], -1.0, None, ALU.mult))
                dve.sem_inc(cols_ready, 1)

                def decay_arg(n, bank, sign):
                    dve.wait_ge(bc_done, n + 1)
                    e = E[n % 2]
                    cm = C("causal")
                    link(tt(e[:, 0:T], cm[:, 0:T], bank[:, 0:T], sign))
                    link(tt(e[:, T:SCORE], cm[:, T:SCORE], bank[:, P:T], sign))
                    dve.sem_inc(bc_read, 1)
                    dve.sem_inc(arg_ready, 1)

                def ml_arg(h):
                    decay_arg(h, ps[2 + h % 2], ALU.subtract)

                def ml_prob(h):
                    dve.wait_ge(exp_ready, h + 1)
                    dve.wait_ge(score_done, h + 1)
                    link(dve.scalar_tensor_tensor(pml[:, h, :], ps[4 + h % 2][:, 0:SCORE], DH ** -0.5, E[h % 2],
                                                  ALU.mult, ALU.mult))
                    dve.sem_inc(score_read, 1)
                    dve.sem_inc(prob_ready, 1)

                def ssm_arg(h):
                    decay_arg(H + h, ps[4 + h % 2], ALU.add)

                def ssm_prob(h):
                    dve.wait_ge(exp_ready, H + h + 1)
                    dve.wait_ge(score_done, 2 * H + 1)
                    link(mul(pss[:, h, :], ps[6 + h // 2][:, 0:SCORE], E[h % 2]))
                    dve.sem_inc(prob_ready, 1)

                def rotate(t):
                    cos = cst[:, CST["cos"]][:, 32 * t:32 * t + 32].unsqueeze(1).broadcast_to([P, 8, 32])
                    sin = cst[:, CST["sin"]][:, 32 * t:32 * t + 32].unsqueeze(1).broadcast_to([P, 8, 32])
                    x1, x2 = aqk[:, t, :, 0, :], aqk[:, t, :, 1, :]
                    link(mul(rot[:, t, :, 0, :], x1, cos))
                    link(mul(rtmp[:, t], x2, sin))
                    link(tt(rot[:, t, :, 0, :], rot[:, t, :, 0, :], rtmp[:, t], ALU.subtract))
                    link(mul(rot[:, t, :, 1, :], x2, cos))
                    link(mul(rtmp[:, t], x1, sin))
                    link(add(rot[:, t, :, 1, :], rot[:, t, :, 1, :], rtmp[:, t]))

                def convolve(c):
                    for i in range(4):
                        w = colp[:, 3 + 4 * c + i:4 + 4 * c + i]
                        if i == 0:
                            link(dve.tensor_scalar(convout[:, c, :], convin[:, c, 0:T], w, None, ALU.mult))
                        else:
                            link(dve.scalar_tensor_tensor(convout[:, c, :], convin[:, c, i:i + T], w,
                                                          convout[:, c, :], ALU.mult, ALU.add))

                def at_arg_of(h):
                    am = C("att_add")
                    dve.wait_ge(score_done, H + h + 1)
                    e, r, bank = E[h % 2], rm[:, h % 2, :], ps[4 + h % 2]
                    link(dve.tensor_tensor_reduce(e[:, 0:P], bank[:, 0:P], am[:, 0:P], -(DH ** -0.5), 3.0e38,
                                                  ALU.add, ALU.min, r[:, 0:1]))
                    link(dve.tensor_tensor_reduce(e[:, P:SCORE], bank[:, P:SCORE], am[:, P:SCORE],
                                                  -(DH ** -0.5), 3.0e38, ALU.add, ALU.min, r[:, 1:2]))
                    dve.sem_inc(score_read, 1)
                    dve.sem_inc(at_arg, 1)

                def at_weights(h):
                    dve.wait_ge(at_exp, h + 1)
                    if h >= 2:
                        dve.wait_ge(at_tr, h - 1)
                    p, e, mm = Pm[h % 2], E[h % 2], C("att_mul")
                    for t, s in ((0, slice(0, P)), (1, slice(P, SCORE))):
                        link(dve.tensor_tensor_reduce(p[:, s], e[:, s], mm[:, s], 1.0, 0.0, ALU.mult, ALU.add,
                                                      aden[:, t, h:h + 1]))
                    dve.sem_inc(at_prob, 1)

                def mean_square(o, src, sq, scale):
                    link(mul(sq, src, src))
                    link(dve.tensor_reduce(o.unsqueeze(3), heads(sq), AX, ALU.add))
                    link(dve.tensor_scalar(o, o, scale, EPS, ALU.mult, ALU.add))

                def row(name):
                    return rowp[:, ROW[name]].unsqueeze(1).broadcast_to([P, NT, 256])

                dve.wait_ge(rows_loaded, 16)
                yml, ysm, yat, ygl = (ACCv[:, :, 256 * i:256 * (i + 1)] for i in range(4))
                dve.wait_ge(proj_read, FIRST["att_qk"] + 2)
                ml_arg(0)
                ml_arg(1)
                rotate(0)
                ml_prob(0)
                ml_prob(1)
                rotate(1)
                dve.sem_inc(rope_ready, 1)
                ml_arg(2)
                ml_arg(3)
                ml_prob(2)
                ml_prob(3)
                dve.wait_ge(gla_exp, 1)
                q, k = gqkT[:, 0, :], gqkT[:, 1, :]
                dve.scalar_tensor_tensor(ge[:, 0, :], q, DK ** -0.5, ge[:, 0, :], ALU.mult, ALU.mult)
                mul(ge[:, 1, :], k, ge[:, 1, :])
                dve.scalar_tensor_tensor(ge[:, 2, :], q, DK ** -0.5, ge[:, 2, :], ALU.mult, ALU.mult)
                for j in range(1, NB):
                    k0 = BLK * (j * (j - 1) // 2)
                    ins = mul(kx[:, k0:k0 + BLK * j], k[:, 0:BLK * j], kx[:, k0:k0 + BLK * j])
                link(ins)
                dve.sem_inc(gla_qk, 1)
                dve.wait_ge(proj_read, FIRST["conv"] + 2)
                convolve(0)
                convolve(1)
                at_arg_of(0)
                at_arg_of(1)
                convolve(2)
                at_weights(0)
                at_weights(1)
                convolve(3)
                dve.sem_inc(conv_raw, 1)
                at_arg_of(2)
                at_arg_of(3)
                at_weights(2)
                at_weights(3)
                dve.wait_ge(sxt_done, 1)
                link(dve.tensor_copy(sx, ps[2].rearrange("p (t c) -> p t c", t=NT)))
                link(mul(heads(xdt), heads(sx), over(RC[:, :, 96:96 + H], DH)))
                dve.sem_inc(sx_ready, 1)
                link(mul(heads(sx), heads(sx), rowp[:, ROW["ssm_d"]].unsqueeze(1).unsqueeze(3)
                         .broadcast_to([P, NT, H, DH])))
                dve.wait_ge(gla_sc, 1)
                for j in range(NB):
                    jj, t = j % 4, j // 4
                    col = BLK * j if t == 0 else 2 * P + BLK * jj
                    r = slice(BLK * jj, BLK * (jj + 1))
                    mul(PT[r, :, col:col + BLK], psA[r, :, col:col + BLK],
                        cst[r, CST["tri"]].unsqueeze(1).broadcast_to([BLK, H, BLK]))
                    if jj > 0:
                        dve.tensor_copy(PT[0:BLK * jj, :, col:col + BLK], psA[0:BLK * jj, :, col:col + BLK])
                link(dve.tensor_copy(PT[:, :, P:2 * P], psA[:, :, P:2 * P]))
                dve.sem_inc(gla_pt, 1)
                ssm_arg(0)
                ssm_arg(1)
                dve.wait_ge(o_done, 1)
                for t in range(NT):
                    o = ps[2 + t][:, 0:H * (DH + 1)].rearrange("p (h d) -> p h d", h=H)
                    den = rden[:, t, :].unsqueeze(2)
                    link(dve.tensor_scalar(den, o[:, :, DH:DH + 1], -1.0, None, ALU.mult))
                    link(tt(den, den, o[:, :, DH:DH + 1], ALU.max))
                    link(tt(rden[:, t, :], rden[:, t, :], enm[:, t, :], ALU.max))
                    link(dve.reciprocal(rden[:, t, :], rden[:, t, :]))
                    link(mul(ACCv[:, t, 0:256].rearrange("p (h d) -> p h d", h=H), o[:, :, 0:DH],
                             den.broadcast_to([P, H, DH])))
                dve.sem_inc(o_read, 1)
                ssm_prob(0)
                ssm_prob(1)
                link(dve.tensor_reduce(st2.unsqueeze(3), heads(yml), AX, ALU.add))
                link(dve.tensor_scalar(st2, st2, 1.0 / DH, None, ALU.mult))
                link(tt(heads(yml), heads(yml), over(st2, DH), ALU.subtract))
                mean_square(st1, yml, tmp, 1.0 / DH)
                ssm_arg(2)
                ssm_arg(3)
                ssm_prob(2)
                ssm_prob(3)
                dve.sem_inc(rms_in, 1)
                link(mul(yml, yml, row("ml_norm")))
                dve.wait_ge(gates_ready, 1)
                link(mul(yml, yml, mo))
                dve.wait_ge(rms_out, 1)
                link(dve.reciprocal(st1, st1))
                link(mul(heads(yml), heads(yml), over(st1, DH)))
                dve.sem_inc(y_ready, 1)
                dve.wait_ge(o_done, 2)
                link(dve.tensor_copy(ygl, ps[0].rearrange("p (t c) -> p t c", t=NT)))
                mean_square(st2, ygl, tmp, 1.0 / DH)
                dve.sem_inc(rms_in, 1)
                link(mul(ygl, ygl, row("gla_norm")))
                dve.wait_ge(gates_ready, 2)
                link(mul(ygl, ygl, gr))
                dve.wait_ge(rms_out, 2)
                link(dve.reciprocal(st2, st2))
                link(mul(heads(ygl), heads(ygl), over(st2, DH)))
                dve.sem_inc(y_ready, 1)
                dve.wait_ge(o_done, 3)
                link(dve.reciprocal(aden, aden))
                link(mul(heads(yat), ps[1].rearrange("p (t h d) -> p t h d", t=NT, h=H), over(aden, DH)))
                dve.sem_inc(y_ready, 1)
                dve.wait_ge(o_done, 4)
                link(add(ysm, sx, ps[2].rearrange("p (t c) -> p t c", t=NT)))
                link(mul(ysm, ysm, sz))
                link(mul(tmp, ysm, ysm))
                link(dve.memset(st3, 1.0))
                link(dve.tensor_reduce(st3[:, :, 0:1], tmp, AX, ALU.add))
                link(dve.tensor_scalar(st3, st3, 1.0 / 256, EPS, ALU.mult, ALU.add))
                dve.sem_inc(rms_in, 1)
                dve.sem_inc(mixers_done, 1)
                link(mul(ysm, ysm, row("ssm_norm")))
                dve.wait_ge(rms_out, 3)
                link(dve.reciprocal(st3, st3))
                link(mul(ysm, ysm, st3[:, :, 0:1].broadcast_to([P, NT, 256])))
                dve.sem_inc(y_ready, 1)
                for t in range(NT):
                    for n in range(2):
                        dve.wait_ge(op_done, 2 * t + n + 1)
                        xs = Xv[:, t, n * 512:(n + 1) * 512]
                        link(dve.scalar_tensor_tensor(xs, xs, ALPHA, ps[4 + 2 * t + n], ALU.mult, ALU.add))
                        half_stats(t, n, Xv)
                    layer_norm(t, Xv, "ln1_g", "ln1_b", 4 + t)
                    dve.sem_inc(x1_ready, 1)
                for t in range(NT):
                    dve.wait_ge(x_hi, t + 1)
                    tt(ACCv[:, t, :], Xv[:, t, :], X3[0][:, t, :], ALU.subtract).then_inc(x_rest, 1)
                link(dve.tensor_copy(ident16, ident))

                def third_part(t):
                    dve.wait_ge(x_mid, t + 1)
                    tt(X3[2][:, t, :], ACCv[:, t, :], X3[1][:, t, :], ALU.subtract).then_inc(x_split, 1)

                third_part(0)
                dve.wait_ge(xt_done, 8)
                dve.wait_ge(xt_read, 7)
                dve.tensor_copy(XT3[:, 4:8, P:T], ps[1].rearrange("p (k t) -> p k t", k=4)).then_inc(xt_read, 1)
                third_part(1)

                def shared_hidden(t):
                    dve.wait_ge(sh_silu, t + 1)
                    link(mul(shh[:, t, :], shh[:, t, :], ps[4 + t][:, 0:F]))
                    mul(shh[:, t, :], shh[:, t, :], ps[4 + t][:, F:2 * F]).then_inc(sh_hid, 1)

                shared_hidden(0)
                dve.wait_ge(score_sig, 1)
                rb = rowp[:, ROW["router_bias"]].unsqueeze(1).broadcast_to([P, NT, EXPERTS])
                link(add(selm, SC, rb))
                for t in range(NT):
                    for g in range(GROUPS):
                        ins = dve.max(m8[:, t, g, :], selm[:, t, 8 * g:8 * g + 8])
                link(ins)
                link(add(grp.unsqueeze(3), m8[:, :, :, 0:1], m8[:, :, :, 1:2]))
                theirs = grp.unsqueeze(2).broadcast_to([P, NT, GROUPS, GROUPS])
                mine = grp.unsqueeze(3).broadcast_to([P, NT, GROUPS, GROUPS])
                link(tt(cmp1, theirs, mine, ALU.is_gt))
                link(tt(cmp2, theirs, mine, ALU.is_equal))
                earlier = C("earlier").rearrange("p (a b) -> p a b", a=GROUPS).unsqueeze(1)\
                    .broadcast_to([P, NT, GROUPS, GROUPS])
                link(mul(cmp2, cmp2, earlier))
                link(add(cmp1, cmp1, cmp2))
                link(dve.tensor_reduce(gmask.unsqueeze(3), cmp1, AX, ALU.add))
                link(dve.tensor_scalar(gmask, gmask, float(GROUPS // 2), None, ALU.is_lt))
                gm = over(gmask, 8)
                s4 = selm.rearrange("p t (g e) -> p t g e", g=GROUPS)
                link(mul(s4, s4, gm))
                link(dve.tensor_scalar(gmask, gmask, -1.0, 1.0e30, ALU.add, ALU.mult))
                link(add(s4, s4, gm))
                for t in range(NT):
                    link(dve.max(t8[:, t, :], selm[:, t, :]))
                    link(dve.match_replace(selr[:, t, :], t8[:, t, :], selm[:, t, :], -3.0e38))
                link(dve.tensor_scalar(Mk, selr, -2.0e38, None, ALU.is_lt))
                dve.sem_inc(mask_ready, 1)
                shared_hidden(1)
                link(mul(G, SC, Mk))
                link(dve.tensor_reduce(gs.unsqueeze(2), G, AX, ALU.add))
                link(dve.reciprocal(gs, gs))
                link(dve.tensor_scalar(gs, gs, 2.5, None, ALU.mult))
                link(mul(G, G, gs.unsqueeze(2).broadcast_to([P, NT, EXPERTS])))
                dve.wait_ge(rank_done, 1)
                rk = ps[3][:, 0:NT * EXPERTS].rearrange("p (t e) -> p t e", t=NT)
                link(dve.scalar_tensor_tensor(rank, rk, 1.0, Mk, ALU.add, ALU.mult))
                link(dve.tensor_scalar(rank, rank, -1.0, None, ALU.add))
                link(dve.tensor_reduce(cnt[:, 0:1], ps[3][:, 2 * EXPERTS:3 * EXPERTS], AX, ALU.max))
                link(dve.memset(cnt[:, 1:2], 1.0))
                for r in range(1, ROUNDS):
                    link(dve.scalar_tensor_tensor(cnt[:, 1:2], cnt[:, 0:1], float(CAP * r), cnt[:, 1:2],
                                                  ALU.is_gt, ALU.add))
                link(dve.tensor_scalar(last_pair2[:, :], cnt[:, 1:2], float(PAIRS // 2), -1.0, ALU.mult, ALU.add))
                dve.sem_inc(rounds_ready, 1)
                link(dve.memset(Gs, 0.0))
                link(dve.tensor_copy(Gs[:, :, :, 0:1], G.unsqueeze(3)))
                link(tt(G.unsqueeze(3), G.unsqueeze(3), Gs[:, :, :, 0:1], ALU.subtract))
                link(dve.tensor_copy(Gs[:, :, :, 1:2], G.unsqueeze(3)))
                link(tt(Gs[:, :, :, 2:3], G.unsqueeze(3), Gs[:, :, :, 1:2], ALU.subtract))
                dve.sem_inc(h_done, 1)
                dve.sem_inc(ys_lo, 2)
                dve.sem_inc(acc_done, 4)
                slot = C("slot").unsqueeze(1).unsqueeze(1).broadcast_to([P, NT, 2, CAP])

                def selection(g, b):
                    e0 = (g % PAIRS) * 2
                    mine = rank[:, :, bass.ds(e0, 2)]
                    tt(Sel[b], slot, over(mine, CAP), ALU.is_equal).then_inc(sel_ready, 1)
                    dve.tensor_copy(Gp[b], Gs[:, :, bass.ds(e0, 2), :]).then_inc(selg_ready, 1)
                    dve.wait_ge(sel_ready, g + 1)
                    dve.tensor_scalar(mine, mine, -float(CAP), None, ALU.add).then_inc(rank_next, 1)
                    dve.wait_ge(rank_next, g + 1)

                def map_columns(g, b):
                    dve.wait_ge(st_tr, g + 1)
                    dve.tensor_copy(SelT[b], selT_ps)
                    for e in range(2):
                        r = slice(CAP * e, CAP * (e + 1))
                        ins = dve.tensor_reduce(gslot[r, :], gate_ps[r, 4 * e:4 * e + 4], AX, ALU.add)
                    ins.then_inc(st_done, 1)

                def gathered_half(g):
                    dve.wait_ge(gathered, 2 * g + 2)
                    dve.tensor_copy(XG[:, 4:8, :], ps[2].rearrange("p (k s) -> p k s", k=4)).then_inc(xg_dve, 1)

                def add_rows(g, halves=range(2)):
                    for n in halves:
                        for t in range(NT):
                            q = 2 * n + t
                            dve.wait_ge(sc_done, 4 * g + q + 1)
                            dve.wait_ge(acc_done, 4 * g + q - 1 + ACC0 - 4)
                            a = ACCv[:, t, n * 512:(n + 1) * 512]
                            add(a, a, ps[SCATTER_BANK[q]]).then_inc(acc_done, 1)

                last = dve.value_load(last_pair2[0:1, 0:1], min_val=PAIRS // 2 - 1, max_val=ROUNDS * PAIRS // 2 - 1)
                pairs2 = last + 1
                selection(0, 0)
                selection(1, 1)
                def start_sum(q):
                    t, n = q // 2, q % 2
                    dve.wait_ge(sho_done, q + 1)
                    s = slice(n * 512, (n + 1) * 512)
                    dve.scalar_tensor_tensor(ACCv[:, t, s], Xv[:, t, s], ALPHA, ps[SHARED_BANK[q]],
                                             ALU.mult, ALU.add).then_inc(acc_done, 1)

                dve.wait_ge(x_split, 2)
                for q in range(3):
                    start_sum(q)
                gathered_half(0)
                map_columns(0, 0)
                start_sum(3)

                def pair(j, b, first=False, final=False, ahead=True):
                    g = 2 * j + b
                    dve.wait_ge(silu_done, g + 1)
                    dve.wait_ge(ht_tr, g + 1)
                    dve.wait_ge(st_done, g + 1)
                    dve.scalar_tensor_tensor(Hh, HS, gslot, ps[0][:, F:2 * F], ALU.mult, ALU.mult)\
                       .then_inc(h_done, 1)
                    if not final:
                        gathered_half(g + 1)
                    if not first:
                        add_rows(g)
                    if not final:
                        map_columns(g + 1, 1 - b)
                    if ahead:
                        selection(g + 2, b)
                    for n, s in enumerate((slice(0, 512), slice(512, D))):
                        dve.wait_ge(ys_hi, 2 * g + n + 1)
                        tt(YR[:, s], ps[3 + n], Y3[:, 0, s], ALU.subtract).then_inc(ys_rest, 1)
                        dve.wait_ge(ys_mid, 2 * g + n + 1)
                        tt(Y3[:, 2, s], YR[:, s], Y3[:, 1, s], ALU.subtract).then_inc(ys_lo, 1)

                dve.sem_inc(in_experts, 1)
                pair(0, 0, first=True)
                pair(0, 1)
                with dve.Fori(1, last) as j:
                    for b in range(2):
                        pair(j, b)
                pair(last, 0, ahead=False)
                pair(last, 1, final=True, ahead=False)
                for n in range(2):
                    add_rows(2 * pairs2, halves=(n,))
                    dve.wait_ge(acc_done, 8 * pairs2 + 2 * n + ACC0 - 2)
                    for t in range(NT):
                        half_stats(t, n, ACCv)
                for t in range(NT):
                    layer_norm(t, ACCv, "ln2_g", "ln2_b", 6 + t)
                dve.reg_add(before_dp, before_dp, pairs2)
                dve.sem_inc(layer_done, 1)
                dve.wait_ge(layer_open, l + 1)


IN_AT = {"mlstm_qk": (0,), "conv": (1288,), "gla_qk": (2572,), "mlstm_vo": (512,), "gla_vr": (2828,),
         "att_qk": (1804,)}


def constants():
    import numpy as np
    c = np.zeros((P, CSTS), np.float32)
    i = np.arange(P)
    c[:, CST["ident"]] = np.eye(P)
    c[:, CST["before"]] = i[:, None] < i[None, :]
    c[:, CST["ones"]] = 1.0
    causal = np.where(i[:, None] <= i[None, :], 0.0, -1.0e30)
    c[:, CST["causal"]] = np.concatenate([causal, np.zeros((P, P)), causal], 1)
    t, s = np.arange(T)[:, None], np.arange(T)[None, :]
    n = ((t >= s) & (t - s <= 128)).astype(np.float32)
    for window, dilation in ((512, 4), (2048, 16)):
        n += (t >= s) & ((t - s) % dilation == 0) & ((t - s) // dilation <= window // dilation)
    n = np.concatenate([n[:P, :P], n[P:, :]], 1)
    c[:, CST["att_mul"]] = n
    c[:, CST["att_add"]] = np.where(n > 0, 0.0, -1.0e30)
    inv = np.float32(10000.0) ** (-np.arange(32, dtype=np.float32) / np.float32(32))
    ang = np.arange(T, dtype=np.float32)[:, None] * inv.astype(np.float32)
    for name, f in (("cos", np.cos), ("sin", np.sin)):
        c[:, CST[name]] = f(ang).astype(np.float32).reshape(NT, P, 32).transpose(1, 0, 2).reshape(P, -1)
    c[:, CST["slot"]] = np.arange(CAP)
    for r in (0, 64):
        for h in range(H):
            c[r + h, CST["head"].start + h * P:CST["head"].start + (h + 1) * P] = 1.0
    c[:, CST["tri"]] = (i % BLK)[:, None] <= np.arange(BLK)[None, :]
    g = np.arange(GROUPS)
    c[:, CST["earlier"]] = (g[None, :] < g[:, None]).reshape(1, -1)
    return c


def layout(w):
    import numpy as np
    w = {k: np.asarray(v) for k, v in w.items()}
    win = w["w_in"].reshape(DEPTH, P, KD, -1)
    small = np.zeros((DEPTH, P, KD, P), np.float32)
    small[..., 0:H] = win[..., 1024:1028]
    small[..., 32:32 + H] = win[..., 1028:1032]
    small[..., 64:64 + H] = win[..., 1800:1804]
    small[..., 96:112] = win[..., 3340:3356]
    parts = [small]
    for name, n, _ in GROUPS_IN[1:]:
        if name == "att_v_ssm_z":
            parts.append(np.concatenate([win[..., 2316:2572], win[..., 1032:1288]], -1))
        else:
            parts.append(win[..., IN_AT[name][0]:IN_AT[name][0] + n])
    w_in = np.concatenate([p.reshape(DEPTH, P, -1) for p in parts], -1)
    rows = np.concatenate([w["ln1_g"], w["ln1_b"], w["ln2_g"], w["ln2_b"], w["ml_norm_w"], w["ssm_norm_w"],
                           w["gla_norm_w"], w["ssm_d"], w["router_bias"]], -1)
    cols = np.zeros((DEPTH, P, COLS), np.float32)
    cols[:, 0:H, 0] = w["ml_i_bias"]
    cols[:, 32:32 + H, 0] = w["ml_f_bias"]
    cols[:, 64:64 + H, 0] = w["ssm_dt_bias"]
    cols[:, 64:64 + H, 1] = w["ssm_a_log"]
    cols[:, :, 2] = w["gla_gate_b"]
    cols[:, :, COL["taps"]] = w["ssm_conv_w"].reshape(DEPTH, 4, 4, P).transpose(0, 3, 2, 1).reshape(DEPTH, P, 16)
    cols[:, :, COL["conv_b"]] = w["ssm_conv_b"].reshape(DEPTH, 4, P).transpose(0, 2, 1)
    cols[:, 96:112, COL["gate_w2"]] = w["gla_gate_w2"]
    return {"x": w["x"][0], "w_in": w_in, "cols": cols, "rows": rows, "cst": constants(), "w_out": w["w_out"],
            "router_w": w["router_w"], "exp_w_gate": w["exp_w_gate"], "exp_w_up": w["exp_w_up"],
            "exp_w_down": w["exp_w_down"], "sh_w_gate": w["sh_w_gate"], "sh_w_up": w["sh_w_up"],
            "sh_w_down": w["sh_w_down"]}


def build(nc, arrays, **more):
    import numpy as np
    a = {}
    for name, v in arrays.items():
        a[name] = nc.dram_tensor(f"in_{name}", v.shape, mybir.dt.from_np(v.dtype), kind="ExternalInput").ap()
    out = nc.dram_tensor("out_0", (T, D), F32, kind="ExternalOutput").ap()
    hybrid_kernel(nc, a["x"], a["w_in"], a["cols"], a["rows"], a["cst"], a["w_out"], a["router_w"],
                  a["exp_w_gate"].rearrange("l (g e) (p k) f -> l g p e k f", e=2, k=KD),
                  a["exp_w_up"].rearrange("l (g e) (p k) f -> l g p e k f", e=2, k=KD),
                  a["exp_w_down"].rearrange("l (g e) (p k) d -> l g p e k d", e=2, k=2),
                  a["sh_w_gate"], a["sh_w_up"], a["sh_w_down"], out, **more)


def kernel(**inputs):
    import numpy as np
    from concourse import bacc
    from concourse.bass_utils import run_bass_kernel_spmd

    arrays = {k: np.ascontiguousarray(v) for k, v in layout(inputs).items()}
    nc = bacc.Bacc("TRN2", target_bir_lowering=False, num_devices=1)
    build(nc, arrays)
    r = run_bass_kernel_spmd(nc, [{f"in_{k}": v for k, v in arrays.items()}], core_ids=[0])
    return r.results[0]["out_0"].reshape(1, T, D)
```
